# Optimizing a Trainium2 kernel written in Bass

```python
import math
import jax
import jax.numpy as jnp
from jax import lax
import numpy as np

D_MODEL = 1024
BATCH = 1
SEQ = 256
DEPTH = 2

CHUNK = 64
RMS_EPS = 1e-6

CONV_WIDTH = D_MODEL // 2
SHORT_CONV_K = 3
SB_HEADS = 8
SB_HEAD_DIM = 64
SB_WIDTH = SB_HEADS * SB_HEAD_DIM
Q_BLOCK = 128
EVEN_PROJ = 3 * CONV_WIDTH + 3 * SB_WIDTH
EVEN_MIX = CONV_WIDTH + SB_WIDTH

D_INNER = 2 * D_MODEL
SSM_HEAD_DIM = 64
SSM_HEADS = D_INNER // SSM_HEAD_DIM
SSM_GROUPS = 8
SSM_HPG = SSM_HEADS // SSM_GROUPS
SSM_STATE = 128
SSM_CONV_K = 4
SSM_CONV_DIM = D_INNER + 2 * SSM_GROUPS * SSM_STATE
ODD_PROJ = D_INNER + SSM_CONV_DIM + SSM_HEADS

N_EXPERT_GROUPS = 4
EXPERTS_PER_GROUP = 8
N_EXPERTS = N_EXPERT_GROUPS * EXPERTS_PER_GROUP
TOP_K_EXPERT = 2
EXPERT_FF = 512
MOE_BLOCK = 256

kernel_name = 'hybrid_conv_stickbreak_ssd_hmoe'

def rmsnorm(x, w):
    xf = x.astype(jnp.float32)
    y = xf * lax.rsqrt(jnp.mean(xf * xf, axis=-1, keepdims=True) + RMS_EPS)
    return (y * w.astype(jnp.float32)).astype(x.dtype)

def causal_dwconv(x, w):
    k, c = w.shape
    return lax.conv_general_dilated(
        x, w[:, None, :].astype(x.dtype), window_strides=(1,), padding=[(k - 1, 0)],
        dimension_numbers=('NWC', 'WIO', 'NWC'), feature_group_count=c)

def stick_breaking_attention(q, k, v):
    seq, dh = q.shape[1], q.shape[3]
    qf = q.astype(jnp.float32) * (dh ** -0.5)
    kf = k.astype(jnp.float32)
    vf = v.astype(jnp.float32)
    outs = []
    for blk in range(seq // Q_BLOCK):
        q0 = blk * Q_BLOCK
        q_end = q0 + Q_BLOCK
        z = jnp.einsum('bqhd,bkhd->bhqk', qf[:, q0:q_end], kf[:, :q_end])
        t_idx = q0 + jnp.arange(Q_BLOCK)
        s_idx = jnp.arange(q_end)
        causal = s_idx[None, :] < t_idx[:, None]
        log_1m = jnp.where(causal, -jax.nn.softplus(z), 0.0)
        suffix = lax.cumsum(log_1m, axis=3, reverse=True) - log_1m
        att = jnp.where(causal, jnp.exp(jax.nn.log_sigmoid(z) + suffix), 0.0)
        outs.append(jnp.einsum('bhqk,bkhd->bqhd', att, vf[:, :q_end]))
    return jnp.concatenate(outs, axis=1)

def conv_stick_mixer(h, w_in, conv_w, w_out):
    bsz, seq, _ = h.shape
    proj = h @ w_in
    c0 = CONV_WIDTH
    gate_b = proj[..., :c0]
    gate_c = proj[..., c0:2 * c0]
    hid = proj[..., 2 * c0:3 * c0]
    off = 3 * c0
    q = proj[..., off:off + SB_WIDTH].reshape(bsz, seq, SB_HEADS, SB_HEAD_DIM)
    k = proj[..., off + SB_WIDTH:off + 2 * SB_WIDTH].reshape(bsz, seq, SB_HEADS, SB_HEAD_DIM)
    v = proj[..., off + 2 * SB_WIDTH:off + 3 * SB_WIDTH].reshape(bsz, seq, SB_HEADS, SB_HEAD_DIM)
    conv_out = gate_b * causal_dwconv(gate_c * hid, conv_w)
    sb_out = stick_breaking_attention(q, k, v).reshape(bsz, seq, SB_WIDTH).astype(h.dtype)
    return jnp.concatenate([conv_out, sb_out], axis=-1) @ w_out

def ssd_scan(x, dt, a, b_mat, c_mat):
    bsz, seq = x.shape[0], x.shape[1]
    n_chunks = seq // CHUNK

    def to_chunks(t):
        return jnp.moveaxis(t.reshape((bsz, n_chunks, CHUNK) + t.shape[2:]), 1, 0)

    lower = jnp.tril(jnp.ones((CHUNK, CHUNK), dtype=bool))

    def step(state, inp):
        xc, dtc, bc, cc = inp
        cs = jnp.cumsum(dtc * a, axis=1)
        seg = cs[:, :, None] - cs[:, None, :]
        decay = jnp.exp(jnp.where(lower[None, :, :, None, None], seg, -jnp.inf))
        xdt = xc * dtc[..., None]
        cb = jnp.einsum('blgn,bsgn->blsg', cc, bc)
        y = jnp.einsum('blsgr,bsgrp->blgrp', cb[..., None] * decay, xdt)
        y = y + jnp.einsum('blgn,bgrpn->blgrp', cc, state) * jnp.exp(cs)[..., None]
        to_end = jnp.exp(cs[:, -1:] - cs)
        state = (state * jnp.exp(cs[:, -1])[..., None, None]
                 + jnp.einsum('bsgn,bsgrp->bgrpn', bc, xdt * to_end[..., None]))
        return state, y

    state0 = jnp.zeros((bsz, SSM_GROUPS, SSM_HPG, SSM_HEAD_DIM, SSM_STATE), jnp.float32)
    _, ys = lax.scan(step, state0, (to_chunks(x), to_chunks(dt), to_chunks(b_mat), to_chunks(c_mat)))
    return jnp.moveaxis(ys, 0, 1).reshape(x.shape)

def mamba2_mixer(h, in_proj, conv_w, conv_b, dt_bias, a_log, d_skip, norm_w, out_proj):
    bsz, seq, _ = h.shape
    proj = h @ in_proj
    z = proj[..., :D_INNER]
    xbc = proj[..., D_INNER:D_INNER + SSM_CONV_DIM]
    dt_raw = proj[..., D_INNER + SSM_CONV_DIM:]
    xbc = jax.nn.silu(causal_dwconv(xbc, conv_w) + conv_b)
    gn = SSM_GROUPS * SSM_STATE
    xs = xbc[..., :D_INNER].astype(jnp.float32).reshape(bsz, seq, SSM_GROUPS, SSM_HPG, SSM_HEAD_DIM)
    b_mat = xbc[..., D_INNER:D_INNER + gn].astype(jnp.float32).reshape(bsz, seq, SSM_GROUPS, SSM_STATE)
    c_mat = xbc[..., D_INNER + gn:].astype(jnp.float32).reshape(bsz, seq, SSM_GROUPS, SSM_STATE)
    dt = jax.nn.softplus(dt_raw.astype(jnp.float32) + dt_bias.astype(jnp.float32))
    dt = dt.reshape(bsz, seq, SSM_GROUPS, SSM_HPG)
    a = -jnp.exp(a_log.astype(jnp.float32)).reshape(SSM_GROUPS, SSM_HPG)
    y = ssd_scan(xs, dt, a, b_mat, c_mat)
    y = y + d_skip.astype(jnp.float32).reshape(SSM_GROUPS, SSM_HPG)[:, :, None] * xs
    y = y.reshape(bsz, seq, D_INNER) * jax.nn.silu(z.astype(jnp.float32))
    yg = y.reshape(bsz, seq, SSM_GROUPS, D_INNER // SSM_GROUPS)
    yg = yg * lax.rsqrt(jnp.mean(yg * yg, axis=-1, keepdims=True) + RMS_EPS)
    y = yg.reshape(bsz, seq, D_INNER) * norm_w.astype(jnp.float32)
    return y.astype(h.dtype) @ out_proj

def hierarchical_moe(x, wg, bg, we, be, w_gate, w_up, w_down):
    bsz, seq, d = x.shape
    xt = x.reshape(-1, d)
    n_tok = xt.shape[0]
    g_prob = jax.nn.softmax((xt @ wg + bg).astype(jnp.float32), axis=-1)
    g_top_p, g_idx = lax.top_k(g_prob, 1)
    e_logits = jnp.einsum('td,gde->tge', xt, we) + be
    e_logits = e_logits[jnp.arange(n_tok), g_idx[:, 0]].astype(jnp.float32)
    e_top_l, e_idx = lax.top_k(e_logits, TOP_K_EXPERT)
    gates = jax.nn.softmax(e_top_l, axis=-1) * g_top_p
    expert = g_idx * EXPERTS_PER_GROUP + e_idx
    n_slots = n_tok * TOP_K_EXPERT
    flat = expert.reshape(-1)
    order = jnp.argsort(flat)
    sorted_e = flat[order]
    counts = jnp.bincount(flat, length=N_EXPERTS)
    starts = jnp.cumsum(counts) - counts
    padded = (counts + MOE_BLOCK - 1) // MOE_BLOCK * MOE_BLOCK
    pends = jnp.cumsum(padded)
    pstarts = pends - padded
    dest = pstarts[sorted_e] + jnp.arange(n_slots) - starts[sorted_e]
    n_blocks = -(-n_slots // MOE_BLOCK) + N_EXPERTS
    tok = order // TOP_K_EXPERT
    buf = jnp.zeros((n_blocks * MOE_BLOCK, d), x.dtype).at[dest].set(xt[tok])
    block_e = jnp.minimum(jnp.searchsorted(pends, jnp.arange(n_blocks) * MOE_BLOCK, side='right'),
                          N_EXPERTS - 1)

    def expert_block(args):
        xb, e = args
        hb = jax.nn.silu(xb @ w_gate[e]) * (xb @ w_up[e])
        return hb @ w_down[e]

    out = lax.map(expert_block, (buf.reshape(n_blocks, MOE_BLOCK, d), block_e)).reshape(-1, d)
    w_sorted = gates.reshape(-1)[order].astype(x.dtype)
    y = jax.ops.segment_sum(out[dest] * w_sorted[:, None], tok, num_segments=n_tok)
    return y.reshape(bsz, seq, d)

def setup_inputs(seed: int = 0) -> dict:
    key = jax.random.key(seed)
    ks = jax.random.split(key, 24)
    n_even = (DEPTH + 1) // 2
    n_odd = DEPTH // 2

    def normal(k, shape, scale):
        return jax.random.normal(k, shape, jnp.float32) * scale

    x = normal(ks[0], (BATCH, SEQ, D_MODEL), 1.0)
    even_w_in = normal(ks[1], (n_even, D_MODEL, EVEN_PROJ), D_MODEL ** -0.5)
    even_conv_w = normal(ks[2], (n_even, SHORT_CONV_K, CONV_WIDTH), SHORT_CONV_K ** -0.5)
    even_w_out = normal(ks[3], (n_even, EVEN_MIX, D_MODEL), EVEN_MIX ** -0.5)
    odd_in_proj = normal(ks[4], (n_odd, D_MODEL, ODD_PROJ), D_MODEL ** -0.5)
    odd_conv_w = normal(ks[5], (n_odd, SSM_CONV_K, SSM_CONV_DIM), SSM_CONV_K ** -0.5)
    odd_conv_b = normal(ks[6], (n_odd, SSM_CONV_DIM), 0.02)
    dt0 = jnp.exp(jax.random.uniform(ks[7], (n_odd, SSM_HEADS), jnp.float32,
                                     minval=math.log(1e-3), maxval=math.log(1e-1)))
    odd_dt_bias = dt0 + jnp.log(-jnp.expm1(-dt0))
    odd_a_log = jnp.log(jax.random.uniform(ks[8], (n_odd, SSM_HEADS), jnp.float32, minval=1.0, maxval=16.0))
    odd_d_skip = 1.0 + normal(ks[9], (n_odd, SSM_HEADS), 0.1)
    odd_norm_w = 1.0 + normal(ks[10], (n_odd, D_INNER), 0.02)
    odd_out_proj = normal(ks[11], (n_odd, D_INNER, D_MODEL), D_INNER ** -0.5)
    norm_mix = 1.0 + normal(ks[12], (DEPTH, D_MODEL), 0.02)
    norm_ffn = 1.0 + normal(ks[13], (DEPTH, D_MODEL), 0.02)
    router_g_w = normal(ks[14], (DEPTH, D_MODEL, N_EXPERT_GROUPS), D_MODEL ** -0.5)
    router_g_b = normal(ks[15], (DEPTH, N_EXPERT_GROUPS), 0.01)
    router_e_w = normal(ks[16], (DEPTH, N_EXPERT_GROUPS, D_MODEL, EXPERTS_PER_GROUP), D_MODEL ** -0.5)
    router_e_b = normal(ks[17], (DEPTH, N_EXPERT_GROUPS, EXPERTS_PER_GROUP), 0.01)
    expert_w_gate = normal(ks[18], (DEPTH, N_EXPERTS, D_MODEL, EXPERT_FF), D_MODEL ** -0.5)
    expert_w_up = normal(ks[19], (DEPTH, N_EXPERTS, D_MODEL, EXPERT_FF), D_MODEL ** -0.5)
    expert_w_down = normal(ks[20], (DEPTH, N_EXPERTS, EXPERT_FF, D_MODEL), EXPERT_FF ** -0.5)
    final_norm = 1.0 + normal(ks[21], (D_MODEL,), 0.02)
    return {'x': x, 'even_w_in': even_w_in, 'even_conv_w': even_conv_w, 'even_w_out': even_w_out,
            'odd_in_proj': odd_in_proj, 'odd_conv_w': odd_conv_w, 'odd_conv_b': odd_conv_b,
            'odd_dt_bias': odd_dt_bias, 'odd_a_log': odd_a_log, 'odd_d_skip': odd_d_skip,
            'odd_norm_w': odd_norm_w, 'odd_out_proj': odd_out_proj,
            'norm_mix': norm_mix, 'norm_ffn': norm_ffn,
            'router_g_w': router_g_w, 'router_g_b': router_g_b,
            'router_e_w': router_e_w, 'router_e_b': router_e_b,
            'expert_w_gate': expert_w_gate, 'expert_w_up': expert_w_up, 'expert_w_down': expert_w_down,
            'final_norm': final_norm}

def reference(x, even_w_in, even_conv_w, even_w_out, odd_in_proj, odd_conv_w, odd_conv_b,
              odd_dt_bias, odd_a_log, odd_d_skip, odd_norm_w, odd_out_proj, norm_mix, norm_ffn,
              router_g_w, router_g_b, router_e_w, router_e_b, expert_w_gate, expert_w_up,
              expert_w_down, final_norm):
    h = x
    for layer in range(DEPTH):
        i = layer // 2
        hn = rmsnorm(h, norm_mix[layer])
        if layer % 2 == 0:
            mix = conv_stick_mixer(hn, even_w_in[i], even_conv_w[i], even_w_out[i])
        else:
            mix = mamba2_mixer(hn, odd_in_proj[i], odd_conv_w[i], odd_conv_b[i], odd_dt_bias[i],
                               odd_a_log[i], odd_d_skip[i], odd_norm_w[i], odd_out_proj[i])
        h = h + mix
        h = h + hierarchical_moe(rmsnorm(h, norm_ffn[layer]), router_g_w[layer], router_g_b[layer],
                                 router_e_w[layer], router_e_b[layer], expert_w_gate[layer],
                                 expert_w_up[layer], expert_w_down[layer])
    return rmsnorm(h, final_norm)


_drawn_inputs = setup_inputs


def setup_inputs(seed=0):
    import zlib

    import numpy as np

    out = dict(_drawn_inputs(seed))
    spreads = {}
    factors = {'odd_norm_w': 8.989, 'router_g_b': 23.086, 'router_e_b': 3.204, 'final_norm': 7.508}
    for name, (base, spread) in spreads.items():
        noise = np.random.default_rng([zlib.crc32(name.encode()), seed]).standard_normal(out[name].shape)
        drawn = base * np.exp(spread * noise) if base else spread * noise
        out[name] = jnp.asarray(drawn.astype(out[name].dtype))
    for name, factor in factors.items():
        out[name] = (out[name] * factor).astype(out[name].dtype)
    return out
```

```python
from contextlib import ExitStack, contextmanager

import concourse.bass as bass
from concourse import mybir

F32 = mybir.dt.float32
BF16 = mybir.dt.bfloat16
I32 = mybir.dt.int32
ALU = mybir.AluOpType
ACT = mybir.ActivationFunctionType
AX = mybir.AxisListType.X

P = 128
D = 1024
KC = D // P
TT = 2
SEQ = TT * P
EVEN_UNITS = 4
ODD_UNITS = 8
HPG = 4
HD = 64
HEADS = 32
XB0, BB0, CB0 = 2048, 4096, 5120
DT0 = 6144
NE = 32
NG = 4
EPG = 8
FF = 512
CAP = 32
MAXB = SEQ // CAP
EPS = 1e-6
BIG = 1.0e30
ds = bass.ds


class Chain:

    def __init__(self, eng, sem, base=0):
        self.eng, self.sem, self.base, self.n = eng, sem, base, 0

    def link(self, ins):
        ins.then_inc(self.sem, 1)
        self.n += 1
        self.eng.wait_ge(self.sem, self.base + self.n)

    @contextmanager
    def loop(self, start, end, per):
        first = self.base + self.n
        with self.eng.Fori(start, end) as i:
            self.base, self.n = (i - start) * per + first, 0
            yield i
            assert self.n == per, (self.n, per)
        self.base, self.n = first + (end - start) * per, 0


SEMS = """
x_in par_vec par_conv par_head par_row par_wr fnorm_in out_stored
consts_pool consts_dve
c0_in c1_in c2_in wo_in
gu_in0 gu_in1 dn_in0 dn_in1
dve_chain act_chain pool_chain ovf_chain
conv_raw_t conv_cols
sum_sq mean_sq rstd_guess hs_dve hs_act hs_t hnt_dve hnt_act h_next zeroed
mix_acc
gc_hid hid_copied ch_done gb_q gb_copied q_copied k_v kv_copied conv_done
z_done z_copied z_log sp_done r_done att_in att_exp att_done av_done av_copied oproj
dt_raw dt_pre dt_exp dt_ln dt_a cum_done cum_used csx_done alog_exp
z1_done z1_exp z1_silu x1_done x1_tap x1_conv x1_exp x1_silu bc_done bc_tap bc_conv bc_exp bc_silu
gsel_done csrow_done seg_done decay_done cb_done decay_used xst_done xdt_done y_done yz_done yss_done yms_done yguess mix1_done
logits route_d route_e mask_done ranks table_done pos_t pg_done
prep_sel b_done g4_done gath_done xs_done gu_done gexp h_done ht_done ht_copied dn_done y_copied comb_done
ov_sel ov_b ov_x ov_gu ov_exp ov_h ov_ht ov_htc ov_dn ov_yc ov_done
""".split()


def trunk_program(nc, x, even_w_in, even_conv_w, even_w_out, odd_in_proj, odd_conv_w, odd_conv_b,
                  odd_dt_bias, odd_a_log, odd_d_skip, odd_norm_w, odd_out_proj, norm_mix, norm_ffn,
                  router_g_w, router_g_b, router_e_w, router_e_b, expert_w_gate, expert_w_up,
                  expert_w_down, final_norm, out):
    with ExitStack() as ctx:
        def sb(name, shape, dt=F32):
            return ctx.enter_context(nc.sbuf_tensor(name, shape, dt))

        def ps(name, shape):
            return ctx.enter_context(nc.psum_tensor(name, shape, F32))

        S = {n: ctx.enter_context(nc.semaphore(n)) for n in SEMS}

        h = sb("h", [P, TT, D])
        hs = sb("hs", [P, TT, KC, P])
        hnT = sb("hnT", [P, KC, SEQ])
        w_gu = [sb(f"w_gu{s}", [P, 2, KC, FF]) for s in range(2)]
        w_dn = [sb(f"w_dn{s}", [P, FF // P, D]) for s in range(2)]
        w_c = [sb(f"w_c{j}", [P, KC, 2, P]) for j in range(3)]
        w_o = sb("w_o", [P, 2, D])

        ident = sb("ident", [P, P])
        upper = sb("upper", [P, P])
        lower = sb("lower", [P, P])
        strict = sb("strict", [P, P])
        ones = sb("ones", [P, P])
        zero_bf = sb("zero_bf", [P, 512], BF16)
        iota = sb("iota", [P, NE])
        slot_id = sb("slot_id", [P, 1])
        descend = sb("descend", [P, NE])
        one_c = sb("one_c", [P, 1])
        group_of = sb("group_of", [HEADS, ODD_UNITS])
        rank_of = sb("rank_of", [HEADS, HPG])
        nmix = sb("nmix", [P, 2, KC])
        nffn = sb("nffn", [P, 2, KC])
        conv_raw = sb("conv_raw", [P, P])
        vec_raw = sb("vec_raw", [60, P])
        conv_cols = sb("conv_cols_sb", [P, P])
        vec_cols = sb("vec_cols", [P, 60])
        skip_row = sb("skip_row", [P, HEADS])
        dskip = sb("dskip", [P, 16])
        wr = sb("wr", [P, 2, KC, NG + NE])
        rbias = sb("rbias", [P, 2, NG + NE])
        dtb = sb("dtb", [P, HEADS])
        alog = sb("alog", [P, HEADS])
        wdt = sb("wdt", [P, KC, HEADS])
        st = sb("st", [P, 8, TT])
        table = sb("table", [1, 2 * (NE + 1)], I32)

        ARENA = 11400
        arena = sb("arena", [P, ARENA])

        def carve():
            at = [0]

            def take(*shape, rows=P):
                n = 1
                for k in shape:
                    n *= k
                v = arena[0:rows, at[0]:at[0] + n]
                at[0] += n
                assert at[0] <= ARENA, at[0]
                if len(shape) == 2:
                    v = v.rearrange("p (a b) -> p a b", a=shape[0])
                if len(shape) == 3:
                    v = v.rearrange("p (a b c) -> p a b c", a=shape[0], b=shape[1])
                return v
            return take

        take = carve()
        qS = [take(SEQ) for _ in range(2)]
        kS = [take(SEQ) for _ in range(2)]
        vS = [take(TT, P) for _ in range(2)]
        hidS, gbS, ch = take(SEQ), take(SEQ), take(SEQ + 2)
        cacc = take(SEQ)
        zS, lS, sp, att = take(2, 384), take(2, 384), take(2, 384), take(2, 384)
        mix = [take(2, SEQ) for _ in range(2)]
        take = carve()
        mix1 = [take(2, SEQ) for _ in range(2)]
        ez = take(2, SEQ)
        sz = [take(2, SEQ) for _ in range(2)]
        xT = [take(2, SEQ) for _ in range(2)]
        bcT = [take(2, SEQ) for _ in range(2)]
        cv, ecv = take(2, SEQ), take(2, SEQ)
        csx = take(2, HPG, P, rows=HEADS)
        gsel = take(P, rows=HEADS)
        decay = take(3, HPG, P)
        cbs = take(384)
        xdt, xw = take(TT, 256), take(256)
        yz, sq = take(2, SEQ), ecv
        ms, rg, rt = take(SEQ), take(SEQ), take(SEQ)
        dtv, dta, csn = (take(TT, HEADS) for _ in range(3))
        w0, dtw = take(HEADS), take(HEADS)
        take = carve()
        pos = take(TT, NE + 1)
        gates = take(TT, NE)
        mask = take(TT, NE)
        lg = take(TT, NG + NE)
        rt1, rt2, oh1, oh2 = (take(TT, NE) for _ in range(4))
        m8 = take(8, TT)
        dd, ee = take(TT, 8), take(TT, 8)
        cnt = take(2 * NE + 8)
        PG = take(2 * SEQ, rows=NE)
        sel = take(P, rows=NE)
        Ssel = [take(TT, CAP) for _ in range(2)]
        G4 = [take(SEQ) for _ in range(2)]
        xs = [take(KC, CAP) for _ in range(2)]
        eg, hb, hT = take(P), take(P), take(P)
        ysb = [take(256) for _ in range(2)]
        o_sel = take(P, rows=NE)
        o_S, o_G4, o_xs = take(TT, CAP), take(SEQ), take(KC, CAP)
        o_eg, o_h, o_hT, o_y = take(P), take(P), take(P), take(256)
        o_iota, o_slot = take(NE), take(1)
        junk = arena[:, ARENA - D:ARENA]
        fnorm = hnT[:, 0:4, :].rearrange("p a b -> p (a b)")
        y_out = w_c[0][:, :, :, :].rearrange("p k a b -> p (k a b)").rearrange("p (t d) -> p t d", t=TT)

        acc = ps("acc", [P, 4, 512])
        pa, pb, wa, wb = (ps(n, [P, 512]) for n in ("pa", "pb", "wa", "wb"))
        BANKS = [pa, pb, wa, wb]
        pa2, pb2 = (b[:, :].rearrange("p (a b) -> p a b", a=2) for b in (pa, pb))
        B_ps = pa
        XG = pb[:, 0:256].rearrange("p (k s) -> p k s", k=KC)
        Y_ps = wb[:, 256:512]
        GU = [wa[:, 256 * s:256 * s + 256].rearrange("p (g n) -> p g n", g=2) for s in range(2)]
        HT_ps = wb[:, 0:P]

        w_in_e = even_w_in[0].rearrange("(p k) (b m) -> p k b m", k=KC, b=6)
        w_in_o = odd_in_proj[0].rearrange("(p k) n -> p k n", k=KC)
        w_out_e = even_w_out[0].rearrange("(a c) n -> c a n", a=2)
        w_out_o = odd_out_proj[0].rearrange("(a c) n -> c a n", c=P)
        h_d = x[0].rearrange("(t p) d -> p t d", p=P)
        out_d = out[0].rearrange("(t p) d -> p t d", p=P)

        block = ctx.enter_context(nc.Block())

        @block.sync
        def _(sp_):
            def chunks_even(u):
                if u:
                    sp_.wait_ge(S["gc_hid"], u)
                sp_.dma_start(w_c[0][:, :, :, :], w_in_e[:, :, 1:3, P * u:P * u + P]).then_inc(S["c0_in"], 16)
                if u:
                    sp_.wait_ge(S["gb_q"], u)
                sp_.dma_start(w_c[1][:, :, :, :], w_in_e[:, :, 0:4:3, P * u:P * u + P]).then_inc(S["c1_in"], 16)
                if u:
                    sp_.wait_ge(S["k_v"], u)
                sp_.dma_start(w_c[2][:, :, :, :], w_in_e[:, :, 4:6, P * u:P * u + P]).then_inc(S["c2_in"], 16)

            def rows_even(u):
                if u:
                    sp_.wait_ge(S["oproj"], u)
                a = w_out_e[P * u:P * u + P]
                sp_.dma_start(w_o[:, :, :], a).then_inc(S["wo_in"], 16)

            def chunks_odd(g, first=False):
                sp_.wait_ge(S["gc_hid"], EVEN_UNITS) if first else sp_.wait_ge(S["z1_done"], g)
                sp_.dma_start(w_c[0][:, :, :, :].rearrange("p k a b -> p k (a b)"),
                              w_in_o[:, :, ds(g * 256, 256)]).then_inc(S["c0_in"], 16)
                sp_.wait_ge(S["gb_q"], EVEN_UNITS) if first else sp_.wait_ge(S["x1_done"], g)
                sp_.dma_start(w_c[1][:, :, :, :].rearrange("p k a b -> p k (a b)"),
                              w_in_o[:, :, ds(g * 256 + XB0, 256)]).then_inc(S["c1_in"], 16)
                sp_.wait_ge(S["k_v"], EVEN_UNITS) if first else sp_.wait_ge(S["bc_done"], g)
                bc = w_in_o[:, :, BB0:DT0].rearrange("p k (a n) -> p k a n", a=2)
                sp_.dma_start(w_c[2][:, :, :, :], bc[:, :, :, ds(g * P, P)]).then_inc(S["c2_in"], 16)

            def rows_odd(g):
                sp_.wait_ge(S["oproj"], g + EVEN_UNITS)
                sp_.dma_start(w_o[:, :, :], w_out_o[:, ds(g * 2, 2), :]).then_inc(S["wo_in"], 16)

            def expert(l, e, s, free=True):
                if free:
                    sp_.wait_ge(S["dn_done"], e + (NE * l - 1))
                    n = sp_.value_load(table[0:1, ds(e + ((NE + 1) * l - 1), 1)], min_val=0, max_val=2 * NE)
                    sp_.wait_ge(S["ov_done"], n + 1)
                g, u, d = (w[l, ds(e, 1), :, :] for w in (expert_w_gate, expert_w_up, expert_w_down))
                gu, dn = (S["gu_in0"], S["gu_in1"])[s], (S["dn_in0"], S["dn_in1"])[s]
                sp_.dma_start(w_gu[s][:, 0], g.rearrange("a (p k) f -> p (a k) f", k=KC)).then_inc(gu, 16)
                sp_.dma_start(w_gu[s][:, 1], u.rearrange("a (p k) f -> p (a k) f", k=KC)).then_inc(gu, 16)
                sp_.dma_start(w_dn[s][:, :, :], d.rearrange("a (j p) n -> p (a j) n", p=P)).then_inc(dn, 16)

            def expert_first(l, s):
                if l:
                    sp_.wait_ge(S["dn_done"], NE * l - 1 + s)
                    n = sp_.value_load(table[0:1, (NE + 1) * l - 2 + s:(NE + 1) * l - 1 + s], min_val=0, max_val=2 * NE)
                    sp_.wait_ge(S["ov_done"], n + 1)
                expert(l, s, s, free=False)

            chunks_even(0)
            rows_even(0)
            chunks_even(1)
            for s in range(2):
                expert_first(0, s)
            for u in range(1, EVEN_UNITS):
                rows_even(u)
                if u + 1 < EVEN_UNITS:
                    chunks_even(u + 1)
            chunks_odd(0, first=True)
            rows_odd(0)
            sp_.wait_ge(S["table_done"], 1)
            with sp_.Fori(1, NE // 2) as i:
                for s in range(2):
                    expert(0, i * 2 + s, s)
            for s in range(2):
                expert_first(1, s)
            with sp_.Fori(1, ODD_UNITS) as g:
                chunks_odd(g)
                rows_odd(g)
            sp_.wait_ge(S["table_done"], 2)
            with sp_.Fori(1, NE // 2) as i:
                for s in range(2):
                    expert(1, i * 2 + s, s)
            sp_.wait_ge(S["h_next"], 5)
            sp_.dma_start(out_d, y_out).then_inc(S["out_stored"], 16)
            sp_.wait_ge(S["out_stored"], 16)

        @block.gpsimd
        def _(pool):
            chain = Chain(pool, S["pool_chain"])
            nc.gpsimd.memset(ones[:, :], 1.0)
            nc.gpsimd.memset(one_c[:, :], 1.0)
            nc.gpsimd.memset(ident[:, :], 0.0)
            nc.gpsimd.memset(zero_bf[:, :], 0.0)
            nc.gpsimd.memset(group_of[:, :], 1.0)
            nc.gpsimd.iota(iota[:, :], pattern=[[1, NE]], base=0, channel_multiplier=0,
                           allow_small_or_imprecise_dtypes=True)
            nc.gpsimd.iota(descend[:, :], pattern=[[-1, NE]], base=NE, channel_multiplier=0,
                           allow_small_or_imprecise_dtypes=True)
            for q in range(4):
                chain.link(nc.gpsimd.iota(slot_id[32 * q:32 * q + 32, :], pattern=[[0, 1]], base=0,
                                          channel_multiplier=1, allow_small_or_imprecise_dtypes=True))
            nc.gpsimd.affine_select(out=ident[:, :], in_=ident[:, :], compare_op=ALU.not_equal, fill=1.0,
                                    base=0, pattern=[[-1, P]], channel_multiplier=1)
            nc.gpsimd.affine_select(out=upper[:, :], in_=ones[:, :], compare_op=ALU.is_ge, fill=0.0,
                                    base=0, pattern=[[1, P]], channel_multiplier=-1)
            nc.gpsimd.affine_select(out=lower[:, :], in_=ones[:, :], compare_op=ALU.is_ge, fill=0.0,
                                    base=0, pattern=[[-1, P]], channel_multiplier=1)
            nc.gpsimd.affine_select(out=strict[:, :], in_=ones[:, :], compare_op=ALU.is_gt, fill=0.0,
                                    base=0, pattern=[[1, P]], channel_multiplier=-1)
            chain.link(nc.gpsimd.affine_select(out=group_of[:, :], in_=group_of[:, :], compare_op=ALU.is_ge,
                                               fill=0.0, base=0, pattern=[[-HPG, ODD_UNITS]],
                                               channel_multiplier=1))
            nc.gpsimd.affine_select(out=group_of[:, :], in_=group_of[:, :], compare_op=ALU.is_ge, fill=0.0,
                                    base=HPG - 1, pattern=[[HPG, ODD_UNITS]],
                                    channel_multiplier=-1).then_inc(S["consts_pool"], 1)

        @block.scalar
        def _(act):
            chain = Chain(act, S["act_chain"])

            def af(*a, **k):
                return nc.scalar.activation(*a, **k)

            act.dma_start(h[:, :, :], h_d).then_inc(S["x_in"], 16)
            act.dma_start(nmix[:, :, :], norm_mix.rearrange("l (p k) -> p l k", k=KC)).then_inc(S["par_vec"], 16)
            act.dma_start(conv_raw[:, :], odd_conv_w[0].rearrange("k (t c) -> (k t) c", c=P)).then_inc(S["par_conv"], 16)
            act.dma_start(vec_raw[0:32, :], odd_conv_b[0].rearrange("(t c) -> t c", c=P)).then_inc(S["par_conv"], 16)
            act.dma_start(vec_raw[32:48, :], odd_norm_w[0].rearrange("(t c) -> t c", c=P)).then_inc(S["par_conv"], 16)
            act.dma_start(vec_raw[48:60, :], even_conv_w[0].rearrange("k (t c) -> (k t) c", c=P)).then_inc(S["par_conv"], 16)

            def late_params():
                act.dma_start(nffn[:, :, :], norm_ffn.rearrange("l (p k) -> p l k", k=KC)).then_inc(S["par_wr"], 16)
                for l in range(2):
                    act.dma_start(wr[:, l, :, 0:NG],
                                  router_g_w[l].rearrange("(p k) g -> p k g", k=KC)).then_inc(S["par_wr"], 16)
                    for g in range(NG):
                        act.dma_start(wr[:, l, :, NG + EPG * g:NG + EPG * g + EPG],
                                      router_e_w[l, g].rearrange("(p k) e -> p k e", k=KC)).then_inc(S["par_wr"], 16)
                    act.dma_start(rbias[:, l, 0:NG], router_g_b[l].partition_broadcast(P)).then_inc(S["par_wr"], 16)
                    act.dma_start(rbias[:, l, NG:], router_e_b[l].rearrange("g e -> (g e)").partition_broadcast(P)
                                  ).then_inc(S["par_wr"], 16)
                act.dma_start(dtb[:, :], odd_dt_bias[0].partition_broadcast(P)).then_inc(S["par_head"], 16)
                act.dma_start(alog[:, :], odd_a_log[0].partition_broadcast(P)).then_inc(S["par_head"], 16)
                act.dma_start(wdt[:, :, :], w_in_o[:, :, DT0:DT0 + HEADS]).then_inc(S["par_head"], 16)
                act.dma_start(skip_row[:, :], odd_d_skip[0].partition_broadcast(P)).then_inc(S["par_head"], 16)

            def norm(n, wcol):
                if n == 0:
                    act.wait_ge(S["x_in"], 16)
                else:
                    act.wait_ge(S["h_next"], n)
                for t in range(TT):
                    ins = af(junk[:, :], h[:, t, :], ACT.Square, accum_out=st[:, 0, t:t + 1])
                    if t == 0:
                        chain.link(ins)
                ins.then_inc(S["sum_sq"], 1)
                act.wait_ge(S["mean_sq"], n + 1)
                chain.link(af(st[:, 2, :], st[:, 1, :], ACT.Ln))
                af(st[:, 3, :], st[:, 2, :], ACT.Exp, scale=-0.5).then_inc(S["rstd_guess"], 1)
                if wcol is None:
                    return
                act.wait_ge(S["hs_dve"], 2 * n + 1)
                af(hs[:, 1, :, :], h[:, 1, :].rearrange("p (q k) -> p k q", k=KC), ACT.Identity,
                   scale=st[:, 4, 1:2]).then_inc(S["hs_act"], 1)
                for b in (2, 3):
                    act.wait_ge(S["hs_t"], 4 * n + b + 1)
                    for j in range(2):
                        k = 2 * b + j
                        af(hnT[:, k, :], BANKS[b][:, 256 * j:256 * j + 256], ACT.Identity,
                           scale=wcol[:, k:k + 1]).then_inc(S["hnt_act"], 1)

            def even_c0(u):
                act.wait_ge(S["gc_hid"], u + 1)
                if u:
                    act.wait_ge(S["ch_done"], u)
                af(hidS, pa[:, SEQ:2 * SEQ], ACT.Copy).then_inc(S["hid_copied"], 1)

            def even_c1(u):
                act.wait_ge(S["gb_q"], u + 1)
                if u:
                    act.wait_ge(S["conv_done"], u)
                af(gbS, pb[:, 0:SEQ], ACT.Copy).then_inc(S["gb_copied"], 1)
                af(qS[u % 2], pb[:, SEQ:2 * SEQ], ACT.Copy, scale=HD ** -0.5).then_inc(S["q_copied"], 1)

            def even_c2(u):
                act.wait_ge(S["k_v"], u + 1)
                af(kS[u % 2], pa[:, 0:SEQ], ACT.Copy).then_inc(S["kv_copied"], 1)
                af(vS[u % 2], pa2[:, 1, :].rearrange("p (t d) -> p t d", t=TT), ACT.Copy).then_inc(S["kv_copied"], 1)

            def even_attention_scores(u):
                for hh, w in enumerate((wa, wb)):
                    act.wait_ge(S["z_done"], 2 * u + hh + 1)
                    ins = af(zS[:, hh, :], w[:, 0:384], ACT.Copy)
                    ins.then_inc(S["z_copied"], 1)
                act.wait_ge(S["z_copied"], 2 * u + 2)
                chain.link(af(lS, zS, ACT.Abs))
                chain.link(af(lS, lS, ACT.Exp, scale=-1.0))
                af(lS, lS, ACT.Ln, bias=one_c[:, :]).then_inc(S["z_log"], 1)

            def even_attention_weights(u):
                act.wait_ge(S["att_in"], u + 1)
                af(att, att, ACT.Exp).then_inc(S["att_exp"], 1)

            def even_attention_out(u):
                act.wait_ge(S["av_done"], u + 1)
                af(mix[u % 2][:, 1, :], wa[:, 0:SEQ], ACT.Copy).then_inc(S["av_copied"], 1)

            act.wait_ge(S["par_vec"], 16)
            norm(0, nmix[:, 0, :])
            late_params()
            even_c0(0)
            even_c1(0)
            even_c2(0)
            for u in range(EVEN_UNITS):
                more = u + 1 < EVEN_UNITS
                even_attention_scores(u)
                if more:
                    even_c0(u + 1)
                even_attention_weights(u)
                if more:
                    even_c1(u + 1)
                even_attention_out(u)
                if more:
                    even_c2(u + 1)

            def expert_block(E, s):
                act.wait_ge(S["gu_done"], E + 1)
                af(eg, GU[s][:, 0, :], ACT.Exp, scale=-1.0).then_inc(S["gexp"], 1)
                act.wait_ge(S["ht_done"], E + 1)
                af(hT, HT_ps, ACT.Copy).then_inc(S["ht_copied"], 1)
                act.wait_ge(S["dn_done"], E + 1)
                af(ysb[s], Y_ps, ACT.Copy).then_inc(S["y_copied"], 1)

            def overflow(k, s):
                act.wait_ge(S["ov_gu"], k + 1)
                af(o_eg, GU[s][:, 0, :], ACT.Exp, scale=-1.0).then_inc(S["ov_exp"], 1)
                act.wait_ge(S["ov_ht"], k + 1)
                af(o_hT, HT_ps, ACT.Copy).then_inc(S["ov_htc"], 1)
                act.wait_ge(S["ov_dn"], k + 1)
                af(o_y, Y_ps, ACT.Copy).then_inc(S["ov_yc"], 1)

            def moe(l):
                if l == 0:
                    act.wait_ge(S["par_wr"], 15 * 16)
                norm(2 * l + 1, nffn[:, l, :])
                act.wait_ge(S["route_d"], l + 1)
                if l:
                    act.dma_start(fnorm, final_norm.partition_broadcast(P)).then_inc(S["fnorm_in"], 16)
                af(ee[:, :, 0:5], dd[:, :, 0:5], ACT.Exp).then_inc(S["route_e"], 1)
                act.wait_ge(S["pos_t"], l + 1)
                af(PG, wa[0:NE, :], ACT.Copy).then_inc(S["pg_done"], 1)
                act.wait_ge(S["table_done"], l + 1)
                with act.Fori(0, NE // 2) as i:
                    for s in range(2):
                        e = i * 2 + s
                        expert_block(e + NE * l, s)
                        k0 = act.value_load(table[0:1, ds(e + (NE + 1) * l, 1)], min_val=0, max_val=2 * NE)
                        k1 = act.value_load(table[0:1, ds(e + ((NE + 1) * l + 1), 1)], min_val=0, max_val=2 * NE)
                        with act.If(k0 < k1):
                            with act.Fori(k0, k1) as k:
                                overflow(k, s)

            moe(0)

            def odd_z(g):
                act.wait_ge(S["z1_done"], g + 1)
                af(ez, pa2, ACT.Exp, scale=-1.0).then_inc(S["z1_exp"], 1)

            def first_tap(src, tiles):
                for j, tile in enumerate(tiles):
                    ins = af(cv[:, j, :], src[:, j, :], ACT.Identity, scale=conv_cols[:, ds(tile + 3 * 32, 1)],
                             bias=vec_cols[:, ds(tile, 1)])
                return ins

            def odd_x(g):
                act.wait_ge(S["x1_done"], g + 1)
                if not isinstance(g, int) or g:
                    act.wait_ge(S["bc_silu"], g)
                first_tap(pb2, [g * 2, g * 2 + 1]).then_inc(S["x1_tap"], 1)
                act.wait_ge(S["x1_conv"], g + 1)
                af(ecv, cv, ACT.Exp, scale=-1.0).then_inc(S["x1_exp"], 1)

            def odd_bc(g):
                act.wait_ge(S["bc_done"], g + 1)
                act.wait_ge(S["x1_silu"], g + 1)
                first_tap(pa2, [g + 16, g + 24]).then_inc(S["bc_tap"], 1)
                act.wait_ge(S["bc_conv"], g + 1)
                af(ecv, cv, ACT.Exp, scale=-1.0).then_inc(S["bc_exp"], 1)

            def odd_decay(g):
                act.wait_ge(S["seg_done"], g + 1)
                af(decay[:, 0:2, :, :], decay[:, 0:2, :, :], ACT.Exp)
                af(decay[:, 2, :, :], wb[:, :].rearrange("p (r l) -> p r l", r=HPG), ACT.Exp
                   ).then_inc(S["decay_done"], 1)

            def odd_rstd(g):
                act.wait_ge(S["yms_done"], g + 1)
                chain.link(af(rg, ms, ACT.Ln))
                af(rg, rg, ACT.Exp, scale=-0.5).then_inc(S["yguess"], 1)

            norm(2, nmix[:, 1, :])
            act.wait_ge(S["par_head"], 4 * 16)
            act.wait_ge(S["dt_pre"], 1)
            chain.link(af(dta, dtv, ACT.Abs))
            chain.link(af(dta, dta, ACT.Exp, scale=-1.0))
            af(dta, dta, ACT.Ln, bias=one_c[:, :]).then_inc(S["dt_ln"], 1)
            af(w0, alog[:, :], ACT.Exp).then_inc(S["alog_exp"], 1)
            act.wait_ge(S["cum_done"], 1)
            act.wait_ge(S["cum_used"], 1)
            af(w0, dtw, ACT.Exp).then_inc(S["alog_exp"], 1)
            odd_z(0)
            odd_x(0)
            odd_bc(0)

            def odd_unit(g, more):
                odd_decay(g)
                if more:
                    odd_z(g + 1)
                    odd_x(g + 1)
                odd_rstd(g)
                if more:
                    odd_bc(g + 1)

            with chain.loop(0, ODD_UNITS - 1, 1) as g:
                odd_unit(g, True)
            odd_unit(ODD_UNITS - 1, False)

            moe(1)
            norm(4, None)

        @block.vector
        def _(dve):
            chain = Chain(dve, S["dve_chain"])
            v = nc.vector
            link = chain.link

            def newton(r, x, tmp):
                link(v.tensor_tensor(tmp, r, r, ALU.mult))
                link(v.tensor_tensor(tmp, tmp, x, ALU.mult))
                link(v.tensor_scalar(tmp, tmp, -0.5, 1.5, ALU.mult, ALU.add))

            def norm(n, wcol):
                dve.wait_ge(S["sum_sq"], n + 1)
                v.tensor_scalar(st[:, 1, :], st[:, 0, :], 1.0 / D, EPS, ALU.mult, ALU.add).then_inc(S["mean_sq"], 1)
                dve.wait_ge(S["rstd_guess"], n + 1)
                newton(st[:, 3, :], st[:, 1, :], st[:, 5, :])
                v.tensor_tensor(st[:, 4, :], st[:, 3, :], st[:, 5, :], ALU.mult).then_inc(S["hs_dve"], 1)
                dve.wait_ge(S["hs_dve"], 2 * n + 1)
                if wcol is None:
                    return
                v.tensor_scalar(hs[:, 0, :, :], h[:, 0, :].rearrange("p (q k) -> p k q", k=KC),
                                st[:, 4, 0:1], None, ALU.mult).then_inc(S["hs_dve"], 1)
                for b in (0, 1):
                    dve.wait_ge(S["hs_t"], 4 * n + b + 1)
                    v.tensor_tensor(hnT[:, 2 * b:2 * b + 2, :], BANKS[b][:, :].rearrange("p (a b) -> p a b", a=2),
                                    wcol[:, 2 * b:2 * b + 2].unsqueeze(2).to_broadcast([P, 2, SEQ]),
                                    ALU.mult).then_inc(S["hnt_dve"], 1)

            def residual_mixer(l):
                dve.wait_ge(S["oproj"], (EVEN_UNITS, EVEN_UNITS + ODD_UNITS)[l])
                for t in range(TT):
                    for n in range(2):
                        ins = v.tensor_tensor(h[:, t, 512 * n:512 * n + 512], h[:, t, 512 * n:512 * n + 512],
                                              acc[:, 2 * t + n, :], ALU.add)
                        if t + n < 2:
                            link(ins)
                ins.then_inc(S["h_next"], 1)

            dve.wait_ge(S["consts_pool"], 1)
            v.tensor_reduce(out=rank_of[:, :], in_=ident[0:HEADS, 0:HEADS].rearrange("p (g r) -> p r g", r=HPG),
                            axis=AX, op=ALU.add).then_inc(S["consts_dve"], 1)
            v.memset(ch[:, 0:2], 0.0).then_inc(S["consts_dve"], 1)
            v.memset(table[:, 0:1], 0).then_inc(S["ov_done"], 1)
            dve.wait_ge(S["conv_raw_t"], 1)
            v.tensor_copy(conv_cols[:, :], pa[:, 0:P]).then_inc(S["conv_cols"], 1)
            v.tensor_copy(vec_cols[:, :], pa[:, P:P + 60]).then_inc(S["conv_cols"], 1)
            dve.wait_ge(S["conv_cols"], 2)

            def even_ch(u):
                dve.wait_ge(S["hid_copied"], u + 1)
                v.tensor_tensor(ch[:, 2:], pa[:, 0:SEQ], hidS, ALU.mult).then_inc(S["ch_done"], 1)
                dve.wait_ge(S["ch_done"], u + 1)

            def even_conv(u):
                def tap(k):
                    return vec_cols[:, 48 + 4 * k + u:49 + 4 * k + u]
                link(v.tensor_scalar(cacc, ch[:, 2:], tap(2), None, ALU.mult))
                link(v.scalar_tensor_tensor(cacc, ch[:, 1:1 + SEQ], tap(1), cacc, ALU.mult, ALU.add))
                link(v.scalar_tensor_tensor(cacc, ch[:, 0:SEQ], tap(0), cacc, ALU.mult, ALU.add))
                dve.wait_ge(S["gb_copied"], u + 1)
                if u >= 2:
                    dve.wait_ge(S["oproj"], u - 1)
                v.tensor_tensor(mix[u % 2][:, 0, :], cacc, gbS, ALU.mult).then_inc(S["conv_done"], 1)

            def diag(a):
                return a.rearrange("p h (b l) -> p h b l", l=P)

            def even_softplus(u):
                dve.wait_ge(S["z_log"], u + 1)
                if u:
                    dve.wait_ge(S["r_done"], 2 * u)
                link(v.scalar_tensor_tensor(sp, zS, 0.0, lS, ALU.max, ALU.add))
                for hh in range(2):
                    d = diag(sp)[:, hh, 0:3:2, :]
                    ins = v.tensor_tensor(d, d, strict[:, :].unsqueeze(1).to_broadcast([P, 2, P]), ALU.mult)
                    ins.then_inc(S["sp_done"], 1)

            def even_weights_in(u):
                for hh, w in enumerate((wa, wb)):
                    dve.wait_ge(S["r_done"], 2 * u + hh + 1)
                    ins = v.tensor_tensor(att[:, hh, :], zS[:, hh, :], w[:, 0:384], ALU.subtract)
                link(ins)
                v.tensor_scalar(att, att, 0.0, None, ALU.min).then_inc(S["att_in"], 1)

            def even_weights_mask(u):
                dve.wait_ge(S["att_exp"], u + 1)
                for hh in range(2):
                    d = diag(att)[:, hh, 0:3:2, :]
                    v.tensor_tensor(d, d, strict[:, :].unsqueeze(1).to_broadcast([P, 2, P]), ALU.mult
                                    ).then_inc(S["att_done"], 1)

            dve.wait_ge(S["par_vec"], 16)
            norm(0, nmix[:, 0, :])
            even_ch(0)
            even_conv(0)
            for u in range(EVEN_UNITS):
                more = u + 1 < EVEN_UNITS
                even_softplus(u)
                if more:
                    even_ch(u + 1)
                even_weights_in(u)
                even_weights_mask(u)
                if more:
                    even_conv(u + 1)
            residual_mixer(0)

            def one_hot_first(dst, src, m, n, tmp):
                def col(a):
                    return a.unsqueeze(2).to_broadcast([P, TT, n])
                link(v.tensor_reduce(out=m, in_=src, axis=AX, op=ALU.max))
                link(v.tensor_tensor(tmp, src, col(m), ALU.is_equal))
                link(v.tensor_tensor(tmp, tmp, descend[:, 0:n].unsqueeze(1).to_broadcast([P, TT, n]), ALU.mult))
                link(v.tensor_reduce(out=m8[:, 7, :], in_=tmp, axis=AX, op=ALU.max))
                link(v.tensor_tensor(dst, tmp, col(m8[:, 7, :]), ALU.is_equal))

            def bc(a, n):
                return a.unsqueeze(2).to_broadcast([P, TT, n])

            def route(l):
                dve.wait_ge(S["logits"], l + 1)
                plog = pa[:, 0:P].rearrange("p (t n) -> p t n", t=TT)[:, :, 0:NG + NE]
                link(v.tensor_tensor(lg, plog, rbias[:, l, :].unsqueeze(1).to_broadcast([P, TT, NG + NE]), ALU.add))
                gmax, m1, m2, gs, s1, g1, g2 = (m8[:, j, :] for j in range(7))
                one_hot_first(rt2[:, :, 0:NG], lg[:, :, 0:NG], gmax, NG, rt1[:, :, 0:NG])
                link(v.tensor_tensor(dd[:, :, 0:NG], lg[:, :, 0:NG], bc(gmax, NG), ALU.subtract))
                link(v.tensor_scalar(rt2[:, :, 0:NG], rt2[:, :, 0:NG], BIG, -BIG, ALU.mult, ALU.add))
                for t in range(TT):
                    link(v.tensor_tensor(lg[:, t, NG:].rearrange("p (g e) -> p g e", g=NG),
                                         lg[:, t, NG:].rearrange("p (g e) -> p g e", g=NG),
                                         rt2[:, t, 0:NG].unsqueeze(2).to_broadcast([P, NG, EPG]), ALU.add))
                ex = lg[:, :, NG:]
                one_hot_first(oh1, ex, m1, NE, rt1)
                link(v.scalar_tensor_tensor(ex, oh1, -2.0 * BIG, ex, ALU.mult, ALU.add))
                one_hot_first(oh2, ex, m2, NE, rt1)
                v.tensor_tensor(dd[:, :, 4:5], m2.unsqueeze(2), m1.unsqueeze(2), ALU.subtract).then_inc(S["route_d"], 1)
                v.tensor_tensor(mask, oh1, oh2, ALU.add).then_inc(S["mask_done"], 1)
                dve.wait_ge(S["route_e"], l + 1)
                link(v.tensor_reduce(out=gs, in_=ee[:, :, 0:NG], axis=AX, op=ALU.add))
                link(v.tensor_scalar(s1, ee[:, :, 4:5].rearrange("p t o -> p (t o)"), 1.0, None, ALU.add))
                link(v.tensor_tensor(s1, s1, gs, ALU.mult))
                link(v.reciprocal(g1, s1))
                link(v.tensor_tensor(g2, g1, ee[:, :, 4:5].rearrange("p t o -> p (t o)"), ALU.mult))
                link(v.tensor_tensor(oh1, oh1, bc(g1, NE), ALU.mult))
                link(v.tensor_tensor(oh2, oh2, bc(g2, NE), ALU.mult))
                link(v.tensor_tensor(gates, oh1, oh2, ALU.add))
                dve.wait_ge(S["ranks"], l + 1)
                prk = pb[:, 0:2 * NE].rearrange("p (t n) -> p t n", t=TT)
                link(v.memset(pos[:, :, NE:], -1.0))
                link(v.tensor_tensor(pos[:, :, 0:NE], prk, mask, ALU.mult))
                v.tensor_scalar(pos[:, :, 0:NE], pos[:, :, 0:NE], -1.0, None, ALU.add).then_inc(S["mask_done"], 1)
                dve.wait_ge(S["mask_done"], 2 * l + 2)
                cs, ov = cnt[0:1, 0:NE], cnt[0:1, NE:2 * NE]
                link(v.tensor_copy(cs, pb[0:1, 2 * NE:3 * NE]))
                link(v.tensor_scalar(ov, cs, float(CAP), None, ALU.is_gt))
                for b in range(2, MAXB):
                    link(v.scalar_tensor_tensor(ov, cs, float(CAP * b), ov, ALU.is_gt, ALU.add))
                base = (NE + 1) * l
                if l:
                    link(v.tensor_copy(table[:, base:base + 1], table[:, base - 1:base]))
                link(v.tensor_copy(cnt[0:1, 2 * NE:2 * NE + 1], table[:, base:base + 1]))
                v.tensor_tensor_scan(table[:, base + 1:base + NE + 1], ones[0:1, 0:NE], ov,
                                     cnt[0:1, 2 * NE:2 * NE + 1], ALU.mult, ALU.add).then_inc(S["table_done"], 1)
                link(v.memset(G4[1], 0.0))
                v.memset(ysb[1], 0.0).then_inc(S["y_copied"], 1)

            def prep_select(e, l, s):
                if isinstance(e, int) and e == 0:
                    link(v.tensor_scalar(sel, ident[0:NE, 0:1].to_broadcast([NE, P]), 1.0, None, ALU.mult))
                else:
                    link(v.tensor_scalar(sel, ident[0:NE, ds(e, 1)].to_broadcast([NE, P]), 1.0, None, ALU.mult))
                v.tensor_tensor(Ssel[s], iota[:, :].unsqueeze(1).to_broadcast([P, TT, CAP]),
                                pos[:, :, ds(e, 1)].to_broadcast([P, TT, CAP]), ALU.is_equal
                                ).then_inc(S["prep_sel"], 1)

            def prep_gates(e, l, s, combine=True):
                dve.wait_ge(S["b_done"], e + (NE + 1) * l + 1)
                if combine:
                    dve.wait_ge(S["comb_done"], e + (NE + 1) * l)
                link(v.tensor_scalar(G4[s], B_ps[:, 0:SEQ], slot_id[:, :], None, ALU.is_equal))
                v.tensor_tensor(G4[s], G4[s], B_ps[:, SEQ:], ALU.mult).then_inc(S["g4_done"], 1)
                dve.wait_ge(S["gath_done"], e + (NE + 1) * l + 1)
                v.tensor_tensor(xs[s], XG, nffn[:, l, :].unsqueeze(2).to_broadcast([P, KC, CAP]), ALU.mult
                                ).then_inc(S["xs_done"], 1)

            def overflow(e, k, l, s):
                oc = Chain(dve, S["ovf_chain"], k * 8)
                dve.wait_ge(S["ov_done"], k + 1)
                oc.link(v.tensor_scalar(o_sel, ident[0:NE, ds(e, 1)].to_broadcast([NE, P]), 1.0, None, ALU.mult))
                v.tensor_tensor(o_S, o_iota.unsqueeze(1).to_broadcast([P, TT, CAP]),
                                pos[:, :, ds(e, 1)].to_broadcast([P, TT, CAP]), ALU.is_equal).then_inc(S["ov_sel"], 1)
                dve.wait_ge(S["ov_b"], k + 1)
                oc.link(v.tensor_scalar(o_G4, B_ps[:, 0:SEQ], o_slot, None, ALU.is_equal))
                oc.link(v.tensor_tensor(o_G4, o_G4, B_ps[:, SEQ:], ALU.mult))
                v.tensor_tensor(o_xs, XG, nffn[:, l, :].unsqueeze(2).to_broadcast([P, KC, CAP]), ALU.mult
                                ).then_inc(S["ov_x"], 1)
                oc.link(v.tensor_scalar(o_iota, o_iota, float(CAP), None, ALU.add))
                oc.link(v.tensor_scalar(o_slot, o_slot, float(CAP), None, ALU.add))
                dve.wait_ge(S["ov_exp"], k + 1)
                oc.link(v.tensor_scalar(o_eg, o_eg, 1.0, None, ALU.add))
                oc.link(v.reciprocal(o_eg, o_eg))
                oc.link(v.tensor_tensor(o_eg, o_eg, GU[s][:, 0, :], ALU.mult))
                v.tensor_tensor(o_h, o_eg, GU[s][:, 1, :], ALU.mult).then_inc(S["ov_h"], 1)
                assert oc.n == 8

            def moe(l):
                if l == 0:
                    dve.wait_ge(S["par_wr"], 15 * 16)
                norm(2 * l + 1, nffn[:, l, :])
                route(l)
                dve.wait_ge(S["pg_done"], l + 1)
                prep_select(0, l, 0)
                prep_gates(0, l, 0, combine=False)
                with chain.loop(0, NE // 2, 2 * 7) as i:
                    for s in range(2):
                        e = i * 2 + s
                        E = e + NE * l
                        prep_select(e + 1, l, 1 - s)
                        dve.wait_ge(S["gexp"], E + 1)
                        link(v.tensor_scalar(eg, eg, 1.0, None, ALU.add))
                        link(v.reciprocal(eg, eg))
                        link(v.tensor_tensor(eg, eg, GU[s][:, 0, :], ALU.mult))
                        v.tensor_tensor(hb, eg, GU[s][:, 1, :], ALU.mult).then_inc(S["h_done"], 1)
                        k0 = dve.value_load(table[0:1, ds(e + (NE + 1) * l, 1)], min_val=0, max_val=2 * NE)
                        k1 = dve.value_load(table[0:1, ds(e + ((NE + 1) * l + 1), 1)], min_val=0, max_val=2 * NE)
                        link(v.tensor_scalar(o_iota, iota[:, :], float(CAP), None, ALU.add))
                        link(v.tensor_scalar(o_slot, slot_id[:, :], float(CAP), None, ALU.add))
                        prep_gates(e + 1, l, 1 - s)
                        with dve.If(k0 < k1):
                            with dve.Fori(k0, k1) as k:
                                overflow(e, k, l, s)
                dve.wait_ge(S["comb_done"], (NE + 1) * (l + 1))
                for c in range(4):
                    a = h[:, :, 256 * c:256 * c + 256]
                    ins = v.tensor_tensor(a, a, acc[:, c, :].rearrange("p (t n) -> p t n", t=TT), ALU.add)
                    if c < 3:
                        link(ins)
                ins.then_inc(S["h_next"], 1)

            moe(0)

            norm(2, nmix[:, 1, :])

            def odd_z(g, p):
                dve.wait_ge(S["z1_exp"], g + 1)
                link(v.tensor_scalar(ez, ez, 1.0, None, ALU.add))
                link(v.reciprocal(ez, ez))
                v.tensor_tensor(sz[p], ez, pa2, ALU.mult).then_inc(S["z1_silu"], 1)

            def taps(src, tiles):
                for m in (1, 2, 3):
                    for j, tile in enumerate(tiles):
                        w = conv_cols[:, ds(tile + (3 - m) * 32, 1)]
                        ins = v.scalar_tensor_tensor(cv[:, j, m:], src[:, j, 0:SEQ - m], w, cv[:, j, m:],
                                                     ALU.mult, ALU.add)
                    if m < 3:
                        link(ins)
                return ins

            def odd_x(g, p):
                dve.wait_ge(S["x1_tap"], g + 1)
                taps(pb2, [g * 2, g * 2 + 1]).then_inc(S["x1_conv"], 1)
                dve.wait_ge(S["x1_exp"], g + 1)
                link(v.tensor_scalar(ecv, ecv, 1.0, None, ALU.add))
                link(v.reciprocal(ecv, ecv))
                v.tensor_tensor(xT[p], cv, ecv, ALU.mult).then_inc(S["x1_silu"], 1)

            def odd_bc(g, p):
                dve.wait_ge(S["bc_tap"], g + 1)
                taps(pa2, [g + 16, g + 24]).then_inc(S["bc_conv"], 1)
                dve.wait_ge(S["bc_exp"], g + 1)
                link(v.tensor_scalar(ecv, ecv, 1.0, None, ALU.add))
                link(v.reciprocal(ecv, ecv))
                v.tensor_tensor(bcT[p], cv, ecv, ALU.mult).then_inc(S["bc_silu"], 1)

            def group_selector(g):
                v.tensor_scalar(gsel, group_of[:, ds(g, 1)].to_broadcast([HEADS, P]), 1.0, None, ALU.mult).then_inc(S["gsel_done"], 1)

            dve.wait_ge(S["par_head"], 4 * 16)
            for q in range(2):
                v.tensor_copy(dskip[64 * q:64 * q + 64, :], skip_row[64 * q:64 * q + 64, q:HEADS:2])
            dve.wait_ge(S["dt_raw"], 1)
            v.tensor_tensor(dtv, pa[:, 0:TT * HEADS].rearrange("p (t n) -> p t n", t=TT),
                            dtb[:, :].unsqueeze(1).to_broadcast([P, TT, HEADS]), ALU.add).then_inc(S["dt_pre"], 1)
            dve.wait_ge(S["dt_ln"], 1)
            link(v.scalar_tensor_tensor(dtv, dtv, 0.0, dta, ALU.max, ALU.add))
            dve.wait_ge(S["alog_exp"], 1)
            link(v.tensor_tensor(dta, dtv, w0.unsqueeze(1).to_broadcast([P, TT, HEADS]), ALU.mult))
            v.tensor_scalar(dta, dta, -1.0, None, ALU.mult).then_inc(S["dt_a"], 1)
            dve.wait_ge(S["cum_done"], 1)
            cum = pb[:, 0:TT * HEADS].rearrange("p (t n) -> p t n", t=TT)
            link(v.tensor_copy(csn, cum))
            v.tensor_tensor(dtw, pb[:, 64:96], csn[:, 0, :], ALU.subtract).then_inc(S["cum_used"], 1)
            for b in range(2):
                link(v.tensor_tensor(csx[:, b, :, :],
                                     wa[0:HEADS, P * b:P * b + P].unsqueeze(1).to_broadcast([HEADS, HPG, P]),
                                     rank_of[:, :].unsqueeze(2).to_broadcast([HEADS, HPG, P]), ALU.mult))
            dve.wait_ge(S["alog_exp"], 2)
            v.tensor_tensor(dtw, dtv[:, 0, :], w0, ALU.mult).then_inc(S["csx_done"], 1)
            group_selector(0)
            odd_z(0, 0)
            odd_x(0, 0)
            odd_bc(0, 0)

            def odd_unit(g, p, more):
                dve.wait_ge(S["csrow_done"], g + 1)
                for b, w in enumerate((wa, wb)):
                    for r in range(HPG):
                        ins = v.tensor_scalar(decay[:, b, r, :], w[:, P * r:P * r + P],
                                              csn[:, b, ds(g * HPG + r, 1)], 0.0, ALU.subtract, ALU.min)
                ins.then_inc(S["seg_done"], 1)
                dve.wait_ge(S["cb_done"], g + 1)
                dve.wait_ge(S["decay_done"], g + 1)
                for c, m in ((0, True), (1, False), (2, True)):
                    a = cbs[:, P * c:P * c + P]
                    src = wa[:, P * c:P * c + P]
                    ins = v.tensor_tensor(a, src, upper[:, :], ALU.mult) if m else v.tensor_copy(a, src)
                link(ins)

                def heads(c):
                    return cbs[:, P * c:P * c + P].unsqueeze(1).to_broadcast([P, HPG, P])
                for b, c in ((0, 0), (1, 2)):
                    v.tensor_tensor(decay[:, b], decay[:, b], heads(c), ALU.mult)
                v.tensor_tensor(decay[:, 2], decay[:, 2], heads(1), ALU.mult)
                dve.wait_ge(S["xst_done"], g + 1)
                for t in range(TT):
                    v.tensor_tensor(xdt[:, t, :].rearrange("p (r d) -> p r d", r=HPG),
                                    wb[:, 256 * t:256 * t + 256].rearrange("p (r d) -> p r d", r=HPG),
                                    dtv[:, t, ds(g * HPG, HPG)].unsqueeze(2).to_broadcast([P, HPG, HD]),
                                    ALU.mult)
                v.tensor_tensor(xw.rearrange("p (r d) -> p r d", r=HPG),
                                wb[:, 0:256].rearrange("p (r d) -> p r d", r=HPG),
                                dtw[:, ds(g * HPG, HPG)].unsqueeze(2).to_broadcast([P, HPG, HD]),
                                ALU.mult).then_inc(S["xdt_done"], 1)
                if more:
                    odd_z(g + 1, 1 - p)
                    odd_x(g + 1, 1 - p)
                dve.wait_ge(S["y_done"], g + 1)
                for j in range(2):
                    ins = v.scalar_tensor_tensor(yz[:, j, :], xT[p][:, j, :], dskip[:, ds(g * 2 + j, 1)],
                                                 wa[:, 256 * j:256 * j + 256], ALU.mult, ALU.add)
                link(ins)
                link(v.tensor_tensor(yz, yz, sz[p], ALU.mult))
                v.tensor_tensor(sq, yz, yz, ALU.mult).then_inc(S["yz_done"], 1)
                dve.wait_ge(S["yss_done"], g + 1)
                v.tensor_scalar(ms, wb[:, 0:SEQ], 1.0 / 256, EPS, ALU.mult, ALU.add).then_inc(S["yms_done"], 1)
                dve.wait_ge(S["yguess"], g + 1)
                newton(rg, ms, rt)
                link(v.tensor_tensor(rg, rg, rt, ALU.mult))
                dve.wait_ge(S["oproj"], g + EVEN_UNITS - 1)
                for j in range(2):
                    ins = v.scalar_tensor_tensor(mix1[p][:, j, :], yz[:, j, :], vec_cols[:, ds(g * 2 + (32 + j), 1)],
                                                 rg, ALU.mult, ALU.mult)
                ins.then_inc(S["mix1_done"], 1)
                if more:
                    group_selector(g + 1)
                    odd_bc(g + 1, 1 - p)

            with chain.loop(0, (ODD_UNITS - 2) // 2, 2 * 17) as i:
                for p in range(2):
                    odd_unit(i * 2 + p, p, True)
            odd_unit(ODD_UNITS - 2, 0, True)
            odd_unit(ODD_UNITS - 1, 1, False)
            residual_mixer(1)

            moe(1)
            norm(4, None)
            dve.wait_ge(S["fnorm_in"], 16)
            for t in range(TT):
                ins = v.scalar_tensor_tensor(y_out[:, t, :], h[:, t, :], st[:, 4, t:t + 1], fnorm,
                                             ALU.mult, ALU.mult)
                if t == 0:
                    link(ins)
            ins.then_inc(S["h_next"], 1)

        @block.tensor
        def _(pe):
            mm = nc.tensor.matmul

            def zero_acc():
                for b in range(4):
                    ins = mm(acc[:, b, :], zero_bf[:, 0:P], zero_bf[:, :], start=True, stop=True,
                             skip_group_check=True)
                return ins

            def transposes(n):
                pe.wait_ge(S["hs_dve"], 2 * n + 2)
                pe.wait_ge(S["hs_act"], n + 1)
                for b in range(4):
                    for j in range(2):
                        for t in range(TT):
                            o = BANKS[b][:, 256 * j + P * t:256 * j + P * t + P]
                            ins = nc.tensor.transpose(o, hs[:, t, 2 * b + j, :], ident[:, :])
                    ins.then_inc(S["hs_t"], 1)
                pe.wait_ge(S["hnt_dve"], 2 * n + 2)
                pe.wait_ge(S["hnt_act"], 4 * n + 4)

            def project(dst, w, j, used=None):
                for k in range(KC):
                    ins = mm(dst, w[:, k, j, :], hnT[:, k, :], start=(k == 0), stop=(k == KC - 1))
                return ins

            def out_project(m, u):
                pe.wait_ge(S["wo_in"], (u + 1) * 16)
                for t in range(TT):
                    for n in range(2):
                        for j in range(2):
                            ins = mm(acc[:, 2 * t + n, :], m[:, j, P * t:P * t + P], w_o[:, j, 512 * n:512 * n + 512],
                                     start=False, stop=False, skip_group_check=True)
                ins.then_inc(S["oproj"], 1)

            pe.wait_ge(S["consts_pool"], 1)
            pe.wait_ge(S["par_conv"], 64)
            nc.tensor.transpose(pa[:, 0:P], conv_raw[:, :], ident[:, :])
            nc.tensor.transpose(pa[:, P:P + 60], vec_raw[:, :], ident[0:60, 0:60]).then_inc(S["conv_raw_t"], 1)
            zero_acc()
            pe.wait_ge(S["conv_cols"], 2)
            transposes(0)

            def even_c0(u):
                pe.wait_ge(S["c0_in"], 16 * (u + 1))
                if u:
                    pe.wait_ge(S["kv_copied"], 2 * u)
                project(pa[:, 0:SEQ], w_c[0], 0)
                project(pa[:, SEQ:], w_c[0], 1).then_inc(S["gc_hid"], 1)

            def even_c1(u):
                pe.wait_ge(S["c1_in"], 16 * (u + 1))
                if u:
                    pe.wait_ge(S["q_copied"], u)
                project(pb[:, 0:SEQ], w_c[1], 0)
                project(pb[:, SEQ:], w_c[1], 1).then_inc(S["gb_q"], 1)

            def even_c2(u):
                pe.wait_ge(S["c2_in"], 16 * (u + 1))
                pe.wait_ge(S["ch_done"], u + 1)
                project(pa[:, 0:SEQ], w_c[2], 0)
                for t in range(TT):
                    for k in range(KC):
                        ins = mm(pa[:, SEQ + P * t:SEQ + P * t + P], hnT[:, k, P * t:P * t + P], w_c[2][:, k, 1, :],
                                 start=(k == 0), stop=(k == KC - 1))
                ins.then_inc(S["k_v"], 1)

            def even_scores(u):
                pe.wait_ge(S["kv_copied"], 2 * u + 2)
                pe.wait_ge(S["q_copied"], u + 1)
                if u:
                    pe.wait_ge(S["av_copied"], u)
                q, k = qS[u % 2], kS[u % 2]
                for hh, w in enumerate((wa, wb)):
                    r = slice(HD * hh, HD * hh + HD)
                    mm(w[:, 0:SEQ], k[r, 0:P], q[r, :], start=True, stop=True)
                    mm(w[:, SEQ:SEQ + P], k[r, P:SEQ], q[r, P:SEQ], start=True, stop=True).then_inc(S["z_done"], 1)

            def even_suffix(u):
                pe.wait_ge(S["sp_done"], 2 * u + 2)
                pe.wait_ge(S["z_copied"], 2 * u + 2)
                for hh, w in enumerate((wa, wb)):
                    mm(w[:, 0:384], lower[:, :], sp[:, hh, :], start=True, stop=False, skip_group_check=True)
                    mm(w[:, P:SEQ], ones[:, :], sp[:, hh, SEQ:], start=False, stop=True,
                       skip_group_check=True).then_inc(S["r_done"], 1)

            def even_values(u):
                pe.wait_ge(S["att_done"], 2 * u + 2)
                vv = vS[u % 2]
                for hh in range(2):
                    o = wa[HD * hh:HD * hh + HD, :]
                    c = slice(HD * hh, HD * hh + HD)
                    mm(o[:, 0:SEQ], vv[:, 0, c], att[:, hh, 0:SEQ], start=True, stop=False, skip_group_check=True)
                    ins = mm(o[:, P:SEQ], vv[:, 1, c], att[:, hh, SEQ:], start=False, stop=True,
                             skip_group_check=True)
                ins.then_inc(S["av_done"], 1)

            def even_out(u):
                pe.wait_ge(S["conv_done"], u + 1)
                pe.wait_ge(S["av_copied"], u + 1)
                out_project(mix[u % 2], u)

            even_c0(0)
            even_c1(0)
            even_c2(0)
            for u in range(EVEN_UNITS):
                more = u + 1 < EVEN_UNITS
                even_scores(u)
                if more:
                    even_c0(u + 1)
                even_suffix(u)
                if more:
                    even_c1(u + 1)
                even_values(u)
                if more:
                    even_c2(u + 1)
                even_out(u)

            def route(l):
                transposes(2 * l + 1)
                if l == 0:
                    pe.wait_ge(S["par_wr"], 15 * 16)
                for t in range(TT):
                    for k in range(KC):
                        ins = mm(pa[:, 64 * t:64 * t + NG + NE], hnT[:, k, P * t:P * t + P], wr[:, l, k, :],
                                 start=(k == 0), stop=(k == KC - 1))
                ins.then_inc(S["logits"], 1)
                pe.wait_ge(S["h_next"], 2 * l + 1)
                zero_acc()
                pe.wait_ge(S["mask_done"], 2 * l + 1)
                mm(pb[:, 0:NE], upper[:, :], mask[:, 0, :], start=True, stop=True)
                mm(pb[:, NE:2 * NE], upper[:, :], mask[:, 1, :], start=True, stop=False)
                mm(pb[:, NE:2 * NE], ones[:, :], mask[:, 0, :], start=False, stop=True)
                mm(pb[:, 2 * NE:3 * NE], ones[:, :], mask[:, 0, :], start=True, stop=False)
                mm(pb[:, 2 * NE:3 * NE], ones[:, :], mask[:, 1, :], start=False, stop=True).then_inc(S["ranks"], 1)
                pe.wait_ge(S["mask_done"], 2 * l + 2)
                for t in range(TT):
                    nc.tensor.transpose(wa[0:NE, P * t:P * t + P], pos[:, t, 0:NE], ident[:, :])
                    ins = nc.tensor.transpose(wa[0:NE, SEQ + P * t:SEQ + P * t + P], gates[:, t, :], ident[:, :])
                ins.then_inc(S["pos_t"], 1)

            def gather(selector, slots, done_b=None):
                ins = mm(B_ps[:, :], selector, PG, start=True, stop=True)
                if done_b is not None:
                    ins.then_inc(done_b, 1)
                for k in range(KC):
                    for t in range(TT):
                        ins = mm(XG[:, k, :], hs[:, t, k, :], slots[:, t, :], start=(t == 0), stop=(t == TT - 1))
                return ins

            def prep(e, l, s):
                pe.wait_ge(S["prep_sel"], e + (NE + 1) * l + 1)
                if l or not (isinstance(e, int) and e == 0):
                    pe.wait_ge(S["g4_done"], e + (NE + 1) * l)
                    pe.wait_ge(S["xs_done"], e + (NE + 1) * l)
                gather(sel, Ssel[s], S["b_done"]).then_inc(S["gath_done"], 1)

            def gate_up(xb, s):
                for k in range(KC):
                    for j in range(4):
                        ins = mm(GU[s][32 * j:32 * j + 32, :, :], xb[:, k, :], w_gu[s][:, :, k, P * j:P * j + P],
                                 start=(k == 0), stop=(k == KC - 1))
                return ins

            def down(ht, s):
                for j in range(4):
                    for c in range(4):
                        ins = mm(Y_ps[32 * c:32 * c + 32, :], ht[:, 32 * j:32 * j + 32],
                                 w_dn[s][:, j, 256 * c:256 * c + 256], start=(j == 0), stop=(j == 3))
                return ins

            def combine(g4, y):
                for t in range(TT):
                    for c in range(4):
                        r = slice(32 * c, 32 * c + 32)
                        ins = mm(acc[:, c, 256 * t:256 * t + 256], g4[r, P * t:P * t + P], y[r, :],
                                 start=False, stop=False, skip_group_check=True, tile_position=(32 * c, 0))
                return ins

            def overflow(k, E, l, s):
                pe.wait_ge(S["ov_sel"], k + 1)
                pe.wait_ge(S["y_copied"], E + (l + 2))
                gather(o_sel, o_S).then_inc(S["ov_b"], 1)
                pe.wait_ge(S["ov_x"], k + 1)
                gate_up(o_xs, s).then_inc(S["ov_gu"], 1)
                pe.wait_ge(S["ov_h"], k + 1)
                nc.tensor.transpose(HT_ps, o_h, ident[:, :]).then_inc(S["ov_ht"], 1)
                pe.wait_ge(S["ov_htc"], k + 1)
                down(o_hT, s).then_inc(S["ov_dn"], 1)
                pe.wait_ge(S["ov_yc"], k + 1)
                combine(o_G4, o_y).then_inc(S["ov_done"], 1)

            def moe(l):
                route(l)
                pe.wait_ge(S["pg_done"], l + 1)
                pe.wait_ge(S["table_done"], l + 1)
                prep(0, l, 0)
                with pe.Fori(0, NE // 2) as i:
                    for s in range(2):
                        e = i * 2 + s
                        E = e + NE * l
                        pe.wait_ge((S["gu_in0"], S["gu_in1"])[s], i * 32 + (NE // 2 * l + 1) * 32)
                        pe.wait_ge(S["xs_done"], e + (NE + 1) * l + 1)
                        gate_up(xs[s], s).then_inc(S["gu_done"], 1)
                        prep(e + 1, l, 1 - s)
                        pe.wait_ge(S["y_copied"], E + (l + 1))
                        pe.wait_ge(S["h_done"], E + 1)
                        nc.tensor.transpose(HT_ps, hb, ident[:, :]).then_inc(S["ht_done"], 1)
                        combine(G4[1 - s], ysb[1 - s]).then_inc(S["comb_done"], 1)
                        pe.wait_ge((S["dn_in0"], S["dn_in1"])[s], i * 16 + (NE // 2 * l + 1) * 16)
                        pe.wait_ge(S["ht_copied"], E + 1)
                        down(hT, s).then_inc(S["dn_done"], 1)
                        k0 = pe.value_load(table[0:1, ds(e + (NE + 1) * l, 1)], min_val=0, max_val=2 * NE)
                        k1 = pe.value_load(table[0:1, ds(e + ((NE + 1) * l + 1), 1)], min_val=0, max_val=2 * NE)
                        with pe.If(k0 < k1):
                            with pe.Fori(k0, k1) as k:
                                overflow(k, E, l, s)
                pe.wait_ge(S["y_copied"], (NE + 1) * (l + 1))
                combine(G4[1], ysb[1]).then_inc(S["comb_done"], 1)

            moe(0)

            transposes(2)
            pe.wait_ge(S["par_head"], 4 * 16)
            for t in range(TT):
                for k in range(KC):
                    ins = mm(pa[:, HEADS * t:HEADS * t + HEADS], hnT[:, k, P * t:P * t + P], wdt[:, k, :],
                             start=(k == 0), stop=(k == KC - 1))
            ins.then_inc(S["dt_raw"], 1)
            pe.wait_ge(S["h_next"], 2)
            zero_acc()
            pe.wait_ge(S["dt_a"], 1)
            for t in range(TT):
                mm(pb[:, HEADS * t:HEADS * t + HEADS], upper[:, :], dta[:, t, :], start=True, stop=True)
                mm(wa[0:HEADS, P * t:P * t + P], dta[:, t, :], upper[:, :], start=True, stop=True)
            mm(pb[:, 64:96], ones[:, :], dta[:, 0, :], start=True, stop=True).then_inc(S["cum_done"], 1)

            def odd_c0(g):
                pe.wait_ge(S["c0_in"], g * 16 + 16 * (EVEN_UNITS + 1))
                if not isinstance(g, int) or g:
                    pe.wait_ge(S["bc_silu"], g)
                project(pa[:, 0:SEQ], w_c[0], 0)
                project(pa[:, SEQ:], w_c[0], 1).then_inc(S["z1_done"], 1)

            def odd_c1(g):
                pe.wait_ge(S["c1_in"], g * 16 + 16 * (EVEN_UNITS + 1))
                if not isinstance(g, int) or g:
                    pe.wait_ge(S["x1_silu"], g)
                else:
                    pe.wait_ge(S["cum_used"], 1)
                project(pb[:, 0:SEQ], w_c[1], 0)
                project(pb[:, SEQ:], w_c[1], 1).then_inc(S["x1_done"], 1)

            def odd_b(g):
                pe.wait_ge(S["c2_in"], g * 16 + 16 * (EVEN_UNITS + 1))
                pe.wait_ge(S["z1_silu"], g + 1)
                project(pa[:, 0:SEQ], w_c[2], 0)

            def odd_c(g):
                project(pa[:, SEQ:], w_c[2], 1).then_inc(S["bc_done"], 1)

            def odd_rows(g):
                pe.wait_ge(S["gsel_done"], g + 1)
                if not isinstance(g, int) or g:
                    pe.wait_ge(S["mix1_done"], g)
                for b, w in enumerate((wa, wb)):
                    ins = mm(w[:, :], gsel, csx[:, b, :, :].rearrange("p r l -> p (r l)"), start=True, stop=True)
                ins.then_inc(S["csrow_done"], 1)

            def odd_scores(g, p):
                pe.wait_ge(S["bc_silu"], g + 1)
                pe.wait_ge(S["x1_silu"], g + 1)
                pe.wait_ge(S["decay_done"], g + 1)
                bt, ct = bcT[p][:, 0, :], bcT[p][:, 1, :]
                mm(wa[:, 0:SEQ], bt[:, 0:P], ct, start=True, stop=True)
                mm(wa[:, SEQ:384], bt[:, P:], ct[:, P:], start=True, stop=True).then_inc(S["cb_done"], 1)
                for t in range(TT):
                    for j in range(2):
                        ins = nc.tensor.transpose(wb[:, 256 * t + P * j:256 * t + P * j + P],
                                                  xT[p][:, j, P * t:P * t + P], ident[:, :])
                ins.then_inc(S["xst_done"], 1)

            def odd_y(g):
                pe.wait_ge(S["xdt_done"], g + 1)
                for r in range(HPG):
                    o = wa[HD * (r % 2):HD * (r % 2) + HD, 256 * (r // 2):256 * (r // 2) + 256]
                    c = slice(HD * r, HD * r + HD)
                    mm(o[:, 0:P], xdt[:, 0, c], decay[:, 0, r, :], start=True, stop=True)
                    mm(o[:, P:], xdt[:, 1, c], decay[:, 1, r, :], start=True, stop=False)
                    ins = mm(o[:, P:], xw[:, c], decay[:, 2, r, :], start=False, stop=True)
                ins.then_inc(S["y_done"], 1)

            def odd_ss(g):
                pe.wait_ge(S["yz_done"], g + 1)
                for j in range(2):
                    ins = mm(wb[:, 0:SEQ], ones[:, :], sq[:, j, :], start=(j == 0), stop=(j == 1))
                ins.then_inc(S["yss_done"], 1)

            def odd_out(g, p):
                pe.wait_ge(S["mix1_done"], g + 1)
                out_project(mix1[p], g + EVEN_UNITS)

            pe.wait_ge(S["dt_pre"], 1)
            odd_c0(0)
            odd_c1(0)
            odd_b(0)
            odd_c(0)
            pe.wait_ge(S["csx_done"], 1)

            def odd_unit(g, p, more):
                odd_rows(g)
                if more:
                    odd_c0(g + 1)
                odd_scores(g, p)
                if more:
                    odd_c1(g + 1)
                odd_y(g)
                if more:
                    odd_b(g + 1)
                odd_ss(g)
                if more:
                    odd_c(g + 1)
                odd_out(g, p)

            with pe.Fori(0, (ODD_UNITS - 2) // 2) as i:
                for p in range(2):
                    odd_unit(i * 2 + p, p, True)
            odd_unit(ODD_UNITS - 2, 0, True)
            odd_unit(ODD_UNITS - 1, 1, False)

            moe(1)


_INS = ['x', 'even_w_in', 'even_conv_w', 'even_w_out', 'odd_in_proj', 'odd_conv_w', 'odd_conv_b',
        'odd_dt_bias', 'odd_a_log', 'odd_d_skip', 'odd_norm_w', 'odd_out_proj', 'norm_mix', 'norm_ffn',
        'router_g_w', 'router_g_b', 'router_e_w', 'router_e_b', 'expert_w_gate', 'expert_w_up',
        'expert_w_down', 'final_norm']


def kernel(**inputs):
    import numpy as _np
    import concourse.bacc as _bacc
    from concourse import mybir as _mybir
    from concourse.bass_utils import run_bass_kernel_spmd as _run

    nc = _bacc.Bacc("TRN2", target_bir_lowering=False, num_devices=1)
    arrays, args = {}, []
    for name in _INS:
        a = _np.ascontiguousarray(inputs[name])
        arrays[f"in_{name}"] = a
        args.append(nc.dram_tensor(f"in_{name}", a.shape, _mybir.dt.from_np(a.dtype), kind="ExternalInput").ap())
    args.append(nc.dram_tensor("out_0", (1, SEQ, D), _mybir.dt.from_np(_np.dtype("float32")),
                               kind="ExternalOutput").ap())
    trunk_program(nc, *args)
    r = _run(nc, [arrays], core_ids=[0])
    return r.results[0]["out_0"]
```

```python
from contextlib import ExitStack, contextmanager

import concourse.bass as bass
from concourse import mybir

F32 = mybir.dt.float32
BF16 = mybir.dt.bfloat16
I32 = mybir.dt.int32
ALU = mybir.AluOpType
ACT = mybir.ActivationFunctionType
AX = mybir.AxisListType.X

P = 128
D = 1024
KC = D // P
TT = 2
SEQ = TT * P
EVEN_UNITS = 4
ODD_UNITS = 8
HPG = 4
HD = 64
HEADS = 32
XB0, BB0, CB0 = 2048, 4096, 5120
DT0 = 6144
NE = 32
NG = 4
EPG = 8
FF = 512
QUAD = 4
CAP = 32
MAXB = SEQ // CAP
EPS = 1e-6
BIG = 1.0e30
ds = bass.ds


class Chain:

    def __init__(self, eng, sem, base=0):
        self.eng, self.sem, self.base, self.n = eng, sem, base, 0

    def link(self, ins):
        ins.then_inc(self.sem, 1)
        self.n += 1
        self.eng.wait_ge(self.sem, self.base + self.n)

    @contextmanager
    def loop(self, start, end, per):
        first = self.base + self.n
        with self.eng.Fori(start, end) as i:
            self.base, self.n = (i - start) * per + first, 0
            yield i
            assert self.n == per, (self.n, per)
        self.base, self.n = first + (end - start) * per, 0


SEMS = """
x_in par_vec par_conv par_head par_row par_wr fnorm_in out_stored
consts_pool consts_dve
c0_in c1_in c2_in wo_in
gu_in0 gu_in1 dn_in0 dn_in1
dve_chain act_chain pool_chain ovf_chain
conv_raw_t conv_cols
sum_sq mean_sq rstd_guess hs_dve hs_act hs_t hnt_dve hnt_act h_next zeroed
mix_acc
gc_hid hid_copied ch_done gb_q gb_copied q_copied k_v kv_copied conv_done
z_done z_copied z_log sp_done r_done att_in att_exp att_done av_done av_copied oproj
dt_raw dt_pre dt_exp dt_ln dt_a cum_done cum_used csx_done alog_exp
z1_done z1_exp z1_silu x1_done x1_tap x1_conv x1_exp x1_silu bc_done bc_tap bc_conv bc_exp bc_silu
gsel_done csrow_done seg_done decay_done cb_done decay_used xst_done xdt_done y_done yz_done yss_done yms_done yguess mix1_done
logits route_d route_e mask_done ranks table_done pos_t pg_done
prep_sel quad_sel b_done g4_done gath_done xs_done gu_done gexp h_done ht_done ht_copied dn_done y_copied comb_done
ov_sel ov_b ov_x ov_gu ov_exp ov_h ov_ht ov_htc ov_dn ov_yc ov_done
""".split()


def trunk_program(nc, x, even_w_in, even_conv_w, even_w_out, odd_in_proj, odd_conv_w, odd_conv_b,
                  odd_dt_bias, odd_a_log, odd_d_skip, odd_norm_w, odd_out_proj, norm_mix, norm_ffn,
                  router_g_w, router_g_b, router_e_w, router_e_b, expert_w_gate, expert_w_up,
                  expert_w_down, final_norm, out):
    with ExitStack() as ctx:
        def sb(name, shape, dt=F32):
            return ctx.enter_context(nc.sbuf_tensor(name, shape, dt))

        def ps(name, shape):
            return ctx.enter_context(nc.psum_tensor(name, shape, F32))

        S = {n: ctx.enter_context(nc.semaphore(n)) for n in SEMS}

        h = sb("h", [P, TT, D])
        hs = sb("hs", [P, TT, KC, P])
        hnT = sb("hnT", [P, KC, SEQ])
        w_gu = [sb(f"w_gu{s}", [P, 2, KC, FF]) for s in range(2)]
        w_dn = [sb(f"w_dn{s}", [P, FF // P, D]) for s in range(2)]
        w_c = [sb(f"w_c{j}", [P, KC, 2, P]) for j in range(3)]
        w_o = sb("w_o", [P, 2, D])

        ident = sb("ident", [P, P])
        upper = sb("upper", [P, P])
        lower = sb("lower", [P, P])
        strict = sb("strict", [P, P])
        ones = sb("ones", [P, P])
        zero_bf = sb("zero_bf", [P, 512], BF16)
        iota = sb("iota", [P, NE])
        slot_id = sb("slot_id", [P, 1])
        descend = sb("descend", [P, NE])
        one_c = sb("one_c", [P, 1])
        group_of = sb("group_of", [HEADS, ODD_UNITS])
        rank_of = sb("rank_of", [HEADS, HPG])
        turned = sb("turned", [NE, NE // QUAD, 2 * QUAD - 1])
        nmix = sb("nmix", [P, 2, KC])
        nffn = sb("nffn", [P, 2, KC])
        conv_raw = sb("conv_raw", [P, P])
        vec_raw = sb("vec_raw", [60, P])
        conv_cols = sb("conv_cols_sb", [P, P])
        vec_cols = sb("vec_cols", [P, 60])
        skip_row = sb("skip_row", [P, HEADS])
        dskip = sb("dskip", [P, 16])
        wr = sb("wr", [P, 2, KC, NG + NE])
        rbias = sb("rbias", [P, 2, NG + NE])
        dtb = sb("dtb", [P, HEADS])
        alog = sb("alog", [P, HEADS])
        wdt = sb("wdt", [P, KC, HEADS])
        st = sb("st", [P, 8, TT])
        table = sb("table", [1, 2 * (NE + 1)], I32)

        ARENA = 11520
        arena = sb("arena", [P, ARENA])

        def carve():
            at = [0]

            def take(*shape, rows=P):
                n = 1
                for k in shape:
                    n *= k
                v = arena[0:rows, at[0]:at[0] + n]
                at[0] += n
                assert at[0] <= ARENA, at[0]
                if len(shape) == 2:
                    v = v.rearrange("p (a b) -> p a b", a=shape[0])
                if len(shape) == 3:
                    v = v.rearrange("p (a b c) -> p a b c", a=shape[0], b=shape[1])
                return v
            return take

        take = carve()
        qS = [take(SEQ) for _ in range(2)]
        kS = [take(SEQ) for _ in range(2)]
        vS = [take(TT, P) for _ in range(2)]
        hidS, gbS, ch = take(SEQ), take(SEQ), take(SEQ + 2)
        cacc = take(SEQ)
        zS, lS, sp, att = take(2, 384), take(2, 384), take(2, 384), take(2, 384)
        mix = [take(2, SEQ) for _ in range(2)]
        take = carve()
        mix1 = [take(2, SEQ) for _ in range(2)]
        ez = take(2, SEQ)
        sz = [take(2, SEQ) for _ in range(2)]
        xT = [take(2, SEQ) for _ in range(2)]
        bcT = [take(2, SEQ) for _ in range(2)]
        cv, ecv = take(2, SEQ), take(2, SEQ)
        csx = take(2, HPG, P, rows=HEADS)
        gsel = take(P, rows=HEADS)
        decay = take(3, HPG, P)
        cbs = take(384)
        xdt, xw = take(TT, 256), take(256)
        yz, sq = take(2, SEQ), take(2, SEQ)
        ms, rg, rt = take(SEQ), take(SEQ), take(SEQ)
        dtv, dta, csn = (take(TT, HEADS) for _ in range(3))
        w0, dtw = take(HEADS), take(HEADS)
        take = carve()
        pos = take(TT, NE + QUAD)
        gates = take(TT, NE)
        mask = take(TT, NE)
        lg = take(TT, NG + NE)
        rt1, rt2, oh1, oh2 = (take(TT, NE) for _ in range(4))
        m8 = take(8, TT)
        dd, ee = take(TT, 8), take(TT, 8)
        cnt = take(2 * NE + 8)
        PG = take(2 * SEQ, rows=NE)
        sel = take(P, rows=NE)
        quad_slots = take(TT, QUAD * CAP)
        G4 = [take(SEQ) for _ in range(QUAD)]
        xs = take(KC, QUAD * CAP)
        eg, hb, hT = take(P), take(P), take(P)
        yq = take(QUAD, 256)
        o_sel = take(P, rows=NE)
        o_S, o_G4, o_xs = take(TT, CAP), take(SEQ), take(KC, CAP)
        o_eg, o_h, o_hT, o_y = take(P), take(P), take(P), take(256)
        o_iota, o_slot = take(NE), take(1)
        junk = arena[:, ARENA - D:ARENA]
        fnorm = hnT[:, 0:4, :].rearrange("p a b -> p (a b)")
        y_out = w_c[0][:, :, :, :].rearrange("p k a b -> p (k a b)").rearrange("p (t d) -> p t d", t=TT)

        acc = ps("acc", [P, 4, 512])
        pa, pb, wa, wb = (ps(n, [P, 512]) for n in ("pa", "pb", "wa", "wb"))
        BANKS = [pa, pb, wa, wb]
        pa2, pb2 = (b[:, :].rearrange("p (a b) -> p a b", a=2) for b in (pa, pb))
        B_ps = pa
        XG = pb[:, :].rearrange("p (k s) -> p k s", k=KC // 2)
        o_XG = pb[:, 0:256].rearrange("p (k s) -> p k s", k=KC)
        Y_ps = wb[:, 256:512]
        GU = [wa[:, 256 * s:256 * s + 256].rearrange("p (g n) -> p g n", g=2) for s in range(2)]
        HT_ps = wb[:, 0:P]

        w_in_e = even_w_in[0].rearrange("(p k) (b m) -> p k b m", k=KC, b=6)
        w_in_o = odd_in_proj[0].rearrange("(p k) n -> p k n", k=KC)
        w_out_e = even_w_out[0].rearrange("(a c) n -> c a n", a=2)
        w_out_o = odd_out_proj[0].rearrange("(a c) n -> c a n", c=P)
        h_d = x[0].rearrange("(t p) d -> p t d", p=P)
        out_d = out[0].rearrange("(t p) d -> p t d", p=P)

        block = ctx.enter_context(nc.Block())

        @block.sync
        def _(sp_):
            def chunk_even(u, c):
                blocks = (slice(1, 3), slice(0, 4, 3), slice(4, 6))[c]
                if u:
                    sp_.wait_ge((S["gc_hid"], S["gb_q"], S["k_v"])[c], u)
                sp_.dma_start(w_c[c][:, :, :, :], w_in_e[:, :, blocks, P * u:P * u + P]
                              ).then_inc((S["c0_in"], S["c1_in"], S["c2_in"])[c], 16)

            def rows_even(u):
                if u:
                    sp_.wait_ge(S["oproj"], u)
                a = w_out_e[P * u:P * u + P]
                sp_.dma_start(w_o[:, :, :], a).then_inc(S["wo_in"], 16)

            def chunks_odd(g, first=False):
                sp_.wait_ge(S["gc_hid"], EVEN_UNITS) if first else sp_.wait_ge(S["z1_done"], g)
                sp_.dma_start(w_c[0][:, :, :, :].rearrange("p k a b -> p k (a b)"),
                              w_in_o[:, :, ds(g * 256, 256)]).then_inc(S["c0_in"], 16)
                sp_.wait_ge(S["gb_q"], EVEN_UNITS) if first else sp_.wait_ge(S["x1_done"], g)
                sp_.dma_start(w_c[1][:, :, :, :].rearrange("p k a b -> p k (a b)"),
                              w_in_o[:, :, ds(g * 256 + XB0, 256)]).then_inc(S["c1_in"], 16)
                sp_.wait_ge(S["k_v"], EVEN_UNITS) if first else sp_.wait_ge(S["bc_done"], g)
                bc = w_in_o[:, :, BB0:DT0].rearrange("p k (a n) -> p k a n", a=2)
                sp_.dma_start(w_c[2][:, :, :, :], bc[:, :, :, ds(g * P, P)]).then_inc(S["c2_in"], 16)

            def rows_odd(g):
                sp_.wait_ge(S["oproj"], g + EVEN_UNITS)
                sp_.dma_start(w_o[:, :, :], w_out_o[:, ds(g * 2, 2), :]).then_inc(S["wo_in"], 16)

            def slot_free(l, e):
                sp_.wait_ge(S["dn_done"], e + (NE * l - 1))
                n = sp_.value_load(table[0:1, ds(e + ((NE + 1) * l - 1), 1)], min_val=0, max_val=2 * NE)
                sp_.wait_ge(S["ov_done"], n + 1)

            def expert_part(l, e, s, part):
                gu, dn = (S["gu_in0"], S["gu_in1"])[s], (S["dn_in0"], S["dn_in1"])[s]
                w = (expert_w_gate, expert_w_up, expert_w_down)[part][l, ds(e, 1), :, :]
                if part < 2:
                    sp_.dma_start(w_gu[s][:, part], w.rearrange("a (p k) f -> p (a k) f", k=KC)).then_inc(gu, 16)
                else:
                    sp_.dma_start(w_dn[s][:, :, :], w.rearrange("a (j p) n -> p (a j) n", p=P)).then_inc(dn, 16)

            def expert_stream(l):
                with sp_.Fori(1, NE // 2) as i:
                    for s in range(2):
                        slot_free(l, i * 2 + s)
                        for part in range(3):
                            expert_part(l, i * 2 + s, s, part)

            sp_.dma_start(h[:, :, :], h_d).then_inc(S["x_in"], 16)
            for c in range(3):
                chunk_even(0, c)
            rows_even(0)
            for c in range(3):
                chunk_even(1, c)
            for u in range(2, EVEN_UNITS):
                for c in range(3):
                    expert_part(0, u - 2, u - 2, c)
                    chunk_even(u, c)
                rows_even(u - 1)
            rows_even(EVEN_UNITS - 1)
            chunks_odd(0, first=True)
            rows_odd(0)
            sp_.wait_ge(S["table_done"], 1)
            expert_stream(0)
            for s in range(2):
                sp_.wait_ge(S["dn_done"], NE - 1 + s)
                n = sp_.value_load(table[0:1, NE - 1 + s:NE + s], min_val=0, max_val=2 * NE)
                sp_.wait_ge(S["ov_done"], n + 1)
                for part in range(3):
                    expert_part(1, s, s, part)
            chunks_odd(1)
            with sp_.Fori(1, ODD_UNITS - 1) as g:
                chunks_odd(g + 1)
                rows_odd(g)
            rows_odd(ODD_UNITS - 1)
            sp_.wait_ge(S["table_done"], 2)
            expert_stream(1)
            sp_.wait_ge(S["h_next"], 5)
            sp_.dma_start(out_d, y_out).then_inc(S["out_stored"], 16)
            sp_.wait_ge(S["out_stored"], 16)

        @block.gpsimd
        def _(pool):
            chain = Chain(pool, S["pool_chain"])
            nc.gpsimd.memset(ones[:, :], 1.0)
            nc.gpsimd.memset(one_c[:, :], 1.0)
            nc.gpsimd.memset(ident[:, :], 0.0)
            nc.gpsimd.memset(zero_bf[:, :], 0.0)
            nc.gpsimd.memset(group_of[:, :], 1.0)
            nc.gpsimd.iota(iota[:, :], pattern=[[1, NE]], base=0, channel_multiplier=0,
                           allow_small_or_imprecise_dtypes=True)
            nc.gpsimd.iota(descend[:, :], pattern=[[-1, NE]], base=NE, channel_multiplier=0,
                           allow_small_or_imprecise_dtypes=True)
            for q in range(4):
                chain.link(nc.gpsimd.iota(slot_id[32 * q:32 * q + 32, :], pattern=[[0, 1]], base=0,
                                          channel_multiplier=1, allow_small_or_imprecise_dtypes=True))
            nc.gpsimd.affine_select(out=ident[:, :], in_=ident[:, :], compare_op=ALU.not_equal, fill=1.0,
                                    base=0, pattern=[[-1, P]], channel_multiplier=1)
            nc.gpsimd.affine_select(out=upper[:, :], in_=ones[:, :], compare_op=ALU.is_ge, fill=0.0,
                                    base=0, pattern=[[1, P]], channel_multiplier=-1)
            nc.gpsimd.affine_select(out=lower[:, :], in_=ones[:, :], compare_op=ALU.is_ge, fill=0.0,
                                    base=0, pattern=[[-1, P]], channel_multiplier=1)
            nc.gpsimd.affine_select(out=strict[:, :], in_=ones[:, :], compare_op=ALU.is_gt, fill=0.0,
                                    base=0, pattern=[[1, P]], channel_multiplier=-1)
            chain.link(nc.gpsimd.affine_select(out=group_of[:, :], in_=group_of[:, :], compare_op=ALU.is_ge,
                                               fill=0.0, base=0, pattern=[[-HPG, ODD_UNITS]],
                                               channel_multiplier=1))
            nc.gpsimd.affine_select(out=group_of[:, :], in_=group_of[:, :], compare_op=ALU.is_ge, fill=0.0,
                                    base=HPG - 1, pattern=[[HPG, ODD_UNITS]],
                                    channel_multiplier=-1).then_inc(S["consts_pool"], 1)

        @block.scalar
        def _(act):
            chain = Chain(act, S["act_chain"])

            def af(*a, **k):
                return nc.scalar.activation(*a, **k)

            act.dma_start(nmix[:, :, :], norm_mix.rearrange("l (p k) -> p l k", k=KC)).then_inc(S["par_vec"], 16)
            act.dma_start(conv_raw[:, :], odd_conv_w[0].rearrange("k (t c) -> (k t) c", c=P)).then_inc(S["par_conv"], 16)
            act.dma_start(vec_raw[0:32, :], odd_conv_b[0].rearrange("(t c) -> t c", c=P)).then_inc(S["par_conv"], 16)
            act.dma_start(vec_raw[32:48, :], odd_norm_w[0].rearrange("(t c) -> t c", c=P)).then_inc(S["par_conv"], 16)
            act.dma_start(vec_raw[48:60, :], even_conv_w[0].rearrange("k (t c) -> (k t) c", c=P)).then_inc(S["par_conv"], 16)

            def late_params():
                act.dma_start(nffn[:, :, :], norm_ffn.rearrange("l (p k) -> p l k", k=KC)).then_inc(S["par_wr"], 16)
                for l in range(2):
                    act.dma_start(wr[:, l, :, 0:NG],
                                  router_g_w[l].rearrange("(p k) g -> p k g", k=KC)).then_inc(S["par_wr"], 16)
                    for g in range(NG):
                        act.dma_start(wr[:, l, :, NG + EPG * g:NG + EPG * g + EPG],
                                      router_e_w[l, g].rearrange("(p k) e -> p k e", k=KC)).then_inc(S["par_wr"], 16)
                    act.dma_start(rbias[:, l, 0:NG], router_g_b[l].partition_broadcast(P)).then_inc(S["par_wr"], 16)
                    act.dma_start(rbias[:, l, NG:], router_e_b[l].rearrange("g e -> (g e)").partition_broadcast(P)
                                  ).then_inc(S["par_wr"], 16)
                act.dma_start(dtb[:, :], odd_dt_bias[0].partition_broadcast(P)).then_inc(S["par_head"], 16)
                act.dma_start(alog[:, :], odd_a_log[0].partition_broadcast(P)).then_inc(S["par_head"], 16)
                act.dma_start(wdt[:, :, :], w_in_o[:, :, DT0:DT0 + HEADS]).then_inc(S["par_head"], 16)
                act.dma_start(skip_row[:, :], odd_d_skip[0].partition_broadcast(P)).then_inc(S["par_head"], 16)

            def norm(n, wcol):
                if n == 0:
                    act.wait_ge(S["x_in"], 16)
                else:
                    act.wait_ge(S["h_next"], n)
                for t in range(TT):
                    ins = af(junk[:, :], h[:, t, :], ACT.Square, accum_out=st[:, 0, t:t + 1])
                    if t == 0:
                        chain.link(ins)
                ins.then_inc(S["sum_sq"], 1)
                act.wait_ge(S["mean_sq"], n + 1)
                chain.link(af(st[:, 2, :], st[:, 1, :], ACT.Ln))
                af(st[:, 3, :], st[:, 2, :], ACT.Exp, scale=-0.5).then_inc(S["rstd_guess"], 1)
                if wcol is None:
                    return
                act.wait_ge(S["hs_dve"], 2 * n + 1)
                af(hs[:, 1, :, :], h[:, 1, :].rearrange("p (q k) -> p k q", k=KC), ACT.Identity,
                   scale=st[:, 4, 1:2]).then_inc(S["hs_act"], 1)
                for b in (2, 3):
                    act.wait_ge(S["hs_t"], 4 * n + b + 1)
                    for j in range(2):
                        k = 2 * b + j
                        af(hnT[:, k, :], BANKS[b][:, 256 * j:256 * j + 256], ACT.Identity,
                           scale=wcol[:, k:k + 1]).then_inc(S["hnt_act"], 1)

            def even_c0(u):
                act.wait_ge(S["gc_hid"], u + 1)
                if u:
                    act.wait_ge(S["ch_done"], u)
                af(hidS, pa[:, SEQ:2 * SEQ], ACT.Copy).then_inc(S["hid_copied"], 1)

            def even_c1(u):
                act.wait_ge(S["gb_q"], u + 1)
                if u:
                    act.wait_ge(S["conv_done"], u)
                af(gbS, pb[:, 0:SEQ], ACT.Copy).then_inc(S["gb_copied"], 1)
                af(qS[u % 2], pb[:, SEQ:2 * SEQ], ACT.Copy, scale=HD ** -0.5).then_inc(S["q_copied"], 1)

            def even_c2(u):
                act.wait_ge(S["k_v"], u + 1)
                af(kS[u % 2], pa[:, 0:SEQ], ACT.Copy).then_inc(S["kv_copied"], 1)
                af(vS[u % 2], pa2[:, 1, :].rearrange("p (t d) -> p t d", t=TT), ACT.Copy).then_inc(S["kv_copied"], 1)

            def even_attention_scores(u):
                for hh, w in enumerate((wa, wb)):
                    act.wait_ge(S["z_done"], 2 * u + hh + 1)
                    ins = af(zS[:, hh, :], w[:, 0:384], ACT.Copy)
                    ins.then_inc(S["z_copied"], 1)
                act.wait_ge(S["z_copied"], 2 * u + 2)
                chain.link(af(lS, zS, ACT.Abs))
                chain.link(af(lS, lS, ACT.Exp, scale=-1.0))
                af(lS, lS, ACT.Ln, bias=one_c[:, :]).then_inc(S["z_log"], 1)

            def even_attention_weights(u):
                act.wait_ge(S["att_in"], u + 1)
                af(att, att, ACT.Exp).then_inc(S["att_exp"], 1)

            def even_attention_out(u):
                act.wait_ge(S["av_done"], u + 1)
                af(mix[u % 2][:, 1, :], wa[:, 0:SEQ], ACT.Copy).then_inc(S["av_copied"], 1)

            act.wait_ge(S["par_vec"], 16)
            norm(0, nmix[:, 0, :])
            late_params()
            even_c0(0)
            even_c1(0)
            even_c2(0)
            for u in range(EVEN_UNITS):
                more = u + 1 < EVEN_UNITS
                even_attention_scores(u)
                if more:
                    even_c0(u + 1)
                even_attention_weights(u)
                if more:
                    even_c1(u + 1)
                even_attention_out(u)
                if more:
                    even_c2(u + 1)

            def expert_block(q, l, E, j):
                s = j % 2
                act.wait_ge(S["gu_done"], E + 1)
                af(eg, GU[s][:, 0, :], ACT.Exp, scale=-1.0).then_inc(S["gexp"], 1)
                act.wait_ge(S["ht_done"], E + 1)
                af(hT, HT_ps, ACT.Copy).then_inc(S["ht_copied"], 1)
                act.wait_ge(S["dn_done"], E + 1)
                if j == 0:
                    act.wait_ge(S["comb_done"], q + (NE // QUAD * l + 1))
                for c in range(4):
                    r = slice(32 * c, 32 * c + 32)
                    ins = af(yq[r, (c + j) % 4, :], Y_ps[r, :], ACT.Copy)
                ins.then_inc(S["y_copied"], 1)

            def overflow(k, s):
                act.wait_ge(S["ov_gu"], k + 1)
                af(o_eg, GU[s][:, 0, :], ACT.Exp, scale=-1.0).then_inc(S["ov_exp"], 1)
                act.wait_ge(S["ov_ht"], k + 1)
                af(o_hT, HT_ps, ACT.Copy).then_inc(S["ov_htc"], 1)
                act.wait_ge(S["ov_dn"], k + 1)
                af(o_y, Y_ps, ACT.Copy).then_inc(S["ov_yc"], 1)

            def moe(l):
                if l == 0:
                    act.wait_ge(S["par_wr"], 15 * 16)
                norm(2 * l + 1, nffn[:, l, :])
                act.wait_ge(S["route_d"], l + 1)
                if l:
                    act.dma_start(fnorm, final_norm.partition_broadcast(P)).then_inc(S["fnorm_in"], 16)
                af(ee[:, :, 0:5], dd[:, :, 0:5], ACT.Exp).then_inc(S["route_e"], 1)
                act.wait_ge(S["pos_t"], l + 1)
                af(PG, wa[0:NE, :], ACT.Copy).then_inc(S["pg_done"], 1)
                act.wait_ge(S["table_done"], l + 1)
                with act.Fori(0, NE // QUAD) as q:
                    for j in range(QUAD):
                        s = j % 2
                        e = q * QUAD + j
                        expert_block(q, l, e + NE * l, j)
                        k0 = act.value_load(table[0:1, ds(e + (NE + 1) * l, 1)], min_val=0, max_val=2 * NE)
                        k1 = act.value_load(table[0:1, ds(e + ((NE + 1) * l + 1), 1)], min_val=0, max_val=2 * NE)
                        with act.If(k0 < k1):
                            with act.Fori(k0, k1) as k:
                                overflow(k, s)

            moe(0)

            def sigmoid(e):
                chain.link(af(e, e, ACT.Ln, bias=one_c[:, :]))
                return af(e, e, ACT.Exp, scale=-1.0)

            def odd_z(g):
                act.wait_ge(S["z1_done"], g + 1)
                chain.link(af(ez, pa2, ACT.Exp, scale=-1.0))
                sigmoid(ez).then_inc(S["z1_exp"], 1)

            def first_tap(src, tiles):
                for j, tile in enumerate(tiles):
                    ins = af(cv[:, j, :], src[:, j, :], ACT.Identity, scale=conv_cols[:, ds(tile + 3 * 32, 1)],
                             bias=vec_cols[:, ds(tile, 1)])
                return ins

            def odd_x(g):
                act.wait_ge(S["x1_done"], g + 1)
                if not isinstance(g, int) or g:
                    act.wait_ge(S["bc_silu"], g)
                first_tap(pb2, [g * 2, g * 2 + 1]).then_inc(S["x1_tap"], 1)
                act.wait_ge(S["x1_conv"], g + 1)
                chain.link(af(ecv, cv, ACT.Exp, scale=-1.0))
                sigmoid(ecv).then_inc(S["x1_exp"], 1)

            def odd_bc(g):
                act.wait_ge(S["bc_done"], g + 1)
                act.wait_ge(S["x1_silu"], g + 1)
                first_tap(pa2, [g + 16, g + 24]).then_inc(S["bc_tap"], 1)
                act.wait_ge(S["bc_conv"], g + 1)
                chain.link(af(ecv, cv, ACT.Exp, scale=-1.0))
                sigmoid(ecv).then_inc(S["bc_exp"], 1)

            def odd_decay(g):
                act.wait_ge(S["seg_done"], g + 1)
                af(decay[:, 0:2, :, :], decay[:, 0:2, :, :], ACT.Exp)
                af(decay[:, 2, :, :], wb[:, :].rearrange("p (r l) -> p r l", r=HPG), ACT.Exp
                   ).then_inc(S["decay_done"], 1)

            def odd_rstd(g):
                act.wait_ge(S["yms_done"], g + 1)
                chain.link(af(rg, ms, ACT.Ln))
                af(rg, rg, ACT.Exp, scale=-0.5).then_inc(S["yguess"], 1)

            norm(2, nmix[:, 1, :])
            act.wait_ge(S["par_head"], 4 * 16)
            act.wait_ge(S["dt_pre"], 1)
            chain.link(af(dta, dtv, ACT.Abs))
            chain.link(af(dta, dta, ACT.Exp, scale=-1.0))
            af(dta, dta, ACT.Ln, bias=one_c[:, :]).then_inc(S["dt_ln"], 1)
            af(w0, alog[:, :], ACT.Exp).then_inc(S["alog_exp"], 1)
            act.wait_ge(S["cum_done"], 1)
            act.wait_ge(S["cum_used"], 1)
            af(w0, dtw, ACT.Exp).then_inc(S["alog_exp"], 1)
            odd_z(0)
            odd_x(0)
            odd_bc(0)

            def odd_unit(g, more):
                odd_decay(g)
                if more:
                    odd_z(g + 1)
                    odd_x(g + 1)
                odd_rstd(g)
                if more:
                    odd_bc(g + 1)

            with chain.loop(0, ODD_UNITS - 1, 7) as g:
                odd_unit(g, True)
            odd_unit(ODD_UNITS - 1, False)

            moe(1)
            norm(4, None)

        @block.vector
        def _(dve):
            chain = Chain(dve, S["dve_chain"])
            v = nc.vector
            link = chain.link

            def newton(r, x, tmp):
                link(v.tensor_tensor(tmp, r, r, ALU.mult))
                link(v.tensor_tensor(tmp, tmp, x, ALU.mult))
                link(v.tensor_scalar(tmp, tmp, -0.5, 1.5, ALU.mult, ALU.add))

            def norm(n, wcol):
                dve.wait_ge(S["sum_sq"], n + 1)
                v.tensor_scalar(st[:, 1, :], st[:, 0, :], 1.0 / D, EPS, ALU.mult, ALU.add).then_inc(S["mean_sq"], 1)
                dve.wait_ge(S["rstd_guess"], n + 1)
                newton(st[:, 3, :], st[:, 1, :], st[:, 5, :])
                v.tensor_tensor(st[:, 4, :], st[:, 3, :], st[:, 5, :], ALU.mult).then_inc(S["hs_dve"], 1)
                dve.wait_ge(S["hs_dve"], 2 * n + 1)
                if wcol is None:
                    return
                v.tensor_scalar(hs[:, 0, :, :], h[:, 0, :].rearrange("p (q k) -> p k q", k=KC),
                                st[:, 4, 0:1], None, ALU.mult).then_inc(S["hs_dve"], 1)
                for b in (0, 1):
                    dve.wait_ge(S["hs_t"], 4 * n + b + 1)
                    v.tensor_tensor(hnT[:, 2 * b:2 * b + 2, :], BANKS[b][:, :].rearrange("p (a b) -> p a b", a=2),
                                    wcol[:, 2 * b:2 * b + 2].unsqueeze(2).to_broadcast([P, 2, SEQ]),
                                    ALU.mult).then_inc(S["hnt_dve"], 1)

            def residual_mixer(l):
                dve.wait_ge(S["oproj"], (EVEN_UNITS, EVEN_UNITS + ODD_UNITS)[l])
                for t in range(TT):
                    for n in range(2):
                        ins = v.tensor_tensor(h[:, t, 512 * n:512 * n + 512], h[:, t, 512 * n:512 * n + 512],
                                              acc[:, 2 * t + n, :], ALU.add)
                        if t + n < 2:
                            link(ins)
                ins.then_inc(S["h_next"], 1)

            dve.wait_ge(S["consts_pool"], 1)
            v.tensor_reduce(out=rank_of[:, :], in_=ident[0:HEADS, 0:HEADS].rearrange("p (g r) -> p r g", r=HPG),
                            axis=AX, op=ALU.add).then_inc(S["consts_dve"], 1)
            for m in range(2 * QUAD - 1):
                v.tensor_copy(turned[:, :, m:m + 1], ident[0:NE, (QUAD - 1 - m) % QUAD:NE:QUAD].unsqueeze(2))
            v.memset(ch[:, 0:2], 0.0).then_inc(S["consts_dve"], 1)
            v.memset(table[:, 0:1], 0).then_inc(S["ov_done"], 1)
            v.memset(cnt[:, 0:1], 0.0).then_inc(S["comb_done"], 1)
            dve.wait_ge(S["conv_raw_t"], 1)
            v.tensor_copy(conv_cols[:, :], pa[:, 0:P]).then_inc(S["conv_cols"], 1)
            v.tensor_copy(vec_cols[:, :], pa[:, P:P + 60]).then_inc(S["conv_cols"], 1)
            dve.wait_ge(S["conv_cols"], 2)

            def even_ch(u):
                dve.wait_ge(S["hid_copied"], u + 1)
                v.tensor_tensor(ch[:, 2:], pa[:, 0:SEQ], hidS, ALU.mult).then_inc(S["ch_done"], 1)
                dve.wait_ge(S["ch_done"], u + 1)

            def even_conv(u):
                def tap(k):
                    return vec_cols[:, 48 + 4 * k + u:49 + 4 * k + u]
                link(v.tensor_scalar(cacc, ch[:, 2:], tap(2), None, ALU.mult))
                link(v.scalar_tensor_tensor(cacc, ch[:, 1:1 + SEQ], tap(1), cacc, ALU.mult, ALU.add))
                link(v.scalar_tensor_tensor(cacc, ch[:, 0:SEQ], tap(0), cacc, ALU.mult, ALU.add))
                dve.wait_ge(S["gb_copied"], u + 1)
                if u >= 2:
                    dve.wait_ge(S["oproj"], u - 1)
                v.tensor_tensor(mix[u % 2][:, 0, :], cacc, gbS, ALU.mult).then_inc(S["conv_done"], 1)

            def diag(a):
                return a.rearrange("p h (b l) -> p h b l", l=P)

            def even_softplus(u):
                dve.wait_ge(S["z_log"], u + 1)
                if u:
                    dve.wait_ge(S["r_done"], 2 * u)
                link(v.scalar_tensor_tensor(sp, zS, 0.0, lS, ALU.max, ALU.add))
                for hh in range(2):
                    d = diag(sp)[:, hh, 0:3:2, :]
                    ins = v.tensor_tensor(d, d, strict[:, :].unsqueeze(1).to_broadcast([P, 2, P]), ALU.mult)
                    ins.then_inc(S["sp_done"], 1)

            def even_weights_in(u):
                for hh, w in enumerate((wa, wb)):
                    dve.wait_ge(S["r_done"], 2 * u + hh + 1)
                    ins = v.tensor_tensor(att[:, hh, :], zS[:, hh, :], w[:, 0:384], ALU.subtract)
                link(ins)
                v.tensor_scalar(att, att, 0.0, None, ALU.min).then_inc(S["att_in"], 1)

            def even_weights_mask(u):
                dve.wait_ge(S["att_exp"], u + 1)
                for hh in range(2):
                    d = diag(att)[:, hh, 0:3:2, :]
                    v.tensor_tensor(d, d, strict[:, :].unsqueeze(1).to_broadcast([P, 2, P]), ALU.mult
                                    ).then_inc(S["att_done"], 1)

            dve.wait_ge(S["par_vec"], 16)
            norm(0, nmix[:, 0, :])
            even_ch(0)
            even_conv(0)
            for u in range(EVEN_UNITS):
                more = u + 1 < EVEN_UNITS
                even_softplus(u)
                if more:
                    even_ch(u + 1)
                even_weights_in(u)
                even_weights_mask(u)
                if more:
                    even_conv(u + 1)
            residual_mixer(0)

            def one_hot_first(dst, src, m, n, tmp):
                def col(a):
                    return a.unsqueeze(2).to_broadcast([P, TT, n])
                link(v.tensor_reduce(out=m, in_=src, axis=AX, op=ALU.max))
                link(v.tensor_tensor(tmp, src, col(m), ALU.is_equal))
                link(v.tensor_tensor(tmp, tmp, descend[:, 0:n].unsqueeze(1).to_broadcast([P, TT, n]), ALU.mult))
                link(v.tensor_reduce(out=m8[:, 7, :], in_=tmp, axis=AX, op=ALU.max))
                link(v.tensor_tensor(dst, tmp, col(m8[:, 7, :]), ALU.is_equal))

            def bc(a, n):
                return a.unsqueeze(2).to_broadcast([P, TT, n])

            def route(l):
                dve.wait_ge(S["logits"], l + 1)
                plog = pa[:, 0:P].rearrange("p (t n) -> p t n", t=TT)[:, :, 0:NG + NE]
                link(v.tensor_tensor(lg, plog, rbias[:, l, :].unsqueeze(1).to_broadcast([P, TT, NG + NE]), ALU.add))
                gmax, m1, m2, gs, s1, g1, g2 = (m8[:, j, :] for j in range(7))
                one_hot_first(rt2[:, :, 0:NG], lg[:, :, 0:NG], gmax, NG, rt1[:, :, 0:NG])
                link(v.tensor_tensor(dd[:, :, 0:NG], lg[:, :, 0:NG], bc(gmax, NG), ALU.subtract))
                link(v.tensor_scalar(rt2[:, :, 0:NG], rt2[:, :, 0:NG], BIG, -BIG, ALU.mult, ALU.add))
                for t in range(TT):
                    link(v.tensor_tensor(lg[:, t, NG:].rearrange("p (g e) -> p g e", g=NG),
                                         lg[:, t, NG:].rearrange("p (g e) -> p g e", g=NG),
                                         rt2[:, t, 0:NG].unsqueeze(2).to_broadcast([P, NG, EPG]), ALU.add))
                ex = lg[:, :, NG:]
                one_hot_first(oh1, ex, m1, NE, rt1)
                link(v.scalar_tensor_tensor(ex, oh1, -2.0 * BIG, ex, ALU.mult, ALU.add))
                one_hot_first(oh2, ex, m2, NE, rt1)
                v.tensor_tensor(dd[:, :, 4:5], m2.unsqueeze(2), m1.unsqueeze(2), ALU.subtract).then_inc(S["route_d"], 1)
                v.tensor_tensor(mask, oh1, oh2, ALU.add).then_inc(S["mask_done"], 1)
                dve.wait_ge(S["route_e"], l + 1)
                link(v.tensor_reduce(out=gs, in_=ee[:, :, 0:NG], axis=AX, op=ALU.add))
                link(v.tensor_scalar(s1, ee[:, :, 4:5].rearrange("p t o -> p (t o)"), 1.0, None, ALU.add))
                link(v.tensor_tensor(s1, s1, gs, ALU.mult))
                link(v.reciprocal(g1, s1))
                link(v.tensor_tensor(g2, g1, ee[:, :, 4:5].rearrange("p t o -> p (t o)"), ALU.mult))
                link(v.tensor_tensor(oh1, oh1, bc(g1, NE), ALU.mult))
                link(v.tensor_tensor(oh2, oh2, bc(g2, NE), ALU.mult))
                link(v.tensor_tensor(gates, oh1, oh2, ALU.add))
                dve.wait_ge(S["ranks"], l + 1)
                prk = pb[:, 0:2 * NE].rearrange("p (t n) -> p t n", t=TT)
                link(v.memset(pos[:, :, NE:], -1.0))
                link(v.tensor_tensor(pos[:, :, 0:NE], prk, mask, ALU.mult))
                v.tensor_scalar(pos[:, :, 0:NE], pos[:, :, 0:NE], -1.0, None, ALU.add).then_inc(S["mask_done"], 1)
                dve.wait_ge(S["mask_done"], 2 * l + 2)
                cs, ov = cnt[0:1, 0:NE], cnt[0:1, NE:2 * NE]
                link(v.tensor_copy(cs, pb[0:1, 2 * NE:3 * NE]))
                link(v.tensor_scalar(ov, cs, float(CAP), None, ALU.is_gt))
                for b in range(2, MAXB):
                    link(v.scalar_tensor_tensor(ov, cs, float(CAP * b), ov, ALU.is_gt, ALU.add))
                base = (NE + 1) * l
                if l:
                    link(v.tensor_copy(table[:, base:base + 1], table[:, base - 1:base]))
                link(v.tensor_copy(cnt[0:1, 2 * NE:2 * NE + 1], table[:, base:base + 1]))
                v.tensor_tensor_scan(table[:, base + 1:base + NE + 1], ones[0:1, 0:NE], ov,
                                     cnt[0:1, 2 * NE:2 * NE + 1], ALU.mult, ALU.add).then_inc(S["table_done"], 1)

            def select_rows(q, b):
                v.tensor_scalar(sel.rearrange("p (o c s) -> p o c s", o=1, c=QUAD),
                                turned[:, ds(q, 1), QUAD - 1 - b:2 * QUAD - 1 - b].unsqueeze(3).to_broadcast(
                                    [NE, 1, QUAD, CAP]), 1.0, None, ALU.mult).then_inc(S["prep_sel"], 1)

            def select_quad(q):
                v.tensor_tensor(quad_slots.rearrange("p t (e s) -> p t e s", e=QUAD),
                                iota[:, :].unsqueeze(1).unsqueeze(1).to_broadcast([P, TT, QUAD, CAP]),
                                pos[:, :, ds(q * QUAD, QUAD)].unsqueeze(3).to_broadcast([P, TT, QUAD, CAP]),
                                ALU.is_equal).then_inc(S["quad_sel"], 1)

            def gathered(q, l, half):
                dve.wait_ge(S["gath_done"], q * 2 + (2 * (NE // QUAD + 1) * l + half + 1))
                k = slice(KC // 2 * half, KC // 2 * half + KC // 2)
                v.tensor_tensor(xs[:, k, :], XG, nffn[:, l, k].unsqueeze(2).to_broadcast([P, KC // 2, QUAD * CAP]),
                                ALU.mult).then_inc(S["xs_done"], 1)

            def slot_gates(q, e, l, b):
                dve.wait_ge(S["b_done"], e + (NE * l + 1))
                if b == 0:
                    dve.wait_ge(S["comb_done"], q + NE // QUAD * l + 1)
                link(v.tensor_scalar(G4[b], B_ps[:, 0:SEQ], slot_id[:, :], None, ALU.is_equal))
                v.tensor_tensor(G4[b], G4[b], B_ps[:, SEQ:], ALU.mult).then_inc(S["g4_done"], 1)

            def overflow(e, k, l, s):
                oc = Chain(dve, S["ovf_chain"], k * 8)
                dve.wait_ge(S["ov_done"], k + 1)
                oc.link(v.tensor_scalar(o_sel, ident[0:NE, ds(e, 1)].to_broadcast([NE, P]), 1.0, None, ALU.mult))
                v.tensor_tensor(o_S, o_iota.unsqueeze(1).to_broadcast([P, TT, CAP]),
                                pos[:, :, ds(e, 1)].to_broadcast([P, TT, CAP]), ALU.is_equal).then_inc(S["ov_sel"], 1)
                dve.wait_ge(S["ov_b"], k + 1)
                oc.link(v.tensor_scalar(o_G4, B_ps[:, 0:SEQ], o_slot, None, ALU.is_equal))
                oc.link(v.tensor_tensor(o_G4, o_G4, B_ps[:, SEQ:], ALU.mult))
                v.tensor_tensor(o_xs, o_XG, nffn[:, l, :].unsqueeze(2).to_broadcast([P, KC, CAP]), ALU.mult
                                ).then_inc(S["ov_x"], 1)
                oc.link(v.tensor_scalar(o_iota, o_iota, float(CAP), None, ALU.add))
                oc.link(v.tensor_scalar(o_slot, o_slot, float(CAP), None, ALU.add))
                dve.wait_ge(S["ov_exp"], k + 1)
                oc.link(v.tensor_scalar(o_eg, o_eg, 1.0, None, ALU.add))
                oc.link(v.reciprocal(o_eg, o_eg))
                oc.link(v.tensor_tensor(o_eg, o_eg, GU[s][:, 0, :], ALU.mult))
                v.tensor_tensor(o_h, o_eg, GU[s][:, 1, :], ALU.mult).then_inc(S["ov_h"], 1)
                assert oc.n == 8

            def moe(l):
                if l == 0:
                    dve.wait_ge(S["par_wr"], 15 * 16)
                norm(2 * l + 1, nffn[:, l, :])
                route(l)
                dve.wait_ge(S["pg_done"], l + 1)
                select_quad(0)
                gathered(0, l, 0)
                gathered(0, l, 1)
                with chain.loop(0, NE // QUAD, QUAD * 6) as q:
                    for j in range(QUAD):
                        s = j % 2
                        e = q * QUAD + j
                        E = e + NE * l
                        select_rows(q, j)
                        if j == 1:
                            select_quad(q + 1)
                        dve.wait_ge(S["gexp"], E + 1)
                        link(v.tensor_scalar(eg, eg, 1.0, None, ALU.add))
                        link(v.reciprocal(eg, eg))
                        link(v.tensor_tensor(eg, eg, GU[s][:, 0, :], ALU.mult))
                        v.tensor_tensor(hb, eg, GU[s][:, 1, :], ALU.mult).then_inc(S["h_done"], 1)
                        k0 = dve.value_load(table[0:1, ds(e + (NE + 1) * l, 1)], min_val=0, max_val=2 * NE)
                        k1 = dve.value_load(table[0:1, ds(e + ((NE + 1) * l + 1), 1)], min_val=0, max_val=2 * NE)
                        link(v.tensor_scalar(o_iota, iota[:, :], float(CAP), None, ALU.add))
                        link(v.tensor_scalar(o_slot, slot_id[:, :], float(CAP), None, ALU.add))
                        slot_gates(q, e, l, j)
                        if j == QUAD - 1:
                            gathered(q + 1, l, 0)
                            gathered(q + 1, l, 1)
                        with dve.If(k0 < k1):
                            with dve.Fori(k0, k1) as k:
                                overflow(e, k, l, s)
                dve.wait_ge(S["comb_done"], NE // QUAD * (l + 1) + 1)
                for c in range(4):
                    a = h[:, :, 256 * c:256 * c + 256]
                    ins = v.tensor_tensor(a, a, acc[:, c, :].rearrange("p (t n) -> p t n", t=TT), ALU.add)
                    if c < 3:
                        link(ins)
                ins.then_inc(S["h_next"], 1)

            moe(0)

            norm(2, nmix[:, 1, :])

            def odd_z(g, p):
                dve.wait_ge(S["z1_exp"], g + 1)
                v.tensor_tensor(sz[p], ez, pa2, ALU.mult).then_inc(S["z1_silu"], 1)

            def taps(src, tiles):
                for m in (1, 2, 3):
                    for j, tile in enumerate(tiles):
                        w = conv_cols[:, ds(tile + (3 - m) * 32, 1)]
                        ins = v.scalar_tensor_tensor(cv[:, j, m:], src[:, j, 0:SEQ - m], w, cv[:, j, m:],
                                                     ALU.mult, ALU.add)
                    if m < 3:
                        link(ins)
                return ins

            def odd_x_taps(g):
                dve.wait_ge(S["x1_tap"], g + 1)
                taps(pb2, [g * 2, g * 2 + 1]).then_inc(S["x1_conv"], 1)

            def odd_x_silu(g, p):
                dve.wait_ge(S["x1_exp"], g + 1)
                v.tensor_tensor(xT[p], cv, ecv, ALU.mult).then_inc(S["x1_silu"], 1)

            def odd_bc(g, p):
                dve.wait_ge(S["bc_tap"], g + 1)
                taps(pa2, [g + 16, g + 24]).then_inc(S["bc_conv"], 1)
                dve.wait_ge(S["bc_exp"], g + 1)
                v.tensor_tensor(bcT[p], cv, ecv, ALU.mult).then_inc(S["bc_silu"], 1)

            def group_selector(g):
                v.tensor_scalar(gsel, group_of[:, ds(g, 1)].to_broadcast([HEADS, P]), 1.0, None, ALU.mult).then_inc(S["gsel_done"], 1)

            dve.wait_ge(S["par_head"], 4 * 16)
            for q in range(2):
                v.tensor_copy(dskip[64 * q:64 * q + 64, :], skip_row[64 * q:64 * q + 64, q:HEADS:2])
            dve.wait_ge(S["dt_raw"], 1)
            v.tensor_tensor(dtv, pa[:, 0:TT * HEADS].rearrange("p (t n) -> p t n", t=TT),
                            dtb[:, :].unsqueeze(1).to_broadcast([P, TT, HEADS]), ALU.add).then_inc(S["dt_pre"], 1)
            dve.wait_ge(S["dt_ln"], 1)
            link(v.scalar_tensor_tensor(dtv, dtv, 0.0, dta, ALU.max, ALU.add))
            dve.wait_ge(S["alog_exp"], 1)
            link(v.tensor_tensor(dta, dtv, w0.unsqueeze(1).to_broadcast([P, TT, HEADS]), ALU.mult))
            v.tensor_scalar(dta, dta, -1.0, None, ALU.mult).then_inc(S["dt_a"], 1)
            dve.wait_ge(S["cum_done"], 1)
            cum = pb[:, 0:TT * HEADS].rearrange("p (t n) -> p t n", t=TT)
            link(v.tensor_copy(csn, cum))
            v.tensor_tensor(dtw, pb[:, 64:96], csn[:, 0, :], ALU.subtract).then_inc(S["cum_used"], 1)
            for b in range(2):
                link(v.tensor_tensor(csx[:, b, :, :],
                                     wa[0:HEADS, P * b:P * b + P].unsqueeze(1).to_broadcast([HEADS, HPG, P]),
                                     rank_of[:, :].unsqueeze(2).to_broadcast([HEADS, HPG, P]), ALU.mult))
            dve.wait_ge(S["alog_exp"], 2)
            v.tensor_tensor(dtw, dtv[:, 0, :], w0, ALU.mult).then_inc(S["csx_done"], 1)
            group_selector(0)
            odd_z(0, 0)
            odd_x_taps(0)
            odd_x_silu(0, 0)
            odd_bc(0, 0)

            def odd_unit(g, p, more):
                dve.wait_ge(S["csrow_done"], g + 1)
                for b, w in enumerate((wa, wb)):
                    for r in range(HPG):
                        ins = v.tensor_scalar(decay[:, b, r, :], w[:, P * r:P * r + P],
                                              csn[:, b, ds(g * HPG + r, 1)], 0.0, ALU.subtract, ALU.min)
                ins.then_inc(S["seg_done"], 1)
                dve.wait_ge(S["cb_done"], g + 1)
                dve.wait_ge(S["decay_done"], g + 1)
                for c, m in ((0, True), (1, False), (2, True)):
                    a = cbs[:, P * c:P * c + P]
                    src = wa[:, P * c:P * c + P]
                    ins = v.tensor_tensor(a, src, upper[:, :], ALU.mult) if m else v.tensor_copy(a, src)
                link(ins)

                def heads(c):
                    return cbs[:, P * c:P * c + P].unsqueeze(1).to_broadcast([P, HPG, P])
                for b, c in ((0, 0), (1, 2)):
                    v.tensor_tensor(decay[:, b], decay[:, b], heads(c), ALU.mult)
                v.tensor_tensor(decay[:, 2], decay[:, 2], heads(1), ALU.mult)
                dve.wait_ge(S["xst_done"], g + 1)
                for t in range(TT):
                    v.tensor_tensor(xdt[:, t, :].rearrange("p (r d) -> p r d", r=HPG),
                                    wb[:, 256 * t:256 * t + 256].rearrange("p (r d) -> p r d", r=HPG),
                                    dtv[:, t, ds(g * HPG, HPG)].unsqueeze(2).to_broadcast([P, HPG, HD]),
                                    ALU.mult)
                v.tensor_tensor(xw.rearrange("p (r d) -> p r d", r=HPG),
                                wb[:, 0:256].rearrange("p (r d) -> p r d", r=HPG),
                                dtw[:, ds(g * HPG, HPG)].unsqueeze(2).to_broadcast([P, HPG, HD]),
                                ALU.mult).then_inc(S["xdt_done"], 1)
                if more:
                    odd_z(g + 1, 1 - p)
                    odd_x_taps(g + 1)
                dve.wait_ge(S["y_done"], g + 1)
                for j in range(2):
                    ins = v.scalar_tensor_tensor(yz[:, j, :], xT[p][:, j, :], dskip[:, ds(g * 2 + j, 1)],
                                                 wa[:, 256 * j:256 * j + 256], ALU.mult, ALU.add)
                link(ins)
                link(v.tensor_tensor(yz, yz, sz[p], ALU.mult))
                v.tensor_tensor(sq, yz, yz, ALU.mult).then_inc(S["yz_done"], 1)
                if more:
                    odd_x_silu(g + 1, 1 - p)
                dve.wait_ge(S["yss_done"], g + 1)
                v.tensor_scalar(ms, wb[:, 0:SEQ], 1.0 / 256, EPS, ALU.mult, ALU.add).then_inc(S["yms_done"], 1)
                dve.wait_ge(S["yguess"], g + 1)
                newton(rg, ms, rt)
                link(v.tensor_tensor(rg, rg, rt, ALU.mult))
                dve.wait_ge(S["oproj"], g + EVEN_UNITS - 1)
                for j in range(2):
                    ins = v.scalar_tensor_tensor(mix1[p][:, j, :], yz[:, j, :], vec_cols[:, ds(g * 2 + (32 + j), 1)],
                                                 rg, ALU.mult, ALU.mult)
                ins.then_inc(S["mix1_done"], 1)
                if more:
                    group_selector(g + 1)
                    odd_bc(g + 1, 1 - p)

            with chain.loop(0, (ODD_UNITS - 2) // 2, 2 * 11) as i:
                for p in range(2):
                    odd_unit(i * 2 + p, p, True)
            odd_unit(ODD_UNITS - 2, 0, True)
            odd_unit(ODD_UNITS - 1, 1, False)
            residual_mixer(1)

            moe(1)
            norm(4, None)
            dve.wait_ge(S["fnorm_in"], 16)
            for t in range(TT):
                ins = v.scalar_tensor_tensor(y_out[:, t, :], h[:, t, :], st[:, 4, t:t + 1], fnorm,
                                             ALU.mult, ALU.mult)
                if t == 0:
                    link(ins)
            ins.then_inc(S["h_next"], 1)

        @block.tensor
        def _(pe):
            mm = nc.tensor.matmul

            def zero_acc():
                for b in range(4):
                    ins = mm(acc[:, b, :], zero_bf[:, 0:P], zero_bf[:, :], start=True, stop=True,
                             skip_group_check=True)
                return ins

            def transposes(n):
                pe.wait_ge(S["hs_dve"], 2 * n + 2)
                pe.wait_ge(S["hs_act"], n + 1)
                for b in range(4):
                    for j in range(2):
                        for t in range(TT):
                            o = BANKS[b][:, 256 * j + P * t:256 * j + P * t + P]
                            ins = nc.tensor.transpose(o, hs[:, t, 2 * b + j, :], ident[:, :])
                    ins.then_inc(S["hs_t"], 1)
                pe.wait_ge(S["hnt_dve"], 2 * n + 2)
                pe.wait_ge(S["hnt_act"], 4 * n + 4)

            def project(dst, w, j, used=None):
                for k in range(KC):
                    ins = mm(dst, w[:, k, j, :], hnT[:, k, :], start=(k == 0), stop=(k == KC - 1))
                return ins

            def out_project(m, u):
                pe.wait_ge(S["wo_in"], (u + 1) * 16)
                for t in range(TT):
                    for n in range(2):
                        for j in range(2):
                            ins = mm(acc[:, 2 * t + n, :], m[:, j, P * t:P * t + P], w_o[:, j, 512 * n:512 * n + 512],
                                     start=False, stop=False, skip_group_check=True)
                ins.then_inc(S["oproj"], 1)

            pe.wait_ge(S["consts_pool"], 1)
            pe.wait_ge(S["par_conv"], 64)
            nc.tensor.transpose(pa[:, 0:P], conv_raw[:, :], ident[:, :])
            nc.tensor.transpose(pa[:, P:P + 60], vec_raw[:, :], ident[0:60, 0:60]).then_inc(S["conv_raw_t"], 1)
            zero_acc()
            pe.wait_ge(S["conv_cols"], 2)
            transposes(0)

            def even_c0(u):
                pe.wait_ge(S["c0_in"], 16 * (u + 1))
                if u:
                    pe.wait_ge(S["kv_copied"], 2 * u)
                project(pa[:, 0:SEQ], w_c[0], 0)
                project(pa[:, SEQ:], w_c[0], 1).then_inc(S["gc_hid"], 1)

            def even_c1(u):
                pe.wait_ge(S["c1_in"], 16 * (u + 1))
                if u:
                    pe.wait_ge(S["q_copied"], u)
                project(pb[:, 0:SEQ], w_c[1], 0)
                project(pb[:, SEQ:], w_c[1], 1).then_inc(S["gb_q"], 1)

            def even_c2(u):
                pe.wait_ge(S["c2_in"], 16 * (u + 1))
                pe.wait_ge(S["ch_done"], u + 1)
                project(pa[:, 0:SEQ], w_c[2], 0)
                for t in range(TT):
                    for k in range(KC):
                        ins = mm(pa[:, SEQ + P * t:SEQ + P * t + P], hnT[:, k, P * t:P * t + P], w_c[2][:, k, 1, :],
                                 start=(k == 0), stop=(k == KC - 1))
                ins.then_inc(S["k_v"], 1)

            def even_scores(u):
                pe.wait_ge(S["kv_copied"], 2 * u + 2)
                pe.wait_ge(S["q_copied"], u + 1)
                if u:
                    pe.wait_ge(S["av_copied"], u)
                q, k = qS[u % 2], kS[u % 2]
                for hh, w in enumerate((wa, wb)):
                    r = slice(HD * hh, HD * hh + HD)
                    mm(w[:, 0:SEQ], k[r, 0:P], q[r, :], start=True, stop=True)
                    mm(w[:, SEQ:SEQ + P], k[r, P:SEQ], q[r, P:SEQ], start=True, stop=True).then_inc(S["z_done"], 1)

            def even_suffix(u):
                pe.wait_ge(S["sp_done"], 2 * u + 2)
                pe.wait_ge(S["z_copied"], 2 * u + 2)
                for hh, w in enumerate((wa, wb)):
                    mm(w[:, 0:384], lower[:, :], sp[:, hh, :], start=True, stop=False, skip_group_check=True)
                    mm(w[:, P:SEQ], ones[:, :], sp[:, hh, SEQ:], start=False, stop=True,
                       skip_group_check=True).then_inc(S["r_done"], 1)

            def even_values(u):
                pe.wait_ge(S["att_done"], 2 * u + 2)
                vv = vS[u % 2]
                for hh in range(2):
                    o = wa[HD * hh:HD * hh + HD, :]
                    c = slice(HD * hh, HD * hh + HD)
                    mm(o[:, 0:SEQ], vv[:, 0, c], att[:, hh, 0:SEQ], start=True, stop=False, skip_group_check=True)
                    ins = mm(o[:, P:SEQ], vv[:, 1, c], att[:, hh, SEQ:], start=False, stop=True,
                             skip_group_check=True)
                ins.then_inc(S["av_done"], 1)

            def even_out(u):
                pe.wait_ge(S["conv_done"], u + 1)
                pe.wait_ge(S["av_copied"], u + 1)
                out_project(mix[u % 2], u)

            even_c0(0)
            even_c1(0)
            even_c2(0)
            for u in range(EVEN_UNITS):
                more = u + 1 < EVEN_UNITS
                even_scores(u)
                if more:
                    even_c0(u + 1)
                even_suffix(u)
                if more:
                    even_c1(u + 1)
                even_values(u)
                if more:
                    even_c2(u + 1)
                even_out(u)

            def route(l):
                transposes(2 * l + 1)
                if l == 0:
                    pe.wait_ge(S["par_wr"], 15 * 16)
                for t in range(TT):
                    for k in range(KC):
                        ins = mm(pa[:, 64 * t:64 * t + NG + NE], hnT[:, k, P * t:P * t + P], wr[:, l, k, :],
                                 start=(k == 0), stop=(k == KC - 1))
                ins.then_inc(S["logits"], 1)
                pe.wait_ge(S["h_next"], 2 * l + 1)
                zero_acc()
                pe.wait_ge(S["mask_done"], 2 * l + 1)
                mm(pb[:, 0:NE], upper[:, :], mask[:, 0, :], start=True, stop=True)
                mm(pb[:, NE:2 * NE], upper[:, :], mask[:, 1, :], start=True, stop=False)
                mm(pb[:, NE:2 * NE], ones[:, :], mask[:, 0, :], start=False, stop=True)
                mm(pb[:, 2 * NE:3 * NE], ones[:, :], mask[:, 0, :], start=True, stop=False)
                mm(pb[:, 2 * NE:3 * NE], ones[:, :], mask[:, 1, :], start=False, stop=True).then_inc(S["ranks"], 1)
                pe.wait_ge(S["mask_done"], 2 * l + 2)
                for t in range(TT):
                    nc.tensor.transpose(wa[0:NE, P * t:P * t + P], pos[:, t, 0:NE], ident[:, :])
                    ins = nc.tensor.transpose(wa[0:NE, SEQ + P * t:SEQ + P * t + P], gates[:, t, :], ident[:, :])
                ins.then_inc(S["pos_t"], 1)

            def rows_of(e, l, j):
                pe.wait_ge(S["prep_sel"], e + (NE * l + 1))
                if l or j:
                    pe.wait_ge(S["g4_done"], e + NE * l)
                mm(B_ps[:, :], sel, PG, start=True, stop=True).then_inc(S["b_done"], 1)

            def gather_quad(q, l, half):
                pe.wait_ge(S["quad_sel"], q + ((NE // QUAD + 1) * l + 1))
                if l or half or not isinstance(q, int):
                    pe.wait_ge(S["xs_done"], q * 2 + (2 * (NE // QUAD + 1) * l + half))
                for k in range(KC // 2):
                    for t in range(TT):
                        ins = mm(XG[:, k, :], hs[:, t, KC // 2 * half + k, :], quad_slots[:, t, :],
                                 start=(t == 0), stop=(t == TT - 1))
                ins.then_inc(S["gath_done"], 1)

            def gate_up(xb, c0, s):
                for k in range(KC):
                    for j in range(4):
                        ins = mm(GU[s][32 * j:32 * j + 32, :, :], xb[:, k, c0:c0 + CAP], w_gu[s][:, :, k, P * j:P * j + P],
                                 start=(k == 0), stop=(k == KC - 1))
                return ins

            def down(ht, s, turn=0):
                for j in range(4):
                    for c in range(4):
                        b = (c + turn) % 4
                        ins = mm(Y_ps[32 * c:32 * c + 32, :], ht[:, 32 * j:32 * j + 32],
                                 w_dn[s][:, j, 256 * b:256 * b + 256], start=(j == 0), stop=(j == 3))
                return ins

            def combine_quad():
                for b in range(4):
                    for t in range(TT):
                        ins = mm(acc[:, b, 256 * t:256 * t + 256], G4[b][:, P * t:P * t + P], yq[:, b, :],
                                 start=False, stop=False, skip_group_check=True)
                return ins

            def combine(g4, y):
                for t in range(TT):
                    for c in range(4):
                        r = slice(32 * c, 32 * c + 32)
                        ins = mm(acc[:, c, 256 * t:256 * t + 256], g4[r, P * t:P * t + P], y[r, :],
                                 start=False, stop=False, skip_group_check=True, tile_position=(32 * c, 0))
                return ins

            def overflow(k, E, l, s):
                pe.wait_ge(S["ov_sel"], k + 1)
                pe.wait_ge(S["y_copied"], E + 1)
                mm(B_ps[:, :], o_sel, PG, start=True, stop=True)
                for c in range(KC):
                    for t in range(TT):
                        ins = mm(o_XG[:, c, :], hs[:, t, c, :], o_S[:, t, :], start=(t == 0), stop=(t == TT - 1))
                ins.then_inc(S["ov_b"], 1)
                pe.wait_ge(S["ov_x"], k + 1)
                gate_up(o_xs, 0, s).then_inc(S["ov_gu"], 1)
                pe.wait_ge(S["ov_h"], k + 1)
                nc.tensor.transpose(HT_ps, o_h, ident[:, :]).then_inc(S["ov_ht"], 1)
                pe.wait_ge(S["ov_htc"], k + 1)
                down(o_hT, s).then_inc(S["ov_dn"], 1)
                pe.wait_ge(S["ov_yc"], k + 1)
                combine(o_G4, o_y).then_inc(S["ov_done"], 1)

            def moe(l):
                route(l)
                pe.wait_ge(S["pg_done"], l + 1)
                pe.wait_ge(S["table_done"], l + 1)
                gather_quad(0, l, 0)
                gather_quad(0, l, 1)
                with pe.Fori(0, NE // QUAD) as q:
                    for j in range(QUAD):
                        s = j % 2
                        i = q * (QUAD // 2) + j // 2
                        e = q * QUAD + j
                        E = e + NE * l
                        pe.wait_ge((S["gu_in0"], S["gu_in1"])[s], i * 32 + (NE // 2 * l + 1) * 32)
                        if j == 0:
                            pe.wait_ge(S["xs_done"], q * 2 + (2 * (NE // QUAD + 1) * l + 2))
                        gate_up(xs, CAP * j, s).then_inc(S["gu_done"], 1)
                        rows_of(e, l, j)
                        if j == QUAD - 1:
                            gather_quad(q + 1, l, 0)
                        if l or j:
                            pe.wait_ge(S["y_copied"], E)
                        pe.wait_ge(S["h_done"], E + 1)
                        nc.tensor.transpose(HT_ps, hb, ident[:, :]).then_inc(S["ht_done"], 1)
                        pe.wait_ge((S["dn_in0"], S["dn_in1"])[s], i * 16 + (NE // 2 * l + 1) * 16)
                        pe.wait_ge(S["ht_copied"], E + 1)
                        down(hT, s, turn=j).then_inc(S["dn_done"], 1)
                        if j == QUAD - 1:
                            gather_quad(q + 1, l, 1)
                            pe.wait_ge(S["y_copied"], E + 1)
                            pe.wait_ge(S["g4_done"], E + 1)
                            combine_quad().then_inc(S["comb_done"], 1)
                        k0 = pe.value_load(table[0:1, ds(e + (NE + 1) * l, 1)], min_val=0, max_val=2 * NE)
                        k1 = pe.value_load(table[0:1, ds(e + ((NE + 1) * l + 1), 1)], min_val=0, max_val=2 * NE)
                        with pe.If(k0 < k1):
                            with pe.Fori(k0, k1) as k:
                                overflow(k, E, l, s)

            moe(0)

            transposes(2)
            pe.wait_ge(S["par_head"], 4 * 16)
            for t in range(TT):
                for k in range(KC):
                    ins = mm(pa[:, HEADS * t:HEADS * t + HEADS], hnT[:, k, P * t:P * t + P], wdt[:, k, :],
                             start=(k == 0), stop=(k == KC - 1))
            ins.then_inc(S["dt_raw"], 1)
            pe.wait_ge(S["h_next"], 2)
            zero_acc()
            pe.wait_ge(S["dt_a"], 1)
            for t in range(TT):
                mm(pb[:, HEADS * t:HEADS * t + HEADS], upper[:, :], dta[:, t, :], start=True, stop=True)
                mm(wa[0:HEADS, P * t:P * t + P], dta[:, t, :], upper[:, :], start=True, stop=True)
            mm(pb[:, 64:96], ones[:, :], dta[:, 0, :], start=True, stop=True).then_inc(S["cum_done"], 1)

            def odd_c0(g):
                pe.wait_ge(S["c0_in"], g * 16 + 16 * (EVEN_UNITS + 1))
                if not isinstance(g, int) or g:
                    pe.wait_ge(S["bc_silu"], g)
                project(pa[:, 0:SEQ], w_c[0], 0)
                project(pa[:, SEQ:], w_c[0], 1).then_inc(S["z1_done"], 1)

            def odd_c1(g):
                pe.wait_ge(S["c1_in"], g * 16 + 16 * (EVEN_UNITS + 1))
                if not isinstance(g, int) or g:
                    pe.wait_ge(S["x1_silu"], g)
                else:
                    pe.wait_ge(S["cum_used"], 1)
                project(pb[:, 0:SEQ], w_c[1], 0)
                project(pb[:, SEQ:], w_c[1], 1).then_inc(S["x1_done"], 1)

            def odd_b(g):
                pe.wait_ge(S["c2_in"], g * 16 + 16 * (EVEN_UNITS + 1))
                pe.wait_ge(S["z1_silu"], g + 1)
                project(pa[:, 0:SEQ], w_c[2], 0)

            def odd_c(g):
                project(pa[:, SEQ:], w_c[2], 1).then_inc(S["bc_done"], 1)

            def odd_rows(g):
                pe.wait_ge(S["gsel_done"], g + 1)
                if not isinstance(g, int) or g:
                    pe.wait_ge(S["mix1_done"], g)
                for b, w in enumerate((wa, wb)):
                    ins = mm(w[:, :], gsel, csx[:, b, :, :].rearrange("p r l -> p (r l)"), start=True, stop=True)
                ins.then_inc(S["csrow_done"], 1)

            def odd_scores(g, p):
                pe.wait_ge(S["bc_silu"], g + 1)
                pe.wait_ge(S["x1_silu"], g + 1)
                pe.wait_ge(S["decay_done"], g + 1)
                bt, ct = bcT[p][:, 0, :], bcT[p][:, 1, :]
                mm(wa[:, 0:SEQ], bt[:, 0:P], ct, start=True, stop=True)
                mm(wa[:, SEQ:384], bt[:, P:], ct[:, P:], start=True, stop=True).then_inc(S["cb_done"], 1)
                for t in range(TT):
                    for j in range(2):
                        ins = nc.tensor.transpose(wb[:, 256 * t + P * j:256 * t + P * j + P],
                                                  xT[p][:, j, P * t:P * t + P], ident[:, :])
                ins.then_inc(S["xst_done"], 1)

            def odd_y(g):
                pe.wait_ge(S["xdt_done"], g + 1)
                for r in range(HPG):
                    o = wa[HD * (r % 2):HD * (r % 2) + HD, 256 * (r // 2):256 * (r // 2) + 256]
                    c = slice(HD * r, HD * r + HD)
                    mm(o[:, 0:P], xdt[:, 0, c], decay[:, 0, r, :], start=True, stop=True)
                    mm(o[:, P:], xdt[:, 1, c], decay[:, 1, r, :], start=True, stop=False)
                    ins = mm(o[:, P:], xw[:, c], decay[:, 2, r, :], start=False, stop=True)
                ins.then_inc(S["y_done"], 1)

            def odd_ss(g):
                pe.wait_ge(S["yz_done"], g + 1)
                for j in range(2):
                    ins = mm(wb[:, 0:SEQ], ones[:, :], sq[:, j, :], start=(j == 0), stop=(j == 1))
                ins.then_inc(S["yss_done"], 1)

            def odd_out(g, p):
                pe.wait_ge(S["mix1_done"], g + 1)
                out_project(mix1[p], g + EVEN_UNITS)

            pe.wait_ge(S["dt_pre"], 1)
            odd_c0(0)
            odd_c1(0)
            odd_b(0)
            odd_c(0)
            pe.wait_ge(S["csx_done"], 1)

            def odd_unit(g, p, more):
                odd_rows(g)
                if more:
                    odd_c0(g + 1)
                odd_scores(g, p)
                if more:
                    odd_c1(g + 1)
                odd_y(g)
                if more:
                    odd_b(g + 1)
                odd_ss(g)
                if more:
                    odd_c(g + 1)
                odd_out(g, p)

            with pe.Fori(0, (ODD_UNITS - 2) // 2) as i:
                for p in range(2):
                    odd_unit(i * 2 + p, p, True)
            odd_unit(ODD_UNITS - 2, 0, True)
            odd_unit(ODD_UNITS - 1, 1, False)

            moe(1)


_INS = ['x', 'even_w_in', 'even_conv_w', 'even_w_out', 'odd_in_proj', 'odd_conv_w', 'odd_conv_b',
        'odd_dt_bias', 'odd_a_log', 'odd_d_skip', 'odd_norm_w', 'odd_out_proj', 'norm_mix', 'norm_ffn',
        'router_g_w', 'router_g_b', 'router_e_w', 'router_e_b', 'expert_w_gate', 'expert_w_up',
        'expert_w_down', 'final_norm']


def kernel(**inputs):
    import numpy as _np
    import concourse.bacc as _bacc
    from concourse import mybir as _mybir
    from concourse.bass_utils import run_bass_kernel_spmd as _run

    nc = _bacc.Bacc("TRN2", target_bir_lowering=False, num_devices=1)
    arrays, args = {}, []
    for name in _INS:
        a = _np.ascontiguousarray(inputs[name])
        arrays[f"in_{name}"] = a
        args.append(nc.dram_tensor(f"in_{name}", a.shape, _mybir.dt.from_np(a.dtype), kind="ExternalInput").ap())
    args.append(nc.dram_tensor("out_0", (1, SEQ, D), _mybir.dt.from_np(_np.dtype("float32")),
                               kind="ExternalOutput").ap())
    trunk_program(nc, *args)
    r = _run(nc, [arrays], core_ids=[0])
    return r.results[0]["out_0"]
```

```python
from contextlib import ExitStack, contextmanager

import concourse.bass as bass
from concourse import mybir

F32 = mybir.dt.float32
BF16 = mybir.dt.bfloat16
I32 = mybir.dt.int32
ALU = mybir.AluOpType
ACT = mybir.ActivationFunctionType
AX = mybir.AxisListType.X

P = 128
D = 1024
KC = D // P
TT = 2
SEQ = TT * P
EVEN_UNITS = 4
ODD_UNITS = 8
HPG = 4
HD = 64
HEADS = 32
XB0, BB0, CB0 = 2048, 4096, 5120
DT0 = 6144
NE = 32
NG = 4
EPG = 8
FF = 512
QUAD = 4
CAP = 32
SLOT = (0, 1, 2, 1)
NORMS = 5
MAXB = SEQ // CAP
EPS = 1e-6
BIG = 1.0e30
ds = bass.ds


class Chain:

    def __init__(self, eng, sem, base=0):
        self.eng, self.sem, self.base, self.n = eng, sem, base, 0

    def link(self, ins):
        ins.then_inc(self.sem, 1)
        self.n += 1
        self.eng.wait_ge(self.sem, self.base + self.n)

    @contextmanager
    def loop(self, start, end, per):
        first = self.base + self.n
        with self.eng.Fori(start, end) as i:
            self.base, self.n = (i - start) * per + first, 0
            yield i
            assert self.n == per, (self.n, per)
        self.base, self.n = first + (end - start) * per, 0


SEMS = """
x_in0 x_in1 par_vec par_conv par_head par_wr fnorm_in out_stored
consts_pool consts_dve
c0_in c1_in c2_in wo_in
gu_in0 gu_in1 gu_in2 dn_in0 dn_in1 dn_in2
dve_chain act_chain pool_chain ovf_chain
conv_raw_t conv_cols
sum_sq mean_sq rstd hs_dve hs_act hs_t hnt_dve hnt_act h_part oproj_t0 y_ready
gc_hid hid_copied ch_done gb_q gb_copied q_copied k_v kv_copied conv_done
z_done z_copied z_log sp_done r_done att_in att_exp att_done av_done av_copied oproj
dt_raw dt_pre dt_ln dt_a cum_done cum_used csx_done alog_exp
z1_done z1_exp z1_silu x1_done x1_tap x1_conv x1_exp x1_silu bc_done bc_tap bc_conv bc_exp bc_silu
gsel_done csrow_done seg_done decay_done cb_done xst_done xdt_done y_done yz_done yss_done yms_done yguess mix1_done
logits route_d route_e mask_done ranks table_done pos_t pg_done
prep_sel quad_sel b_done g4_done gath_done xs_done gu_done gexp h_done ht_done ht_copied dn_done y_copied comb_part
ov_sel ov_b ov_x ov_gu ov_exp ov_h ov_ht ov_htc ov_dn ov_yc ov_done
""".split()


def trunk_program(nc, x, even_w_in, even_conv_w, even_w_out, odd_in_proj, odd_conv_w, odd_conv_b,
                  odd_dt_bias, odd_a_log, odd_d_skip, odd_norm_w, odd_out_proj, norm_mix, norm_ffn,
                  router_g_w, router_g_b, router_e_w, router_e_b, expert_w_gate, expert_w_up,
                  expert_w_down, final_norm, out):
    with ExitStack() as ctx:
        def sb(name, shape, dt=F32):
            return ctx.enter_context(nc.sbuf_tensor(name, shape, dt))

        def ps(name, shape):
            return ctx.enter_context(nc.psum_tensor(name, shape, F32))

        S = {n: ctx.enter_context(nc.semaphore(n)) for n in SEMS}

        h = sb("h", [P, TT, D])
        hs = sb("hs", [P, TT, KC, P])
        hnT = sb("hnT", [P, KC, SEQ])
        w_gu = [sb(f"w_gu{s}", [P, 2, KC, FF]) for s in range(2)]
        w_dn = [sb(f"w_dn{s}", [P, FF // P, D]) for s in range(2)]
        w_x = sb("w_x", [P, 4, 2 * D])
        w_c = [w_x[:, j, :].rearrange("p (k a b) -> p k a b", k=KC, a=2) for j in range(3)]
        w_o = w_x[:, 3, :].rearrange("p (j n) -> p j n", j=2)
        w_gu.append(w_x[:, :, :].rearrange("p (g a) (k f) -> p g (a k) f", g=2, k=KC // 2))

        ident = sb("ident", [P, P])
        upper = sb("upper", [P, P])
        lower = sb("lower", [P, P])
        strict = sb("strict", [P, P])
        ones = sb("ones", [P, P])
        zero_bf = sb("zero_bf", [P, 512], BF16)
        iota = sb("iota", [P, NE])
        slot_id = sb("slot_id", [P, 1])
        descend = sb("descend", [P, NE])
        one_c = sb("one_c", [P, 1])
        minus_half = sb("minus_half", [P, TT])
        group_of = sb("group_of", [HEADS, ODD_UNITS])
        rank_of = sb("rank_of", [HEADS, HPG])
        turned = sb("turned", [NE, NE // QUAD, 2 * QUAD - 1])
        nmix = sb("nmix", [P, 2, KC])
        nffn = sb("nffn", [P, 2, KC])
        conv_raw = sb("conv_raw", [P, P])
        vec_raw = sb("vec_raw", [60, P])
        conv_cols = sb("conv_cols_sb", [P, P])
        vec_cols = sb("vec_cols", [P, 60])
        skip_row = sb("skip_row", [P, HEADS])
        dskip = sb("dskip", [P, 16])
        wr = sb("wr", [P, 2, KC, NG + NE])
        rbias = sb("rbias", [P, 2, NG + NE])
        dtb = sb("dtb", [P, HEADS])
        alog = sb("alog", [P, HEADS])
        wdt = sb("wdt", [P, KC, HEADS])
        st = sb("st", [P, 6, TT])
        table = sb("table", [1, 2 * (NE + 1)], I32)

        ARENA = 11520
        arena = sb("arena", [P, ARENA])
        XDN = ARENA - FF // P * D
        w_dn.append(arena[:, XDN:].rearrange("p (j n) -> p j n", n=D))

        def carve(limit):
            at = [0]

            def take(*shape, rows=P):
                n = 1
                for k in shape:
                    n *= k
                v = arena[0:rows, at[0]:at[0] + n]
                at[0] += n
                assert at[0] <= limit, at[0]
                if len(shape) == 2:
                    v = v.rearrange("p (a b) -> p a b", a=shape[0])
                if len(shape) == 3:
                    v = v.rearrange("p (a b c) -> p a b c", a=shape[0], b=shape[1])
                return v
            return take

        take = carve(XDN)
        qS = [take(SEQ) for _ in range(2)]
        kS = [take(SEQ) for _ in range(2)]
        vS = [take(TT, P) for _ in range(2)]
        hidS, gbS, ch = take(SEQ), take(SEQ), take(SEQ + 2)
        cacc = take(SEQ)
        zS, lS, sp, att = take(2, 384), take(2, 384), take(2, 384), take(2, 384)
        mix = [take(2, SEQ) for _ in range(2)]
        take = carve(ARENA)
        mix1 = [take(2, SEQ) for _ in range(2)]
        ez = take(2, SEQ)
        sz = [take(2, SEQ) for _ in range(2)]
        xT = [take(2, SEQ) for _ in range(2)]
        bcT = [take(2, SEQ) for _ in range(2)]
        cv, ecv = take(2, SEQ), take(2, SEQ)
        csx = take(2, HPG, P, rows=HEADS)
        gsel = take(P, rows=HEADS)
        decay = take(3, HPG, P)
        cbs = take(384)
        xdt, xw = take(TT, 256), take(256)
        yz, sq = take(2, SEQ), take(2, SEQ)
        ms, rg, rt = take(SEQ), take(SEQ), take(SEQ)
        dtv, dta, csn = (take(TT, HEADS) for _ in range(3))
        w0, dtw = take(HEADS), take(HEADS)
        take = carve(XDN)
        pos = take(TT, NE + QUAD)
        gates = take(TT, NE)
        mask = take(TT, NE)
        lg = take(TT, NG + NE)
        rt1, rt2, oh1, oh2 = (take(TT, NE) for _ in range(4))
        m8 = take(8, TT)
        dd, ee = take(TT, 8), take(TT, 8)
        cnt = take(2 * NE + 8)
        PG = take(2 * SEQ, rows=NE)
        sel = take(P, rows=NE)
        quad_slots = take(TT, QUAD * CAP)
        G4 = [take(SEQ) for _ in range(QUAD)]
        xs = take(KC, QUAD * CAP)
        eg, hb, hT = take(P), take(P), take(P)
        yq = take(QUAD, 256)
        o_sel = take(P, rows=NE)
        o_S, o_G4, o_xs = take(TT, CAP), take(SEQ), take(KC, CAP)
        o_eg, o_h, o_hT, o_y = take(P), take(P), take(P), take(256)
        o_iota, o_slot = take(NE), take(1)
        squares = hs[:, :, :, :].rearrange("p t k m -> p t (k m)")

        def norm_parts(n):
            if n == 0:
                return [(t, slice(0, D)) for t in range(TT)]
            if n % 2:
                return [(t, slice(512 * c, 512 * c + 512)) for t in range(TT) for c in range(2)]
            return [(t, slice(256 * c, 256 * c + 256)) for c in range(4) for t in range(TT)]
        sums = st[:, 0:4, :].rearrange("p a t -> p (a t)").rearrange("p (t a) -> p t a", t=TT)
        fnorm = hnT[:, 0:4, :].rearrange("p a b -> p (a b)")
        y_out = w_c[0][:, :, :, :].rearrange("p k a b -> p (k a b)").rearrange("p (t d) -> p t d", t=TT)

        acc = ps("acc", [P, 4, 512])
        pa, pb, wa, wb = (ps(n, [P, 512]) for n in ("pa", "pb", "wa", "wb"))
        BANKS = [pa, pb, wa, wb]
        pa2, pb2 = (b[:, :].rearrange("p (a b) -> p a b", a=2) for b in (pa, pb))
        B_ps = pa
        XG = pb[:, :].rearrange("p (k s) -> p k s", k=KC // 2)
        o_XG = pb[:, 0:256].rearrange("p (k s) -> p k s", k=KC)
        Y_ps = wb[:, 256:512]
        GU = [wa[:, 256 * s:256 * s + 256].rearrange("p (g n) -> p g n", g=2) for s in range(2)]
        HT_ps = wb[:, 0:P]

        w_in_e = even_w_in[0].rearrange("(p k) (b m) -> p k b m", k=KC, b=6)
        w_in_o = odd_in_proj[0].rearrange("(p k) n -> p k n", k=KC)
        w_out_e = even_w_out[0].rearrange("(a c) n -> c a n", a=2)
        w_out_o = odd_out_proj[0].rearrange("(a c) n -> c a n", c=P)
        h_d = x[0].rearrange("(t p) d -> p t d", p=P)
        out_d = out[0].rearrange("(t p) d -> p t d", p=P)

        block = ctx.enter_context(nc.Block())

        @block.sync
        def _(sp_):
            def chunk_even(u, c):
                blocks = (slice(1, 3), slice(0, 4, 3), slice(4, 6))[c]
                if u:
                    sp_.wait_ge((S["gc_hid"], S["gb_q"], S["k_v"])[c], u)
                sp_.dma_start(w_c[c][:, :, :, :], w_in_e[:, :, blocks, P * u:P * u + P]
                              ).then_inc((S["c0_in"], S["c1_in"], S["c2_in"])[c], 16)

            def rows_even(u):
                if u:
                    sp_.wait_ge(S["oproj"], u)
                a = w_out_e[P * u:P * u + P]
                sp_.dma_start(w_o[:, :, :], a).then_inc(S["wo_in"], 16)

            def chunks_odd(g):
                if not isinstance(g, int) or g:
                    sp_.wait_ge(S["z1_done"], g)
                sp_.dma_start(w_c[0][:, :, :, :].rearrange("p k a b -> p k (a b)"),
                              w_in_o[:, :, ds(g * 256, 256)]).then_inc(S["c0_in"], 16)
                if not isinstance(g, int) or g:
                    sp_.wait_ge(S["x1_done"], g)
                sp_.dma_start(w_c[1][:, :, :, :].rearrange("p k a b -> p k (a b)"),
                              w_in_o[:, :, ds(g * 256 + XB0, 256)]).then_inc(S["c1_in"], 16)
                if not isinstance(g, int) or g:
                    sp_.wait_ge(S["bc_done"], g)
                bc = w_in_o[:, :, BB0:DT0].rearrange("p k (a n) -> p k a n", a=2)
                sp_.dma_start(w_c[2][:, :, :, :], bc[:, :, :, ds(g * P, P)]).then_inc(S["c2_in"], 16)

            def rows_odd(g):
                sp_.wait_ge(S["oproj"], g + EVEN_UNITS)
                sp_.dma_start(w_o[:, :, :], w_out_o[:, ds(g * 2, 2), :]).then_inc(S["wo_in"], 16)

            def expert_through(l, e):
                sp_.wait_ge(S["dn_done"], e + (NE * l + 1))
                n = sp_.value_load(table[0:1, ds(e + ((NE + 1) * l + 1), 1)], min_val=0, max_val=2 * NE)
                sp_.wait_ge(S["ov_done"], n + 1)

            def expert_part(l, e, s, part):
                w = (expert_w_gate, expert_w_up, expert_w_down)[part][l, ds(e, 1), :, :]
                if part < 2:
                    sp_.dma_start(w_gu[s][:, part], w.rearrange("a (p k) f -> p (a k) f", k=KC)
                                  ).then_inc((S["gu_in0"], S["gu_in1"], S["gu_in2"])[s], 16)
                else:
                    sp_.dma_start(w_dn[s][:, :, :], w.rearrange("a (j p) n -> p (a j) n", p=P)
                                  ).then_inc((S["dn_in0"], S["dn_in1"], S["dn_in2"])[s], 16)

            def expert(l, e, j, parts=range(3)):
                expert_through(l, e - (4, 2, 4, 2)[j])
                for part in parts:
                    expert_part(l, e, SLOT[j], part)

            def expert_stream(l):
                expert(l, QUAD, 0, (0, 1))
                expert(l, QUAD - 1, QUAD - 1)
                expert_part(l, QUAD, SLOT[0], 2)
                for j in range(1, QUAD):
                    expert(l, QUAD + j, j)
                with sp_.Fori(2, NE // QUAD) as q:
                    for j in range(QUAD):
                        expert(l, q * QUAD + j, j)

            for t in range(TT):
                sp_.dma_start(h[:, t, :], h_d[:, t, :]).then_inc((S["x_in0"], S["x_in1"])[t], 16)
            for c in range(3):
                chunk_even(0, c)
            rows_even(0)
            for c in range(3):
                chunk_even(1, c)
            for u in range(2, EVEN_UNITS):
                for c in range(3):
                    expert_part(0, u - 2, u - 2, c)
                    chunk_even(u, c)
                rows_even(u - 1)
            rows_even(EVEN_UNITS - 1)
            expert_part(0, 2, 2, 2)
            sp_.wait_ge(S["gc_hid"], EVEN_UNITS)
            sp_.wait_ge(S["gb_q"], EVEN_UNITS)
            expert_part(0, 2, 2, 0)
            sp_.wait_ge(S["k_v"], EVEN_UNITS)
            sp_.wait_ge(S["oproj"], EVEN_UNITS)
            expert_part(0, 2, 2, 1)
            sp_.wait_ge(S["table_done"], 1)
            expert_stream(0)
            expert_through(0, NE - 2)
            chunks_odd(0)
            rows_odd(0)
            for s in range(2):
                expert_through(0, (NE - QUAD, NE - 1)[s])
                for part in range(3):
                    expert_part(1, s, s, part)
            chunks_odd(1)
            with sp_.Fori(1, ODD_UNITS - 1) as g:
                chunks_odd(g + 1)
                rows_odd(g)
            rows_odd(ODD_UNITS - 1)
            sp_.wait_ge(S["z1_done"], ODD_UNITS)
            sp_.wait_ge(S["x1_done"], ODD_UNITS)
            expert_part(1, 2, 2, 0)
            sp_.wait_ge(S["bc_done"], ODD_UNITS)
            sp_.wait_ge(S["oproj"], EVEN_UNITS + ODD_UNITS)
            expert_part(1, 2, 2, 1)
            expert_part(1, 2, 2, 2)
            sp_.wait_ge(S["table_done"], 2)
            expert_stream(1)
            for t in range(TT):
                sp_.wait_ge(S["y_ready"], t + 1)
                sp_.dma_start(out_d[:, t, :], y_out[:, t, :]).then_inc(S["out_stored"], 16)
            sp_.wait_ge(S["out_stored"], 16 * TT)

        @block.gpsimd
        def _(pool):
            chain = Chain(pool, S["pool_chain"])
            nc.gpsimd.memset(ones[:, :], 1.0)
            nc.gpsimd.memset(one_c[:, :], 1.0)
            nc.gpsimd.memset(minus_half[:, :], -0.5)
            nc.gpsimd.memset(ident[:, :], 0.0)
            nc.gpsimd.memset(zero_bf[:, :], 0.0)
            nc.gpsimd.memset(group_of[:, :], 1.0)
            nc.gpsimd.iota(iota[:, :], pattern=[[1, NE]], base=0, channel_multiplier=0,
                           allow_small_or_imprecise_dtypes=True)
            nc.gpsimd.iota(descend[:, :], pattern=[[-1, NE]], base=NE, channel_multiplier=0,
                           allow_small_or_imprecise_dtypes=True)
            for q in range(4):
                chain.link(nc.gpsimd.iota(slot_id[32 * q:32 * q + 32, :], pattern=[[0, 1]], base=0,
                                          channel_multiplier=1, allow_small_or_imprecise_dtypes=True))
            nc.gpsimd.affine_select(out=ident[:, :], in_=ident[:, :], compare_op=ALU.not_equal, fill=1.0,
                                    base=0, pattern=[[-1, P]], channel_multiplier=1)
            nc.gpsimd.affine_select(out=upper[:, :], in_=ones[:, :], compare_op=ALU.is_ge, fill=0.0,
                                    base=0, pattern=[[1, P]], channel_multiplier=-1)
            nc.gpsimd.affine_select(out=lower[:, :], in_=ones[:, :], compare_op=ALU.is_ge, fill=0.0,
                                    base=0, pattern=[[-1, P]], channel_multiplier=1)
            nc.gpsimd.affine_select(out=strict[:, :], in_=ones[:, :], compare_op=ALU.is_gt, fill=0.0,
                                    base=0, pattern=[[1, P]], channel_multiplier=-1)
            chain.link(nc.gpsimd.affine_select(out=group_of[:, :], in_=group_of[:, :], compare_op=ALU.is_ge,
                                               fill=0.0, base=0, pattern=[[-HPG, ODD_UNITS]],
                                               channel_multiplier=1))
            nc.gpsimd.affine_select(out=group_of[:, :], in_=group_of[:, :], compare_op=ALU.is_ge, fill=0.0,
                                    base=HPG - 1, pattern=[[HPG, ODD_UNITS]],
                                    channel_multiplier=-1).then_inc(S["consts_pool"], 1)

            for n in range(NORMS):
                pool.wait_ge(S["mean_sq"], n + 1)
                nc.gpsimd.tensor_tensor(st[:, 4, :], st[:, 5, :], minus_half[:, :], ALU.pow).then_inc(S["rstd"], 1)

        @block.scalar
        def _(act):
            chain = Chain(act, S["act_chain"])

            def af(*a, **k):
                return nc.scalar.activation(*a, **k)

            act.dma_start(nmix[:, :, :], norm_mix.rearrange("l (p k) -> p l k", k=KC)).then_inc(S["par_vec"], 16)
            act.dma_start(conv_raw[:, :], odd_conv_w[0].rearrange("k (t c) -> (k t) c", c=P)).then_inc(S["par_conv"], 16)
            act.dma_start(vec_raw[0:32, :], odd_conv_b[0].rearrange("(t c) -> t c", c=P)).then_inc(S["par_conv"], 16)
            act.dma_start(vec_raw[32:48, :], odd_norm_w[0].rearrange("(t c) -> t c", c=P)).then_inc(S["par_conv"], 16)
            act.dma_start(vec_raw[48:60, :], even_conv_w[0].rearrange("k (t c) -> (k t) c", c=P)).then_inc(S["par_conv"], 16)

            def late_params():
                act.dma_start(nffn[:, :, :], norm_ffn.rearrange("l (p k) -> p l k", k=KC)).then_inc(S["par_wr"], 16)
                for l in range(2):
                    act.dma_start(wr[:, l, :, 0:NG],
                                  router_g_w[l].rearrange("(p k) g -> p k g", k=KC)).then_inc(S["par_wr"], 16)
                    for g in range(NG):
                        act.dma_start(wr[:, l, :, NG + EPG * g:NG + EPG * g + EPG],
                                      router_e_w[l, g].rearrange("(p k) e -> p k e", k=KC)).then_inc(S["par_wr"], 16)
                    act.dma_start(rbias[:, l, 0:NG], router_g_b[l].partition_broadcast(P)).then_inc(S["par_wr"], 16)
                    act.dma_start(rbias[:, l, NG:], router_e_b[l].rearrange("g e -> (g e)").partition_broadcast(P)
                                  ).then_inc(S["par_wr"], 16)
                act.dma_start(dtb[:, :], odd_dt_bias[0].partition_broadcast(P)).then_inc(S["par_head"], 16)
                act.dma_start(alog[:, :], odd_a_log[0].partition_broadcast(P)).then_inc(S["par_head"], 16)
                act.dma_start(wdt[:, :, :], w_in_o[:, :, DT0:DT0 + HEADS]).then_inc(S["par_head"], 16)
                act.dma_start(skip_row[:, :], odd_d_skip[0].partition_broadcast(P)).then_inc(S["par_head"], 16)

            def norm(n, wcol):
                for i, (t, cols) in enumerate(norm_parts(n)):
                    if n == 0:
                        act.wait_ge((S["x_in0"], S["x_in1"])[t], 16)
                    else:
                        act.wait_ge(S["h_part"], 4 * n - 3 + (i if n % 2 else i // TT))
                    c = cols.start // (cols.stop - cols.start)
                    ins = af(squares[:, t, cols], h[:, t, cols], ACT.Square, accum_out=sums[:, t, c:c + 1])
                ins.then_inc(S["sum_sq"], 1)
                if wcol is None:
                    return
                act.wait_ge(S["rstd"], n + 1)
                af(hs[:, 1, :, :], h[:, 1, :].rearrange("p (q k) -> p k q", k=KC), ACT.Identity,
                   scale=st[:, 4, 1:2]).then_inc(S["hs_act"], 1)
                for b in (2, 3):
                    act.wait_ge(S["hs_t"], 4 * n + b + 1)
                    for j in range(2):
                        k = 2 * b + j
                        af(hnT[:, k, :], BANKS[b][:, 256 * j:256 * j + 256], ACT.Identity,
                           scale=wcol[:, k:k + 1]).then_inc(S["hnt_act"], 1)

            def even_c0(u):
                act.wait_ge(S["gc_hid"], u + 1)
                if u:
                    act.wait_ge(S["ch_done"], u)
                af(hidS, pa[:, SEQ:2 * SEQ], ACT.Copy).then_inc(S["hid_copied"], 1)

            def even_c1(u):
                act.wait_ge(S["gb_q"], u + 1)
                if u:
                    act.wait_ge(S["conv_done"], u)
                af(gbS, pb[:, 0:SEQ], ACT.Copy).then_inc(S["gb_copied"], 1)
                af(qS[u % 2], pb[:, SEQ:2 * SEQ], ACT.Copy, scale=HD ** -0.5).then_inc(S["q_copied"], 1)

            def even_c2(u):
                act.wait_ge(S["k_v"], u + 1)
                af(kS[u % 2], pa[:, 0:SEQ], ACT.Copy).then_inc(S["kv_copied"], 1)
                af(vS[u % 2], pa2[:, 1, :].rearrange("p (t d) -> p t d", t=TT), ACT.Copy).then_inc(S["kv_copied"], 1)

            def even_attention_scores(u):
                for hh, w in enumerate((wa, wb)):
                    act.wait_ge(S["z_done"], 2 * u + hh + 1)
                    ins = af(zS[:, hh, :], w[:, 0:384], ACT.Copy)
                    ins.then_inc(S["z_copied"], 1)
                act.wait_ge(S["z_copied"], 2 * u + 2)
                chain.link(af(lS, zS, ACT.Abs))
                chain.link(af(lS, lS, ACT.Exp, scale=-1.0))
                af(lS, lS, ACT.Ln, bias=one_c[:, :]).then_inc(S["z_log"], 1)

            def even_attention_weights(u):
                act.wait_ge(S["att_in"], u + 1)
                af(att, att, ACT.Exp).then_inc(S["att_exp"], 1)

            def even_attention_out(u):
                act.wait_ge(S["av_done"], u + 1)
                af(mix[u % 2][:, 1, :], wa[:, 0:SEQ], ACT.Copy).then_inc(S["av_copied"], 1)

            act.wait_ge(S["par_vec"], 16)
            norm(0, nmix[:, 0, :])
            late_params()
            even_c0(0)
            even_c1(0)
            even_c2(0)
            for u in range(EVEN_UNITS):
                more = u + 1 < EVEN_UNITS
                even_attention_scores(u)
                if more:
                    even_c0(u + 1)
                even_attention_weights(u)
                if more:
                    even_c1(u + 1)
                even_attention_out(u)
                if more:
                    even_c2(u + 1)

            def expert_block(q, l, E, j):
                s = j % 2
                act.wait_ge(S["gu_done"], E + 1)
                af(eg, GU[s][:, 0, :], ACT.Exp, scale=-1.0).then_inc(S["gexp"], 1)
                act.wait_ge(S["ht_done"], E + 1)
                af(hT, HT_ps, ACT.Copy).then_inc(S["ht_copied"], 1)
                act.wait_ge(S["dn_done"], E + 1)
                if j == 0:
                    act.wait_ge(S["comb_part"], q * 4 + (NE * l + 4))
                for c in range(4):
                    r = slice(32 * c, 32 * c + 32)
                    ins = af(yq[r, (c + j) % 4, :], Y_ps[r, :], ACT.Copy)
                ins.then_inc(S["y_copied"], 1)

            def overflow(k, s):
                act.wait_ge(S["ov_gu"], k + 1)
                af(o_eg, GU[s][:, 0, :], ACT.Exp, scale=-1.0).then_inc(S["ov_exp"], 1)
                act.wait_ge(S["ov_ht"], k + 1)
                af(o_hT, HT_ps, ACT.Copy).then_inc(S["ov_htc"], 1)
                act.wait_ge(S["ov_dn"], k + 1)
                af(o_y, Y_ps, ACT.Copy).then_inc(S["ov_yc"], 1)

            def moe(l):
                if l == 0:
                    act.wait_ge(S["par_wr"], 15 * 16)
                norm(2 * l + 1, nffn[:, l, :])
                act.wait_ge(S["route_d"], l + 1)
                if l:
                    act.dma_start(fnorm, final_norm.partition_broadcast(P)).then_inc(S["fnorm_in"], 16)
                af(ee[:, :, 0:5], dd[:, :, 0:5], ACT.Exp).then_inc(S["route_e"], 1)
                act.wait_ge(S["pos_t"], l + 1)
                af(PG, wa[0:NE, :], ACT.Copy).then_inc(S["pg_done"], 1)
                act.wait_ge(S["table_done"], l + 1)
                with act.Fori(0, NE // QUAD) as q:
                    for j in range(QUAD):
                        s = j % 2
                        e = q * QUAD + j
                        expert_block(q, l, e + NE * l, j)
                        k0 = act.value_load(table[0:1, ds(e + (NE + 1) * l, 1)], min_val=0, max_val=2 * NE)
                        k1 = act.value_load(table[0:1, ds(e + ((NE + 1) * l + 1), 1)], min_val=0, max_val=2 * NE)
                        with act.If(k0 < k1):
                            with act.Fori(k0, k1) as k:
                                overflow(k, s)

            moe(0)

            def sigmoid(e):
                chain.link(af(e, e, ACT.Ln, bias=one_c[:, :]))
                return af(e, e, ACT.Exp, scale=-1.0)

            def odd_z(g):
                act.wait_ge(S["z1_done"], g + 1)
                chain.link(af(ez, pa2, ACT.Exp, scale=-1.0))
                sigmoid(ez).then_inc(S["z1_exp"], 1)

            def first_tap(src, tiles):
                for j, tile in enumerate(tiles):
                    ins = af(cv[:, j, :], src[:, j, :], ACT.Identity, scale=conv_cols[:, ds(tile + 3 * 32, 1)],
                             bias=vec_cols[:, ds(tile, 1)])
                return ins

            def odd_x(g):
                act.wait_ge(S["x1_done"], g + 1)
                if not isinstance(g, int) or g:
                    act.wait_ge(S["bc_silu"], g)
                first_tap(pb2, [g * 2, g * 2 + 1]).then_inc(S["x1_tap"], 1)
                act.wait_ge(S["x1_conv"], g + 1)
                chain.link(af(ecv, cv, ACT.Exp, scale=-1.0))
                sigmoid(ecv).then_inc(S["x1_exp"], 1)

            def odd_bc(g):
                act.wait_ge(S["bc_done"], g + 1)
                act.wait_ge(S["x1_silu"], g + 1)
                first_tap(pa2, [g + 16, g + 24]).then_inc(S["bc_tap"], 1)
                act.wait_ge(S["bc_conv"], g + 1)
                chain.link(af(ecv, cv, ACT.Exp, scale=-1.0))
                sigmoid(ecv).then_inc(S["bc_exp"], 1)

            def odd_decay(g):
                act.wait_ge(S["seg_done"], g + 1)
                af(decay[:, 0:2, :, :], decay[:, 0:2, :, :], ACT.Exp)
                af(decay[:, 2, :, :], wb[:, :].rearrange("p (r l) -> p r l", r=HPG), ACT.Exp
                   ).then_inc(S["decay_done"], 1)

            def odd_rstd(g):
                act.wait_ge(S["yms_done"], g + 1)
                chain.link(af(rg, ms, ACT.Ln))
                af(rg, rg, ACT.Exp, scale=-0.5).then_inc(S["yguess"], 1)

            norm(2, nmix[:, 1, :])
            act.wait_ge(S["par_head"], 4 * 16)
            act.wait_ge(S["dt_pre"], 1)
            chain.link(af(dta, dtv, ACT.Abs))
            chain.link(af(dta, dta, ACT.Exp, scale=-1.0))
            af(dta, dta, ACT.Ln, bias=one_c[:, :]).then_inc(S["dt_ln"], 1)
            af(w0, alog[:, :], ACT.Exp).then_inc(S["alog_exp"], 1)
            act.wait_ge(S["cum_done"], 1)
            act.wait_ge(S["cum_used"], 1)
            af(w0, dtw, ACT.Exp).then_inc(S["alog_exp"], 1)
            odd_z(0)
            odd_x(0)
            odd_bc(0)

            def odd_unit(g, more):
                odd_decay(g)
                if more:
                    odd_z(g + 1)
                    odd_x(g + 1)
                odd_rstd(g)
                if more:
                    odd_bc(g + 1)

            with chain.loop(0, ODD_UNITS - 1, 7) as g:
                odd_unit(g, True)
            odd_unit(ODD_UNITS - 1, False)

            moe(1)
            norm(4, None)

        @block.vector
        def _(dve):
            chain = Chain(dve, S["dve_chain"])
            v = nc.vector
            link = chain.link

            def newton(r, x, tmp):
                link(v.tensor_tensor(tmp, r, r, ALU.mult))
                link(v.tensor_tensor(tmp, tmp, x, ALU.mult))
                link(v.tensor_scalar(tmp, tmp, -0.5, 1.5, ALU.mult, ALU.add))

            def norm(n, wcol):
                dve.wait_ge(S["sum_sq"], n + 1)
                parts = 1 if n == 0 else 2 if n % 2 else 4
                link(v.tensor_reduce(out=st[:, 5, :], in_=sums[:, :, 0:parts], axis=AX, op=ALU.add))
                v.tensor_scalar(st[:, 5, :], st[:, 5, :], 1.0 / D, EPS, ALU.mult, ALU.add).then_inc(S["mean_sq"], 1)
                dve.wait_ge(S["rstd"], n + 1)
                if wcol is None:
                    return
                v.tensor_scalar(hs[:, 0, :, :], h[:, 0, :].rearrange("p (q k) -> p k q", k=KC),
                                st[:, 4, 0:1], None, ALU.mult).then_inc(S["hs_dve"], 1)
                for b in (0, 1):
                    dve.wait_ge(S["hs_t"], 4 * n + b + 1)
                    v.tensor_tensor(hnT[:, 2 * b:2 * b + 2, :], BANKS[b][:, :].rearrange("p (a b) -> p a b", a=2),
                                    wcol[:, 2 * b:2 * b + 2].unsqueeze(2).to_broadcast([P, 2, SEQ]),
                                    ALU.mult).then_inc(S["hnt_dve"], 1)

            def residual_mixer(l):
                for t in range(TT):
                    dve.wait_ge((S["oproj_t0"], S["oproj"])[t], (EVEN_UNITS, EVEN_UNITS + ODD_UNITS)[l])
                    for n in range(2):
                        v.tensor_tensor(h[:, t, 512 * n:512 * n + 512], h[:, t, 512 * n:512 * n + 512],
                                        acc[:, 2 * t + n, :], ALU.add).then_inc(S["h_part"], 1)

            dve.wait_ge(S["consts_pool"], 1)
            v.tensor_reduce(out=rank_of[:, :], in_=ident[0:HEADS, 0:HEADS].rearrange("p (g r) -> p r g", r=HPG),
                            axis=AX, op=ALU.add).then_inc(S["consts_dve"], 1)
            for m in range(2 * QUAD - 1):
                v.tensor_copy(turned[:, :, m:m + 1], ident[0:NE, (QUAD - 1 - m) % QUAD:NE:QUAD].unsqueeze(2))
            v.memset(ch[:, 0:2], 0.0).then_inc(S["consts_dve"], 1)
            v.memset(table[:, 0:1], 0).then_inc(S["ov_done"], 1)
            v.memset(cnt[:, 0:1], 0.0).then_inc(S["comb_part"], 4)
            dve.wait_ge(S["conv_raw_t"], 1)
            v.tensor_copy(conv_cols[:, :], pa[:, 0:P]).then_inc(S["conv_cols"], 1)
            v.tensor_copy(vec_cols[:, :], pa[:, P:P + 60]).then_inc(S["conv_cols"], 1)
            dve.wait_ge(S["conv_cols"], 2)

            def even_ch(u):
                dve.wait_ge(S["hid_copied"], u + 1)
                v.tensor_tensor(ch[:, 2:], pa[:, 0:SEQ], hidS, ALU.mult).then_inc(S["ch_done"], 1)
                dve.wait_ge(S["ch_done"], u + 1)

            def even_conv(u):
                def tap(k):
                    return vec_cols[:, 48 + 4 * k + u:49 + 4 * k + u]
                link(v.tensor_scalar(cacc, ch[:, 2:], tap(2), None, ALU.mult))
                link(v.scalar_tensor_tensor(cacc, ch[:, 1:1 + SEQ], tap(1), cacc, ALU.mult, ALU.add))
                link(v.scalar_tensor_tensor(cacc, ch[:, 0:SEQ], tap(0), cacc, ALU.mult, ALU.add))
                dve.wait_ge(S["gb_copied"], u + 1)
                if u >= 2:
                    dve.wait_ge(S["oproj"], u - 1)
                v.tensor_tensor(mix[u % 2][:, 0, :], cacc, gbS, ALU.mult).then_inc(S["conv_done"], 1)

            def diag(a):
                return a.rearrange("p h (b l) -> p h b l", l=P)

            def even_softplus(u):
                dve.wait_ge(S["z_log"], u + 1)
                if u:
                    dve.wait_ge(S["r_done"], 2 * u)
                link(v.scalar_tensor_tensor(sp, zS, 0.0, lS, ALU.max, ALU.add))
                for hh in range(2):
                    d = diag(sp)[:, hh, 0:3:2, :]
                    ins = v.tensor_tensor(d, d, strict[:, :].unsqueeze(1).to_broadcast([P, 2, P]), ALU.mult)
                    ins.then_inc(S["sp_done"], 1)

            def even_weights_in(u):
                for hh, w in enumerate((wa, wb)):
                    dve.wait_ge(S["r_done"], 2 * u + hh + 1)
                    ins = v.tensor_tensor(att[:, hh, :], zS[:, hh, :], w[:, 0:384], ALU.subtract)
                link(ins)
                v.tensor_scalar(att, att, 0.0, None, ALU.min).then_inc(S["att_in"], 1)

            def even_weights_mask(u):
                dve.wait_ge(S["att_exp"], u + 1)
                for hh in range(2):
                    d = diag(att)[:, hh, 0:3:2, :]
                    v.tensor_tensor(d, d, strict[:, :].unsqueeze(1).to_broadcast([P, 2, P]), ALU.mult
                                    ).then_inc(S["att_done"], 1)

            dve.wait_ge(S["par_vec"], 16)
            norm(0, nmix[:, 0, :])
            even_ch(0)
            even_conv(0)
            for u in range(EVEN_UNITS):
                more = u + 1 < EVEN_UNITS
                even_softplus(u)
                if more:
                    even_ch(u + 1)
                even_weights_in(u)
                even_weights_mask(u)
                if more:
                    even_conv(u + 1)
            residual_mixer(0)

            def one_hot_first(dst, src, m, n, tmp):
                def col(a):
                    return a.unsqueeze(2).to_broadcast([P, TT, n])
                link(v.tensor_reduce(out=m, in_=src, axis=AX, op=ALU.max))
                link(v.tensor_tensor(tmp, src, col(m), ALU.is_equal))
                link(v.tensor_tensor(tmp, tmp, descend[:, 0:n].unsqueeze(1).to_broadcast([P, TT, n]), ALU.mult))
                link(v.tensor_reduce(out=m8[:, 7, :], in_=tmp, axis=AX, op=ALU.max))
                link(v.tensor_tensor(dst, tmp, col(m8[:, 7, :]), ALU.is_equal))

            def bc(a, n):
                return a.unsqueeze(2).to_broadcast([P, TT, n])

            def route(l):
                dve.wait_ge(S["logits"], l + 1)
                plog = acc[:, 0:TT, 0:NG + NE]
                link(v.tensor_tensor(lg, plog, rbias[:, l, :].unsqueeze(1).to_broadcast([P, TT, NG + NE]), ALU.add))
                gmax, m1, m2, gs, s1, g1, g2 = (m8[:, j, :] for j in range(7))
                one_hot_first(rt2[:, :, 0:NG], lg[:, :, 0:NG], gmax, NG, rt1[:, :, 0:NG])
                link(v.tensor_tensor(dd[:, :, 0:NG], lg[:, :, 0:NG], bc(gmax, NG), ALU.subtract))
                link(v.tensor_scalar(rt2[:, :, 0:NG], rt2[:, :, 0:NG], BIG, -BIG, ALU.mult, ALU.add))
                for t in range(TT):
                    link(v.tensor_tensor(lg[:, t, NG:].rearrange("p (g e) -> p g e", g=NG),
                                         lg[:, t, NG:].rearrange("p (g e) -> p g e", g=NG),
                                         rt2[:, t, 0:NG].unsqueeze(2).to_broadcast([P, NG, EPG]), ALU.add))
                ex = lg[:, :, NG:]
                one_hot_first(oh1, ex, m1, NE, rt1)
                link(v.scalar_tensor_tensor(ex, oh1, -2.0 * BIG, ex, ALU.mult, ALU.add))
                one_hot_first(oh2, ex, m2, NE, rt1)
                v.tensor_tensor(dd[:, :, 4:5], m2.unsqueeze(2), m1.unsqueeze(2), ALU.subtract).then_inc(S["route_d"], 1)
                v.tensor_tensor(mask, oh1, oh2, ALU.add).then_inc(S["mask_done"], 1)
                dve.wait_ge(S["route_e"], l + 1)
                link(v.tensor_reduce(out=gs, in_=ee[:, :, 0:NG], axis=AX, op=ALU.add))
                link(v.tensor_scalar(s1, ee[:, :, 4:5].rearrange("p t o -> p (t o)"), 1.0, None, ALU.add))
                link(v.tensor_tensor(s1, s1, gs, ALU.mult))
                link(v.reciprocal(g1, s1))
                link(v.tensor_tensor(g2, g1, ee[:, :, 4:5].rearrange("p t o -> p (t o)"), ALU.mult))
                link(v.tensor_tensor(oh1, oh1, bc(g1, NE), ALU.mult))
                link(v.tensor_tensor(oh2, oh2, bc(g2, NE), ALU.mult))
                link(v.tensor_tensor(gates, oh1, oh2, ALU.add))
                dve.wait_ge(S["ranks"], l + 1)
                prk = pb[:, 0:2 * NE].rearrange("p (t n) -> p t n", t=TT)
                cs, ov = cnt[0:1, 0:NE], cnt[0:1, NE:2 * NE]
                v.tensor_copy(cs, pb[0:1, 2 * NE:3 * NE])
                link(v.memset(pos[:, :, NE:], -1.0))
                link(v.tensor_tensor(pos[:, :, 0:NE], prk, mask, ALU.mult))
                v.tensor_scalar(pos[:, :, 0:NE], pos[:, :, 0:NE], -1.0, None, ALU.add).then_inc(S["mask_done"], 1)
                dve.wait_ge(S["mask_done"], 2 * l + 2)
                select_quad(0)
                link(v.tensor_scalar(ov, cs, float(CAP), None, ALU.is_gt))
                for b in range(2, MAXB):
                    link(v.scalar_tensor_tensor(ov, cs, float(CAP * b), ov, ALU.is_gt, ALU.add))
                base = (NE + 1) * l
                if l:
                    link(v.tensor_copy(table[:, base:base + 1], table[:, base - 1:base]))
                link(v.tensor_copy(cnt[0:1, 2 * NE:2 * NE + 1], table[:, base:base + 1]))
                v.tensor_tensor_scan(table[:, base + 1:base + NE + 1], ones[0:1, 0:NE], ov,
                                     cnt[0:1, 2 * NE:2 * NE + 1], ALU.mult, ALU.add).then_inc(S["table_done"], 1)

            def select_rows(q, b):
                v.tensor_scalar(sel.rearrange("p (o c s) -> p o c s", o=1, c=QUAD),
                                turned[:, ds(q, 1), QUAD - 1 - b:2 * QUAD - 1 - b].unsqueeze(3).to_broadcast(
                                    [NE, 1, QUAD, CAP]), 1.0, None, ALU.mult).then_inc(S["prep_sel"], 1)

            def select_quad(q):
                v.tensor_tensor(quad_slots.rearrange("p t (e s) -> p t e s", e=QUAD),
                                iota[:, :].unsqueeze(1).unsqueeze(1).to_broadcast([P, TT, QUAD, CAP]),
                                pos[:, :, ds(q * QUAD, QUAD)].unsqueeze(3).to_broadcast([P, TT, QUAD, CAP]),
                                ALU.is_equal).then_inc(S["quad_sel"], 1)

            def gathered(q, l, half):
                dve.wait_ge(S["gath_done"], q * 2 + (2 * (NE // QUAD + 1) * l + half + 1))
                k = slice(KC // 2 * half, KC // 2 * half + KC // 2)
                v.tensor_tensor(xs[:, k, :], XG, nffn[:, l, k].unsqueeze(2).to_broadcast([P, KC // 2, QUAD * CAP]),
                                ALU.mult).then_inc(S["xs_done"], 1)

            def slot_gates(q, e, l, b):
                dve.wait_ge(S["b_done"], e + (NE * l + 1))
                if b == 0:
                    dve.wait_ge(S["comb_part"], q * 4 + (NE * l + 4))
                link(v.tensor_scalar(G4[b], B_ps[:, 0:SEQ], slot_id[:, :], None, ALU.is_equal))
                v.tensor_tensor(G4[b], G4[b], B_ps[:, SEQ:], ALU.mult).then_inc(S["g4_done"], 1)

            def overflow(e, k, l, s):
                oc = Chain(dve, S["ovf_chain"], k * 8)
                dve.wait_ge(S["ov_done"], k + 1)
                oc.link(v.tensor_scalar(o_sel, ident[0:NE, ds(e, 1)].to_broadcast([NE, P]), 1.0, None, ALU.mult))
                v.tensor_tensor(o_S, o_iota.unsqueeze(1).to_broadcast([P, TT, CAP]),
                                pos[:, :, ds(e, 1)].to_broadcast([P, TT, CAP]), ALU.is_equal).then_inc(S["ov_sel"], 1)
                dve.wait_ge(S["ov_b"], k + 1)
                oc.link(v.tensor_scalar(o_G4, B_ps[:, 0:SEQ], o_slot, None, ALU.is_equal))
                oc.link(v.tensor_tensor(o_G4, o_G4, B_ps[:, SEQ:], ALU.mult))
                v.tensor_tensor(o_xs, o_XG, nffn[:, l, :].unsqueeze(2).to_broadcast([P, KC, CAP]), ALU.mult
                                ).then_inc(S["ov_x"], 1)
                oc.link(v.tensor_scalar(o_iota, o_iota, float(CAP), None, ALU.add))
                oc.link(v.tensor_scalar(o_slot, o_slot, float(CAP), None, ALU.add))
                dve.wait_ge(S["ov_exp"], k + 1)
                oc.link(v.tensor_scalar(o_eg, o_eg, 1.0, None, ALU.add))
                oc.link(v.reciprocal(o_eg, o_eg))
                oc.link(v.tensor_tensor(o_eg, o_eg, GU[s][:, 0, :], ALU.mult))
                v.tensor_tensor(o_h, o_eg, GU[s][:, 1, :], ALU.mult).then_inc(S["ov_h"], 1)
                assert oc.n == 8

            def moe(l):
                if l == 0:
                    dve.wait_ge(S["par_wr"], 15 * 16)
                norm(2 * l + 1, nffn[:, l, :])
                route(l)
                gathered(0, l, 0)
                gathered(0, l, 1)
                with chain.loop(0, NE // QUAD, QUAD * 6) as q:
                    for j in range(QUAD):
                        s = j % 2
                        e = q * QUAD + j
                        E = e + NE * l
                        select_rows(q, j)
                        if j == 1:
                            select_quad(q + 1)
                        dve.wait_ge(S["gexp"], E + 1)
                        link(v.tensor_scalar(eg, eg, 1.0, None, ALU.add))
                        link(v.reciprocal(eg, eg))
                        link(v.tensor_tensor(eg, eg, GU[s][:, 0, :], ALU.mult))
                        v.tensor_tensor(hb, eg, GU[s][:, 1, :], ALU.mult).then_inc(S["h_done"], 1)
                        k0 = dve.value_load(table[0:1, ds(e + (NE + 1) * l, 1)], min_val=0, max_val=2 * NE)
                        k1 = dve.value_load(table[0:1, ds(e + ((NE + 1) * l + 1), 1)], min_val=0, max_val=2 * NE)
                        link(v.tensor_scalar(o_iota, iota[:, :], float(CAP), None, ALU.add))
                        link(v.tensor_scalar(o_slot, slot_id[:, :], float(CAP), None, ALU.add))
                        slot_gates(q, e, l, j)
                        if j == QUAD - 1:
                            gathered(q + 1, l, 0)
                            gathered(q + 1, l, 1)
                        with dve.If(k0 < k1):
                            with dve.Fori(k0, k1) as k:
                                overflow(e, k, l, s)
                for c in range(4):
                    dve.wait_ge(S["comb_part"], NE * (l + 1) + c + 1)
                    a = h[:, :, 256 * c:256 * c + 256]
                    v.tensor_tensor(a, a, acc[:, c, :].rearrange("p (t n) -> p t n", t=TT), ALU.add
                                    ).then_inc(S["h_part"], 1)

            moe(0)

            norm(2, nmix[:, 1, :])

            def odd_z(g, p):
                dve.wait_ge(S["z1_exp"], g + 1)
                v.tensor_tensor(sz[p], ez, pa2, ALU.mult).then_inc(S["z1_silu"], 1)

            def taps(src, tiles):
                for m in (1, 2, 3):
                    for j, tile in enumerate(tiles):
                        w = conv_cols[:, ds(tile + (3 - m) * 32, 1)]
                        ins = v.scalar_tensor_tensor(cv[:, j, m:], src[:, j, 0:SEQ - m], w, cv[:, j, m:],
                                                     ALU.mult, ALU.add)
                    if m < 3:
                        link(ins)
                return ins

            def odd_x_taps(g):
                dve.wait_ge(S["x1_tap"], g + 1)
                taps(pb2, [g * 2, g * 2 + 1]).then_inc(S["x1_conv"], 1)

            def odd_x_silu(g, p):
                dve.wait_ge(S["x1_exp"], g + 1)
                v.tensor_tensor(xT[p], cv, ecv, ALU.mult).then_inc(S["x1_silu"], 1)

            def odd_bc(g, p):
                dve.wait_ge(S["bc_tap"], g + 1)
                taps(pa2, [g + 16, g + 24]).then_inc(S["bc_conv"], 1)
                dve.wait_ge(S["bc_exp"], g + 1)
                v.tensor_tensor(bcT[p], cv, ecv, ALU.mult).then_inc(S["bc_silu"], 1)

            def group_selector(g):
                v.tensor_scalar(gsel, group_of[:, ds(g, 1)].to_broadcast([HEADS, P]), 1.0, None, ALU.mult).then_inc(S["gsel_done"], 1)

            dve.wait_ge(S["par_head"], 4 * 16)
            for q in range(2):
                v.tensor_copy(dskip[64 * q:64 * q + 64, :], skip_row[64 * q:64 * q + 64, q:HEADS:2])
            dve.wait_ge(S["dt_raw"], 1)
            v.tensor_tensor(dtv, acc[:, 0:TT, 0:HEADS],
                            dtb[:, :].unsqueeze(1).to_broadcast([P, TT, HEADS]), ALU.add).then_inc(S["dt_pre"], 1)
            dve.wait_ge(S["dt_ln"], 1)
            link(v.scalar_tensor_tensor(dtv, dtv, 0.0, dta, ALU.max, ALU.add))
            dve.wait_ge(S["alog_exp"], 1)
            link(v.tensor_tensor(dta, dtv, w0.unsqueeze(1).to_broadcast([P, TT, HEADS]), ALU.mult))
            v.tensor_scalar(dta, dta, -1.0, None, ALU.mult).then_inc(S["dt_a"], 1)
            dve.wait_ge(S["cum_done"], 1)
            cum = pb[:, 0:TT * HEADS].rearrange("p (t n) -> p t n", t=TT)
            link(v.tensor_copy(csn, cum))
            v.tensor_tensor(dtw, pb[:, 64:96], csn[:, 0, :], ALU.subtract).then_inc(S["cum_used"], 1)
            for b in range(2):
                link(v.tensor_tensor(csx[:, b, :, :],
                                     wa[0:HEADS, P * b:P * b + P].unsqueeze(1).to_broadcast([HEADS, HPG, P]),
                                     rank_of[:, :].unsqueeze(2).to_broadcast([HEADS, HPG, P]), ALU.mult))
            dve.wait_ge(S["alog_exp"], 2)
            v.tensor_tensor(dtw, dtv[:, 0, :], w0, ALU.mult).then_inc(S["csx_done"], 1)
            group_selector(0)
            odd_z(0, 0)
            odd_x_taps(0)
            odd_x_silu(0, 0)
            odd_bc(0, 0)

            def odd_unit(g, p, more):
                dve.wait_ge(S["csrow_done"], g + 1)
                for b, w in enumerate((wa, wb)):
                    for r in range(HPG):
                        ins = v.tensor_scalar(decay[:, b, r, :], w[:, P * r:P * r + P],
                                              csn[:, b, ds(g * HPG + r, 1)], 0.0, ALU.subtract, ALU.min)
                ins.then_inc(S["seg_done"], 1)
                dve.wait_ge(S["cb_done"], g + 1)
                dve.wait_ge(S["decay_done"], g + 1)
                for c, m in ((0, True), (1, False), (2, True)):
                    a = cbs[:, P * c:P * c + P]
                    src = wa[:, P * c:P * c + P]
                    ins = v.tensor_tensor(a, src, upper[:, :], ALU.mult) if m else v.tensor_copy(a, src)
                link(ins)

                def heads(c):
                    return cbs[:, P * c:P * c + P].unsqueeze(1).to_broadcast([P, HPG, P])
                for b, c in ((0, 0), (1, 2)):
                    v.tensor_tensor(decay[:, b], decay[:, b], heads(c), ALU.mult)
                v.tensor_tensor(decay[:, 2], decay[:, 2], heads(1), ALU.mult)
                dve.wait_ge(S["xst_done"], g + 1)
                for t in range(TT):
                    v.tensor_tensor(xdt[:, t, :].rearrange("p (r d) -> p r d", r=HPG),
                                    wb[:, 256 * t:256 * t + 256].rearrange("p (r d) -> p r d", r=HPG),
                                    dtv[:, t, ds(g * HPG, HPG)].unsqueeze(2).to_broadcast([P, HPG, HD]),
                                    ALU.mult)
                v.tensor_tensor(xw.rearrange("p (r d) -> p r d", r=HPG),
                                wb[:, 0:256].rearrange("p (r d) -> p r d", r=HPG),
                                dtw[:, ds(g * HPG, HPG)].unsqueeze(2).to_broadcast([P, HPG, HD]),
                                ALU.mult).then_inc(S["xdt_done"], 1)
                if more:
                    odd_z(g + 1, 1 - p)
                    odd_x_taps(g + 1)
                dve.wait_ge(S["y_done"], g + 1)
                for j in range(2):
                    ins = v.scalar_tensor_tensor(yz[:, j, :], xT[p][:, j, :], dskip[:, ds(g * 2 + j, 1)],
                                                 wa[:, 256 * j:256 * j + 256], ALU.mult, ALU.add)
                link(ins)
                link(v.tensor_tensor(yz, yz, sz[p], ALU.mult))
                v.tensor_tensor(sq, yz, yz, ALU.mult).then_inc(S["yz_done"], 1)
                if more:
                    odd_x_silu(g + 1, 1 - p)
                dve.wait_ge(S["yss_done"], g + 1)
                v.tensor_scalar(ms, wb[:, 0:SEQ], 1.0 / 256, EPS, ALU.mult, ALU.add).then_inc(S["yms_done"], 1)
                dve.wait_ge(S["yguess"], g + 1)
                newton(rg, ms, rt)
                link(v.tensor_tensor(rg, rg, rt, ALU.mult))
                dve.wait_ge(S["oproj"], g + EVEN_UNITS - 1)
                for j in range(2):
                    ins = v.scalar_tensor_tensor(mix1[p][:, j, :], yz[:, j, :], vec_cols[:, ds(g * 2 + (32 + j), 1)],
                                                 rg, ALU.mult, ALU.mult)
                ins.then_inc(S["mix1_done"], 1)
                if more:
                    group_selector(g + 1)
                    odd_bc(g + 1, 1 - p)

            with chain.loop(0, (ODD_UNITS - 2) // 2, 2 * 11) as i:
                for p in range(2):
                    odd_unit(i * 2 + p, p, True)
            odd_unit(ODD_UNITS - 2, 0, True)
            odd_unit(ODD_UNITS - 1, 1, False)
            residual_mixer(1)

            moe(1)
            norm(4, None)
            dve.wait_ge(S["fnorm_in"], 16)
            for t in range(TT):
                v.scalar_tensor_tensor(y_out[:, t, :], h[:, t, :], st[:, 4, t:t + 1], fnorm,
                                       ALU.mult, ALU.mult).then_inc(S["y_ready"], 1)

        @block.tensor
        def _(pe):
            mm = nc.tensor.matmul

            def zero_acc():
                for b in range(4):
                    ins = mm(acc[:, b, :], zero_bf[:, 0:P], zero_bf[:, :], start=True, stop=True,
                             skip_group_check=True)
                return ins

            def transposes(n):
                pe.wait_ge(S["hs_dve"], n + 1)
                pe.wait_ge(S["hs_act"], n + 1)
                for b in range(4):
                    for j in range(2):
                        for t in range(TT):
                            o = BANKS[b][:, 256 * j + P * t:256 * j + P * t + P]
                            ins = nc.tensor.transpose(o, hs[:, t, 2 * b + j, :], ident[:, :])
                    ins.then_inc(S["hs_t"], 1)

            def by_tile(n, dst, w):
                for b in range(4):
                    if b < 2:
                        pe.wait_ge(S["hnt_dve"], 2 * n + b + 1)
                    else:
                        pe.wait_ge(S["hnt_act"], 4 * n + 2 * b - 2)
                    for k in (2 * b, 2 * b + 1):
                        for t in range(TT):
                            ins = mm(dst[t], hnT[:, k, P * t:P * t + P], w[:, k, :], start=(k == 0), stop=(k == KC - 1))
                return ins

            def project(dst, w, j):
                for k in range(KC):
                    ins = mm(dst, w[:, k, j, :], hnT[:, k, :], start=(k == 0), stop=(k == KC - 1))
                return ins

            def out_project(m, u):
                pe.wait_ge(S["wo_in"], (u + 1) * 16)
                for t in range(TT):
                    for n in range(2):
                        for j in range(2):
                            ins = mm(acc[:, 2 * t + n, :], m[:, j, P * t:P * t + P], w_o[:, j, 512 * n:512 * n + 512],
                                     start=False, stop=False, skip_group_check=True)
                    ins.then_inc((S["oproj_t0"], S["oproj"])[t], 1)

            pe.wait_ge(S["consts_pool"], 1)
            pe.wait_ge(S["par_conv"], 64)
            nc.tensor.transpose(pa[:, 0:P], conv_raw[:, :], ident[:, :])
            nc.tensor.transpose(pa[:, P:P + 60], vec_raw[:, :], ident[0:60, 0:60]).then_inc(S["conv_raw_t"], 1)
            zero_acc()
            pe.wait_ge(S["conv_cols"], 2)
            transposes(0)
            pe.wait_ge(S["hnt_dve"], 2)
            pe.wait_ge(S["hnt_act"], 4)

            def even_c0(u):
                pe.wait_ge(S["c0_in"], 16 * (u + 1))
                if u:
                    pe.wait_ge(S["kv_copied"], 2 * u)
                project(pa[:, 0:SEQ], w_c[0], 0)
                project(pa[:, SEQ:], w_c[0], 1).then_inc(S["gc_hid"], 1)

            def even_c1(u):
                pe.wait_ge(S["c1_in"], 16 * (u + 1))
                if u:
                    pe.wait_ge(S["q_copied"], u)
                project(pb[:, 0:SEQ], w_c[1], 0)
                project(pb[:, SEQ:], w_c[1], 1).then_inc(S["gb_q"], 1)

            def even_c2(u):
                pe.wait_ge(S["c2_in"], 16 * (u + 1))
                pe.wait_ge(S["ch_done"], u + 1)
                project(pa[:, 0:SEQ], w_c[2], 0)
                for t in range(TT):
                    for k in range(KC):
                        ins = mm(pa[:, SEQ + P * t:SEQ + P * t + P], hnT[:, k, P * t:P * t + P], w_c[2][:, k, 1, :],
                                 start=(k == 0), stop=(k == KC - 1))
                ins.then_inc(S["k_v"], 1)

            def even_scores(u):
                pe.wait_ge(S["kv_copied"], 2 * u + 2)
                pe.wait_ge(S["q_copied"], u + 1)
                if u:
                    pe.wait_ge(S["av_copied"], u)
                q, k = qS[u % 2], kS[u % 2]
                for hh, w in enumerate((wa, wb)):
                    r = slice(HD * hh, HD * hh + HD)
                    mm(w[:, 0:SEQ], k[r, 0:P], q[r, :], start=True, stop=True)
                    mm(w[:, SEQ:SEQ + P], k[r, P:SEQ], q[r, P:SEQ], start=True, stop=True).then_inc(S["z_done"], 1)

            def even_suffix(u):
                pe.wait_ge(S["sp_done"], 2 * u + 2)
                pe.wait_ge(S["z_copied"], 2 * u + 2)
                for hh, w in enumerate((wa, wb)):
                    mm(w[:, 0:384], lower[:, :], sp[:, hh, :], start=True, stop=False, skip_group_check=True)
                    mm(w[:, P:SEQ], ones[:, :], sp[:, hh, SEQ:], start=False, stop=True,
                       skip_group_check=True).then_inc(S["r_done"], 1)

            def even_values(u):
                pe.wait_ge(S["att_done"], 2 * u + 2)
                vv = vS[u % 2]
                for hh in range(2):
                    o = wa[HD * hh:HD * hh + HD, :]
                    c = slice(HD * hh, HD * hh + HD)
                    mm(o[:, 0:SEQ], vv[:, 0, c], att[:, hh, 0:SEQ], start=True, stop=False, skip_group_check=True)
                    ins = mm(o[:, P:SEQ], vv[:, 1, c], att[:, hh, SEQ:], start=False, stop=True,
                             skip_group_check=True)
                ins.then_inc(S["av_done"], 1)

            def even_out(u):
                pe.wait_ge(S["conv_done"], u + 1)
                pe.wait_ge(S["av_copied"], u + 1)
                out_project(mix[u % 2], u)

            even_c0(0)
            even_c1(0)
            even_c2(0)
            for u in range(EVEN_UNITS):
                more = u + 1 < EVEN_UNITS
                even_scores(u)
                if more:
                    even_c0(u + 1)
                even_suffix(u)
                if more:
                    even_c1(u + 1)
                even_values(u)
                if more:
                    even_c2(u + 1)
                even_out(u)

            def route(l):
                transposes(2 * l + 1)
                if l == 0:
                    pe.wait_ge(S["par_wr"], 15 * 16)
                pe.wait_ge(S["h_part"], 4 * (2 * l + 1))
                by_tile(2 * l + 1, [acc[:, t, 0:NG + NE] for t in range(TT)], wr[:, l]).then_inc(S["logits"], 1)
                pe.wait_ge(S["mask_done"], 2 * l + 1)
                mm(pb[:, 0:NE], upper[:, :], mask[:, 0, :], start=True, stop=True)
                mm(pb[:, NE:2 * NE], upper[:, :], mask[:, 1, :], start=True, stop=False)
                mm(pb[:, NE:2 * NE], ones[:, :], mask[:, 0, :], start=False, stop=True)
                mm(pb[:, 2 * NE:3 * NE], ones[:, :], mask[:, 0, :], start=True, stop=False)
                mm(pb[:, 2 * NE:3 * NE], ones[:, :], mask[:, 1, :], start=False, stop=True).then_inc(S["ranks"], 1)
                zero_acc()
                pe.wait_ge(S["mask_done"], 2 * l + 2)
                for t in range(TT):
                    nc.tensor.transpose(wa[0:NE, P * t:P * t + P], pos[:, t, 0:NE], ident[:, :])
                    ins = nc.tensor.transpose(wa[0:NE, SEQ + P * t:SEQ + P * t + P], gates[:, t, :], ident[:, :])
                ins.then_inc(S["pos_t"], 1)

            def rows_of(e, l, j):
                pe.wait_ge(S["prep_sel"], e + (NE * l + 1))
                if l or j:
                    pe.wait_ge(S["g4_done"], e + NE * l)
                mm(B_ps[:, :], sel, PG, start=True, stop=True).then_inc(S["b_done"], 1)

            def gather_quad(q, l, half):
                pe.wait_ge(S["quad_sel"], q + ((NE // QUAD + 1) * l + 1))
                if l or half or not isinstance(q, int):
                    pe.wait_ge(S["xs_done"], q * 2 + (2 * (NE // QUAD + 1) * l + half))
                for k in range(KC // 2):
                    for t in range(TT):
                        ins = mm(XG[:, k, :], hs[:, t, KC // 2 * half + k, :], quad_slots[:, t, :],
                                 start=(t == 0), stop=(t == TT - 1))
                ins.then_inc(S["gath_done"], 1)

            def gate_up(xb, c0, J):
                s = SLOT[J]
                for k in range(KC):
                    for j in range(4):
                        ins = mm(GU[J % 2][32 * j:32 * j + 32, :, :], xb[:, k, c0:c0 + CAP], w_gu[s][:, :, k, P * j:P * j + P],
                                 start=(k == 0), stop=(k == KC - 1))
                return ins

            def down(ht, J, turn=0):
                s = SLOT[J]
                for j in range(4):
                    for c in range(4):
                        b = (c + turn) % 4
                        ins = mm(Y_ps[32 * c:32 * c + 32, :], ht[:, 32 * j:32 * j + 32],
                                 w_dn[s][:, j, 256 * b:256 * b + 256], start=(j == 0), stop=(j == 3))
                return ins

            def combine_quad():
                for b in range(4):
                    for t in range(TT):
                        ins = mm(acc[:, b, 256 * t:256 * t + 256], G4[b][:, P * t:P * t + P], yq[:, b, :],
                                 start=False, stop=False, skip_group_check=True)
                    ins.then_inc(S["comb_part"], 1)

            def combine(g4, y):
                for t in range(TT):
                    for c in range(4):
                        r = slice(32 * c, 32 * c + 32)
                        ins = mm(acc[:, c, 256 * t:256 * t + 256], g4[r, P * t:P * t + P], y[r, :],
                                 start=False, stop=False, skip_group_check=True, tile_position=(32 * c, 0))
                return ins

            def overflow(k, E, l, J):
                pe.wait_ge(S["ov_sel"], k + 1)
                pe.wait_ge(S["y_copied"], E + 1)
                mm(B_ps[:, :], o_sel, PG, start=True, stop=True)
                for c in range(KC):
                    for t in range(TT):
                        ins = mm(o_XG[:, c, :], hs[:, t, c, :], o_S[:, t, :], start=(t == 0), stop=(t == TT - 1))
                ins.then_inc(S["ov_b"], 1)
                pe.wait_ge(S["ov_x"], k + 1)
                gate_up(o_xs, 0, J).then_inc(S["ov_gu"], 1)
                pe.wait_ge(S["ov_h"], k + 1)
                nc.tensor.transpose(HT_ps, o_h, ident[:, :]).then_inc(S["ov_ht"], 1)
                pe.wait_ge(S["ov_htc"], k + 1)
                down(o_hT, J).then_inc(S["ov_dn"], 1)
                pe.wait_ge(S["ov_yc"], k + 1)
                combine(o_G4, o_y).then_inc(S["ov_done"], 1)

            def moe(l):
                route(l)
                gather_quad(0, l, 0)
                gather_quad(0, l, 1)
                pe.wait_ge(S["pg_done"], l + 1)
                pe.wait_ge(S["table_done"], l + 1)
                with pe.Fori(0, NE // QUAD) as q:
                    for j in range(QUAD):
                        s = SLOT[j]
                        n = q * 2 + (2 * (NE // QUAD) * l + j // 2 + 1) if s == 1 else q + (NE // QUAD * l + 1)
                        e = q * QUAD + j
                        E = e + NE * l
                        pe.wait_ge((S["gu_in0"], S["gu_in1"], S["gu_in2"])[s], n * 32)
                        if j == 0:
                            pe.wait_ge(S["xs_done"], q * 2 + (2 * (NE // QUAD + 1) * l + 2))
                        gate_up(xs, CAP * j, j).then_inc(S["gu_done"], 1)
                        rows_of(e, l, j)
                        if j == QUAD - 1:
                            gather_quad(q + 1, l, 0)
                        if l or j:
                            pe.wait_ge(S["y_copied"], E)
                        pe.wait_ge(S["h_done"], E + 1)
                        nc.tensor.transpose(HT_ps, hb, ident[:, :]).then_inc(S["ht_done"], 1)
                        pe.wait_ge((S["dn_in0"], S["dn_in1"], S["dn_in2"])[s], n * 16)
                        pe.wait_ge(S["ht_copied"], E + 1)
                        down(hT, j, turn=j).then_inc(S["dn_done"], 1)
                        if j == QUAD - 1:
                            gather_quad(q + 1, l, 1)
                        k0 = pe.value_load(table[0:1, ds(e + (NE + 1) * l, 1)], min_val=0, max_val=2 * NE)
                        k1 = pe.value_load(table[0:1, ds(e + ((NE + 1) * l + 1), 1)], min_val=0, max_val=2 * NE)
                        with pe.If(k0 < k1):
                            with pe.Fori(k0, k1) as k:
                                overflow(k, E, l, j)
                        if j == QUAD - 1:
                            pe.wait_ge(S["y_copied"], E + 1)
                            pe.wait_ge(S["g4_done"], E + 1)
                            combine_quad()

            moe(0)

            def odd_c0(g):
                pe.wait_ge(S["c0_in"], g * 16 + 16 * (EVEN_UNITS + 1))
                if not isinstance(g, int) or g:
                    pe.wait_ge(S["bc_silu"], g)
                project(pa[:, 0:SEQ], w_c[0], 0)
                project(pa[:, SEQ:], w_c[0], 1).then_inc(S["z1_done"], 1)

            transposes(2)
            pe.wait_ge(S["par_head"], 4 * 16)
            pe.wait_ge(S["h_part"], 8)
            by_tile(2, [acc[:, t, 0:HEADS] for t in range(TT)], wdt).then_inc(S["dt_raw"], 1)
            odd_c0(0)
            pe.wait_ge(S["dt_a"], 1)
            for t in range(TT):
                mm(pb[:, HEADS * t:HEADS * t + HEADS], upper[:, :], dta[:, t, :], start=True, stop=True)
                mm(wa[0:HEADS, P * t:P * t + P], dta[:, t, :], upper[:, :], start=True, stop=True)
            mm(pb[:, 64:96], ones[:, :], dta[:, 0, :], start=True, stop=True).then_inc(S["cum_done"], 1)
            zero_acc()

            def odd_c1(g):
                pe.wait_ge(S["c1_in"], g * 16 + 16 * (EVEN_UNITS + 1))
                if not isinstance(g, int) or g:
                    pe.wait_ge(S["x1_silu"], g)
                else:
                    pe.wait_ge(S["cum_used"], 1)
                project(pb[:, 0:SEQ], w_c[1], 0)
                project(pb[:, SEQ:], w_c[1], 1).then_inc(S["x1_done"], 1)

            def odd_b(g):
                pe.wait_ge(S["c2_in"], g * 16 + 16 * (EVEN_UNITS + 1))
                pe.wait_ge(S["z1_silu"], g + 1)
                project(pa[:, 0:SEQ], w_c[2], 0)

            def odd_c(g):
                project(pa[:, SEQ:], w_c[2], 1).then_inc(S["bc_done"], 1)

            def odd_rows(g):
                pe.wait_ge(S["gsel_done"], g + 1)
                if not isinstance(g, int) or g:
                    pe.wait_ge(S["mix1_done"], g)
                for b, w in enumerate((wa, wb)):
                    ins = mm(w[:, :], gsel, csx[:, b, :, :].rearrange("p r l -> p (r l)"), start=True, stop=True)
                ins.then_inc(S["csrow_done"], 1)

            def odd_scores(g, p):
                pe.wait_ge(S["bc_silu"], g + 1)
                pe.wait_ge(S["x1_silu"], g + 1)
                pe.wait_ge(S["decay_done"], g + 1)
                bt, ct = bcT[p][:, 0, :], bcT[p][:, 1, :]
                mm(wa[:, 0:SEQ], bt[:, 0:P], ct, start=True, stop=True)
                mm(wa[:, SEQ:384], bt[:, P:], ct[:, P:], start=True, stop=True).then_inc(S["cb_done"], 1)
                for t in range(TT):
                    for j in range(2):
                        ins = nc.tensor.transpose(wb[:, 256 * t + P * j:256 * t + P * j + P],
                                                  xT[p][:, j, P * t:P * t + P], ident[:, :])
                ins.then_inc(S["xst_done"], 1)

            def odd_y(g):
                pe.wait_ge(S["xdt_done"], g + 1)
                for r in range(HPG):
                    o = wa[HD * (r % 2):HD * (r % 2) + HD, 256 * (r // 2):256 * (r // 2) + 256]
                    c = slice(HD * r, HD * r + HD)
                    mm(o[:, 0:P], xdt[:, 0, c], decay[:, 0, r, :], start=True, stop=True)
                    mm(o[:, P:], xdt[:, 1, c], decay[:, 1, r, :], start=True, stop=False)
                    ins = mm(o[:, P:], xw[:, c], decay[:, 2, r, :], start=False, stop=True)
                ins.then_inc(S["y_done"], 1)

            def odd_ss(g):
                pe.wait_ge(S["yz_done"], g + 1)
                for j in range(2):
                    ins = mm(wb[:, 0:SEQ], ones[:, :], sq[:, j, :], start=(j == 0), stop=(j == 1))
                ins.then_inc(S["yss_done"], 1)

            def odd_out(g, p):
                pe.wait_ge(S["mix1_done"], g + 1)
                out_project(mix1[p], g + EVEN_UNITS)

            pe.wait_ge(S["dt_pre"], 1)
            odd_c1(0)
            odd_b(0)
            odd_c(0)
            pe.wait_ge(S["csx_done"], 1)

            def odd_unit(g, p, more):
                odd_rows(g)
                if more:
                    odd_c0(g + 1)
                odd_scores(g, p)
                if more:
                    odd_c1(g + 1)
                odd_y(g)
                if more:
                    odd_b(g + 1)
                odd_ss(g)
                if more:
                    odd_c(g + 1)
                odd_out(g, p)

            with pe.Fori(0, (ODD_UNITS - 2) // 2) as i:
                for p in range(2):
                    odd_unit(i * 2 + p, p, True)
            odd_unit(ODD_UNITS - 2, 0, True)
            odd_unit(ODD_UNITS - 1, 1, False)

            moe(1)


_INS = ['x', 'even_w_in', 'even_conv_w', 'even_w_out', 'odd_in_proj', 'odd_conv_w', 'odd_conv_b',
        'odd_dt_bias', 'odd_a_log', 'odd_d_skip', 'odd_norm_w', 'odd_out_proj', 'norm_mix', 'norm_ffn',
        'router_g_w', 'router_g_b', 'router_e_w', 'router_e_b', 'expert_w_gate', 'expert_w_up',
        'expert_w_down', 'final_norm']


def kernel(**inputs):
    import numpy as _np
    import concourse.bacc as _bacc
    from concourse import mybir as _mybir
    from concourse.bass_utils import run_bass_kernel_spmd as _run

    nc = _bacc.Bacc("TRN2", target_bir_lowering=False, num_devices=1)
    arrays, args = {}, []
    for name in _INS:
        a = _np.ascontiguousarray(inputs[name])
        arrays[f"in_{name}"] = a
        args.append(nc.dram_tensor(f"in_{name}", a.shape, _mybir.dt.from_np(a.dtype), kind="ExternalInput").ap())
    args.append(nc.dram_tensor("out_0", (1, SEQ, D), _mybir.dt.from_np(_np.dtype("float32")),
                               kind="ExternalOutput").ap())
    trunk_program(nc, *args)
    r = _run(nc, [arrays], core_ids=[0])
    return r.results[0]["out_0"]
```
